# Optimizing a Trainium2 kernel written in Bass

```python
import jax, jax.numpy as jnp
from jax import lax
import numpy as np

D_MODEL = 1024
BATCH = 1
SEQ = 2048
DEPTH = 1

ATT_HEADS = 8
ATT_KV_HEADS = 2
HEAD_DIM = 64
ATT_WIDTH = ATT_HEADS * HEAD_DIM
KV_WIDTH = ATT_KV_HEADS * HEAD_DIM
IDX_HEADS = 8
IDX_DIM = 64
TOPK_MAX = 256
Q_BLOCK = 128
ROPE_THETA = 500000.0
ROPE_FRACTION = 4
HG_HEADS = 4
HG_KDIM = 128
HG_VDIM = 128
HG_FWIDTH = HG_HEADS * HG_KDIM
HG_WIDTH = HG_HEADS * HG_VDIM
CHUNK = 64
MIX_WIDTH = ATT_WIDTH + HG_WIDTH
D_FF = ((-(-8 * D_MODEL // 3) + 255) // 256) * 256
NORM_EPS = 1e-6
IN_SPLITS = (ATT_WIDTH, KV_WIDTH, KV_WIDTH, IDX_HEADS * IDX_DIM, IDX_DIM, IDX_HEADS,
             HG_FWIDTH, HG_FWIDTH, HG_WIDTH, HG_WIDTH)
IN_WIDTH = sum(IN_SPLITS)

kernel_name = "hymba_dsa_hgrn2_sandwich_layer"

def rms_norm(x, gain):
    x32 = x.astype(jnp.float32)
    y = x32 * lax.rsqrt(jnp.mean(x32 * x32, axis=-1, keepdims=True) + NORM_EPS)
    return (y * gain.astype(jnp.float32)).astype(x.dtype)

def partial_rope(x, pos):
    d = x.shape[-1]
    rd = d // ROPE_FRACTION
    half = rd // 2
    inv = ROPE_THETA ** (-jnp.arange(half, dtype=jnp.float32) / half)
    ang = pos.astype(jnp.float32)[:, None] * inv[None, :]
    ang = ang.reshape((ang.shape[0],) + (1,) * (x.ndim - 3) + (half,))
    cos = jnp.cos(ang).astype(x.dtype)
    sin = jnp.sin(ang).astype(x.dtype)
    x1 = x[..., :half]
    x2 = x[..., half:rd]
    return jnp.concatenate([x1 * cos - x2 * sin, x2 * cos + x1 * sin, x[..., rd:]], axis=-1)

def split_columns(p):
    pts = []
    acc = 0
    for s in IN_SPLITS[:-1]:
        acc += s
        pts.append(acc)
    return jnp.split(p, pts, axis=-1)

def dsa_attention(q, k, v, qi, ki, wi):
    B, T = q.shape[0], q.shape[1]
    S = k.shape[1]
    topk = min(TOPK_MAX, S // 4)
    nb = T // Q_BLOCK
    key_pos = jnp.arange(S)
    group = ATT_HEADS // ATT_KV_HEADS

    def to_blocks(a):
        return jnp.swapaxes(a.reshape((B, nb, Q_BLOCK) + a.shape[2:]), 0, 1)

    qpos = jnp.arange(T).reshape(nb, Q_BLOCK)

    def block(args):
        qb, qib, wib, tpos = args
        rel = jax.nn.relu(jnp.einsum('bthd,bsd->btsh', qib, ki))
        iscore = jnp.einsum('btsh,bth->bts', rel, wib).astype(jnp.float32)
        causal = key_pos[None, :] <= tpos[:, None]
        iscore = jnp.where(causal[None], iscore, -jnp.inf)
        _, idx = lax.top_k(iscore, topk)
        valid = idx <= tpos[None, :, None]
        ksel = jax.vmap(lambda kk, ii: kk[ii])(k, idx)
        vsel = jax.vmap(lambda vv, ii: vv[ii])(v, idx)
        qg = qb.reshape(B, Q_BLOCK, ATT_KV_HEADS, group, HEAD_DIM)
        s = jnp.einsum('btgrd,btkgd->btgrk', qg, ksel).astype(jnp.float32) * (HEAD_DIM ** -0.5)
        s = jnp.where(valid[:, :, None, None, :], s, -jnp.inf)
        p = jax.nn.softmax(s, axis=-1).astype(v.dtype)
        o = jnp.einsum('btgrk,btkgd->btgrd', p, vsel)
        return o.reshape(B, Q_BLOCK, ATT_WIDTH)

    out = lax.map(block, (to_blocks(q), to_blocks(qi), to_blocks(wi), qpos))
    return jnp.swapaxes(out, 0, 1).reshape(B, T, ATT_WIDTH)

def hgrn2_chunkwise(q, k, v, logf):
    B, T, H, K = q.shape
    V = v.shape[-1]
    nc = T // CHUNK

    def chunks(a):
        return jnp.moveaxis(a.reshape(B, nc, CHUNK, H, a.shape[-1]), 1, 0)

    tri = jnp.tril(jnp.ones((CHUNK, CHUNK), dtype=bool))

    def step(state, inp):
        qc, kc, vc, gc = inp
        b = jnp.cumsum(gc, axis=1)
        o_inter = jnp.einsum('bthk,bhkv->bthv', qc * jnp.exp(b), state)
        diff = b[:, :, None] - b[:, None, :]
        decay = jnp.exp(jnp.where(tri[None, :, :, None, None], diff, -jnp.inf))
        a = jnp.einsum('bthk,bshk,btshk->bhts', qc, kc, decay)
        o_intra = jnp.einsum('bhts,bshv->bthv', a, vc)
        b_last = b[:, -1]
        new_state = jnp.exp(b_last)[..., None] * state + jnp.einsum(
            'bshk,bshv->bhkv', kc * jnp.exp(b_last[:, None] - b), vc)
        return new_state, o_inter + o_intra

    s0 = jnp.zeros((B, H, K, V), jnp.float32)
    _, o = lax.scan(step, s0, (chunks(q), chunks(k), chunks(v), chunks(logf)))
    return jnp.moveaxis(o, 0, 1).reshape(B, T, H, V)

def hgrn2_mixer(hq, hf, hi, hg, lb_param, out_gain, layer):
    B, T = hq.shape[0], hq.shape[1]
    lb = jnp.cumsum(jax.nn.softmax(lb_param.astype(jnp.float32), axis=0), axis=0)[layer]
    f = lb + (1.0 - lb) * jax.nn.sigmoid(hf.astype(jnp.float32))
    logf = jnp.log(f).reshape(B, T, HG_HEADS, HG_KDIM)
    k = (1.0 - f).reshape(B, T, HG_HEADS, HG_KDIM)
    q = jax.nn.silu(hq.astype(jnp.float32)).reshape(B, T, HG_HEADS, HG_KDIM)
    v = hi.astype(jnp.float32).reshape(B, T, HG_HEADS, HG_VDIM)
    o = hgrn2_chunkwise(q, k, v, logf)
    o = rms_norm(o, out_gain.reshape(HG_HEADS, HG_VDIM))
    o = o.reshape(B, T, HG_WIDTH) * jax.nn.silu(hg.astype(jnp.float32))
    return o.astype(hq.dtype)

def setup_inputs(seed: int = 0) -> dict:
    key = jax.random.key(seed)
    ks = jax.random.split(key, 13)
    f32 = jnp.float32

    def w(k, shape, fan_in):
        return jax.random.normal(k, shape, f32) * (fan_in ** -0.5)

    def gain(k, shape):
        return 1.0 + 0.02 * jax.random.normal(k, shape, f32)

    return {
        "x": jax.random.normal(ks[0], (BATCH, SEQ, D_MODEL), f32),
        "norm_pre_mix": gain(ks[1], (DEPTH, D_MODEL)),
        "w_in": w(ks[2], (DEPTH, D_MODEL, IN_WIDTH), D_MODEL),
        "w_out": w(ks[3], (DEPTH, MIX_WIDTH, D_MODEL), MIX_WIDTH),
        "norm_post_mix": gain(ks[4], (DEPTH, D_MODEL)),
        "hg_lower_bound": jax.random.normal(ks[5], (DEPTH + 1, HG_FWIDTH), f32),
        "hg_out_norm": gain(ks[6], (DEPTH, HG_WIDTH)),
        "norm_pre_ffn": gain(ks[7], (DEPTH, D_MODEL)),
        "w_gate": w(ks[8], (DEPTH, D_MODEL, D_FF), D_MODEL),
        "w_up": w(ks[9], (DEPTH, D_MODEL, D_FF), D_MODEL),
        "w_down": w(ks[10], (DEPTH, D_FF, D_MODEL), D_FF),
        "norm_post_ffn": gain(ks[11], (DEPTH, D_MODEL)),
    }

def reference(x, norm_pre_mix, w_in, w_out, norm_post_mix, hg_lower_bound, hg_out_norm,
              norm_pre_ffn, w_gate, w_up, w_down, norm_post_ffn):
    B, T, _ = x.shape
    pos = jnp.arange(T)
    idx_scale = (IDX_HEADS ** -0.5) * (IDX_DIM ** -0.5)
    for l in range(DEPTH):
        h = rms_norm(x, norm_pre_mix[l])
        proj = jnp.einsum('btd,de->bte', h, w_in[l])
        q, k, v, qi, ki, wi, hq, hf, hi, hg = split_columns(proj)
        q = partial_rope(q.reshape(B, T, ATT_HEADS, HEAD_DIM), pos)
        k = partial_rope(k.reshape(B, T, ATT_KV_HEADS, HEAD_DIM), pos)
        v = v.reshape(B, T, ATT_KV_HEADS, HEAD_DIM)
        qi = partial_rope(qi.reshape(B, T, IDX_HEADS, IDX_DIM), pos)
        ki = partial_rope(ki, pos)
        wi = wi * idx_scale
        att_out = dsa_attention(q, k, v, qi, ki, wi)
        hg_out = hgrn2_mixer(hq, hf, hi, hg, hg_lower_bound, hg_out_norm[l], l)
        mix = jnp.einsum('bte,ed->btd', jnp.concatenate([att_out, hg_out], axis=-1), w_out[l])
        x = x + rms_norm(mix, norm_post_mix[l])
        h2 = rms_norm(x, norm_pre_ffn[l])
        ff = jax.nn.silu(jnp.einsum('btd,df->btf', h2, w_gate[l])) * jnp.einsum('btd,df->btf', h2, w_up[l])
        ff = jnp.einsum('btf,fd->btd', ff, w_down[l])
        x = x + rms_norm(ff, norm_post_ffn[l])
    return x


_drawn_inputs = setup_inputs


def setup_inputs(seed=0):
    import zlib

    import numpy as np

    out = dict(_drawn_inputs(seed))
    spreads = {}
    factors = {'norm_post_mix': 3.496,
     'hg_out_norm': 3.459,
     'norm_pre_ffn': 3.443,
     'norm_post_ffn': 4.894}
    for name, (base, spread) in spreads.items():
        noise = np.random.default_rng([zlib.crc32(name.encode()), seed]).standard_normal(out[name].shape)
        drawn = base * np.exp(spread * noise) if base else spread * noise
        out[name] = __import__('jax').numpy.asarray(drawn.astype(out[name].dtype))
    for name, factor in factors.items():
        out[name] = (out[name] * factor).astype(out[name].dtype)
    return out
```

```python
from contextlib import ExitStack

import numpy as np

import concourse.bass as bass
from concourse import mybir

F32 = mybir.dt.float32
F32R = mybir.dt.float32r
BF16 = mybir.dt.bfloat16
ALU = mybir.AluOpType
ACT = mybir.ActivationFunctionType
AX_X = mybir.AxisListType.X

P = 128
T, D = 2048, 1024
NB = T // P
KD = D // P
HEADS, KV, HD = 8, 2, 64
GROUP = HEADS // KV
IH = 8
TOPK = 256
HG, HK = 4, 128
FF = 2816
NF = FF // P
EPS = 1e-6
ROPE = 8
THETA = 500000.0
SPLITS = (512, 128, 128, 512, 64, 8, 512, 512, 512, 512)
Q0, K0, V0, QI0, KI0, WI0, HQ0, HF0, HI0, HG0 = [sum(SPLITS[:n]) for n in range(10)]
IN_W = sum(SPLITS)
NC_IN = 10
CW = IN_W // NC_IN
IDX_SCALE = (IH ** -0.5) * (HD ** -0.5)
SM_SCALE = HD ** -0.5
NEG = -1.0e30
TAKEN = -3.0e38
LEVELS = (64, 32, 16, 8, 4, 2, 1)
NM = len(LEVELS) + 1
SB = 512
NS = T // SB
TS = SB // P


def shape_constants():
    t = np.arange(P)
    ident = np.eye(P, dtype=np.float32)
    sums = np.zeros((P, NM + 1, P), np.float32)
    pick = np.zeros((P, NM, P), np.float32)
    u, tt = t[:, None], t[None, :]
    for n, h in enumerate(LEVELS):
        mid = (tt // (2 * h)) * 2 * h + h
        sums[:, n] = np.where(tt >= mid, (u >= mid) & (u <= tt), (u > tt) & (u < mid))
        pick[:, n] = (u // (2 * h) == tt // (2 * h)) & (u % (2 * h) < h) & (tt % (2 * h) >= h)
    sums[:, NM - 1] = u <= tt
    sums[:, NM] = u > tt
    pick[:, NM - 1] = u == tt
    causal = np.where(tt <= u, 0.0, NEG).astype(np.float32)
    half = ROPE
    inv = THETA ** (-np.arange(half, dtype=np.float32) / np.float32(half))
    ang = np.arange(T, dtype=np.float32)[:, None] * inv[None, :].astype(np.float32)
    rope = np.stack([np.cos(ang), np.sin(ang)], 1).astype(np.float32)
    rope = np.ascontiguousarray(rope.reshape(NB, P, 2, half).transpose(1, 0, 2, 3))
    return dict(c_ident=ident, c_sums=sums, c_pick=pick, c_causal=causal, c_rope=rope)


def project_phase(nc, a, proj_d):
    with ExitStack() as ctx:
        def sb(name, shape, dt=F32):
            return ctx.enter_context(nc.sbuf_tensor(name, shape, dt))

        def sem(name):
            return ctx.enter_context(nc.semaphore(name))

        h_hi = sb("h_hi", [P, KD, T], F32R)
        h_lo = sb("h_lo", [P, KD, T], F32R)
        w_raw = sb("w_raw", [P, KD, CW])
        w_hi = sb("w_hi", [P, 2, KD, CW], F32R)
        w_lo = sb("w_lo", [P, 2, KD, CW], F32R)
        stage = sb("stage", [P, 2, 2, CW])
        xt = sb("xt", [P, 2, D])
        gain = sb("gain_in", [P, D])
        ident = sb("ident_p", [P, P])
        ss = sb("ss_p", [P, 2])
        var = sb("var_p", [P, 2])
        rstd = sb("rstd_p", [P, 2])
        mhalf = sb("mhalf_p", [P, 2])
        junk = stage[:, :, :, :].rearrange("p a b c -> p (a b c)")[:, 0:D]
        ps = ctx.enter_context(nc.psum_tensor("ps_proj", [P, 8, 512], F32))

        const_in = sem("p_const_in")
        x_in = [sem("p_x_in0"), sem("p_x_in1")]
        ss_ready = sem("p_ss_ready")
        pool_step = sem("p_pool_step")
        rstd_ready = sem("p_rstd_ready")
        xn_ready = sem("p_xn_ready")
        xT_ready = sem("p_xT_ready")
        h_hi_ready = sem("p_h_hi_ready")
        bank_free = sem("p_bank_free")
        w_in = sem("p_w_in")
        w_hi_ready = sem("p_w_hi_ready")
        w_lo_ready = sem("p_w_lo_ready")
        tile_done = sem("p_tile_done")
        staged = sem("p_staged")
        stored = [sem("p_stored0"), sem("p_stored1")]
        block = ctx.enter_context(nc.Block())

        @block.sync
        def _(sp):
            sp.dma_start(ident[:], a["c_ident"]).then_inc(const_in, 16)
            sp.dma_start(gain[:], a["norm_pre_mix"].broadcast_to([P, D])).then_inc(const_in, 16)
            for i in range(NB):
                if i >= 2:
                    sp.wait_ge(xT_ready, 2 * (i - 1))
                sp.dma_start(xt[:, i % 2, :], a["x"][0, i * P:(i + 1) * P, :]).then_inc(x_in[i % 2], 16)
                if i == 1:
                    sp.dma_start(w_raw[:], a["w_in"][0]).then_inc(w_in, 16)

            def store(c, k):
                sp.wait_ge(staged, 16 * c + 2 * k + 2)
                rows = proj_d[2 * k * P:(2 * k + 2) * P, :].rearrange("(i p) e -> p i e", p=P)
                sp.dma_start(rows[:, :, bass.ds(c * CW, CW)], stage[:, k % 2]).then_inc(stored[k % 2], 16)

            with sp.Fori(0, NC_IN - 1) as c:
                sp.wait_ge(w_lo_ready, c + 1)
                sp.dma_start(w_raw[:], a["w_in"][c + 1]).then_inc(w_in, 16)
                for k in range(NB // 2):
                    store(c, k)
            for k in range(NB // 2):
                store(NC_IN - 1, k)
            for half in stored:
                sp.wait_ge(half, 16 * NC_IN * NB // 4)

        @block.gpsimd
        def _(pool):
            nc.gpsimd.memset(mhalf[:], -0.5).then_inc(pool_step, 1)
            pool.wait_ge(pool_step, 1)
            for i in range(NB):
                s = slice(i % 2, i % 2 + 1)
                pool.wait_ge(ss_ready, i + 1)
                nc.gpsimd.tensor_scalar(var[:, s], ss[:, s], 1.0 / D, EPS, ALU.mult, ALU.add).then_inc(pool_step, 1)
                pool.wait_ge(pool_step, i + 2)
                nc.gpsimd.tensor_tensor(rstd[:, s], var[:, s], mhalf[:, s], ALU.pow).then_inc(rstd_ready, 1)

        @block.scalar
        def _(act):
            def square(i):
                act.wait_ge(x_in[i % 2], 16 * (i // 2 + 1))
                if i >= 2:
                    act.wait_ge(rstd_ready, i - 1)
                if i >= 1:
                    act.wait_ge(ss_ready, i)
                nc.scalar.activation(junk, xt[:, i % 2, :], ACT.Square,
                                     accum_out=ss[:, i % 2:i % 2 + 1]).then_inc(ss_ready, 1)

            def split_hi(i):
                for k in range(2):
                    act.wait_ge(xT_ready, 2 * i + k + 1)
                    nc.scalar.activation(h_hi[:, 4 * k:4 * k + 4, i * P:(i + 1) * P],
                                         ps[:, (2 * i + k) % 8, :].rearrange("p (k t) -> p k t", k=4),
                                         ACT.Copy).then_inc(h_hi_ready, 1)
            square(0)
            for i in range(NB):
                if i + 1 < NB:
                    square(i + 1)
                split_hi(i)
            act.wait_ge(w_in, 16)
            nc.scalar.activation(w_hi[:, 0], w_raw[:], ACT.Copy).then_inc(w_hi_ready, 1)

            def evacuate(c, u, first):
                for i in range(NB):
                    act.wait_ge(tile_done, 16 * c + i + 1)
                    if i % 2 == 0 and not (first and i < 4):
                        act.wait_ge(stored[(i // 2) % 2], 16 * (4 * c + i // 4))
                    nc.scalar.activation(stage[:, (i // 2) % 2, i % 2, :], ps[:, i % 8, 0:CW],
                                         ACT.Copy).then_inc(staged, 1)

            def next_hi(c, u, first):
                act.wait_ge(w_in, 16 * (c + 2))
                if not first:
                    act.wait_ge(tile_done, 16 * c)
                nc.scalar.activation(w_hi[:, 1 - u], w_raw[:], ACT.Copy).then_inc(w_hi_ready, 1)

            next_hi(0, 0, True)
            act.wait_ge(ss_ready, NB)
            evacuate(0, 0, True)
            with act.Fori(0, NC_IN // 2 - 1) as j:
                for c, u in ((2 * j + 1, 1), (2 * j + 2, 0)):
                    next_hi(c, u, False)
                    evacuate(c, u, False)
            evacuate(NC_IN - 1, 1, False)

        @block.vector
        def _(dve):
            dve.wait_ge(const_in, 32)

            def normalise(i):
                dve.wait_ge(rstd_ready, i + 1)
                x = xt[:, i % 2, :]
                nc.vector.scalar_tensor_tensor(x, x, rstd[:, i % 2:i % 2 + 1], gain[:], ALU.mult,
                                               ALU.mult).then_inc(xn_ready, 1)

            def split_lo(i):
                for k in range(2):
                    dve.wait_ge(h_hi_ready, 2 * i + k + 1)
                    to = slice(4 * k, 4 * k + 4), slice(i * P, (i + 1) * P)
                    nc.vector.tensor_tensor(h_lo[:, to[0], to[1]],
                                            ps[:, (2 * i + k) % 8, :].rearrange("p (k t) -> p k t", k=4),
                                            h_hi[:, to[0], to[1]].bitcast(F32),
                                            ALU.subtract).then_inc(bank_free, 1)
            normalise(0)
            for i in range(NB):
                if i + 1 < NB:
                    normalise(i + 1)
                split_lo(i)

            def w_low(c, u):
                dve.wait_ge(w_hi_ready, c + 1)
                nc.vector.tensor_tensor(w_lo[:, u], w_raw[:], w_hi[:, u].bitcast(F32),
                                        ALU.subtract).then_inc(w_lo_ready, 1)
            with dve.Fori(0, NC_IN // 2) as j:
                for u in range(2):
                    w_low(2 * j + u, u)

        @block.tensor
        def _(pe):
            pe.wait_ge(const_in, 32)
            for i in range(NB):
                pe.wait_ge(xn_ready, i + 1)
                for k in range(2):
                    n = 2 * i + k
                    if n >= 8:
                        pe.wait_ge(bank_free, n - 7)
                    for q in range(4):
                        last = nc.tensor.transpose(ps[:, n % 8, q * P:(q + 1) * P],
                                                   xt[:, i % 2, (4 * k + q) * P:(4 * k + q + 1) * P], ident[:])
                    last.then_inc(xT_ready, 1)
            pe.wait_ge(bank_free, 2 * NB)

            def chunk(c, u, first):
                pe.wait_ge(w_lo_ready, c + 1)
                for i in range(NB):
                    if not (first and i < 8):
                        pe.wait_ge(staged, 16 * c + i - 7)
                    tok = slice(i * P, (i + 1) * P)
                    out = ps[:, i % 8, 0:CW]
                    for k in range(KD):
                        nc.tensor.matmul(out, h_hi[:, k, tok], w_hi[:, u, k, :], start=(k == 0), stop=False)
                        nc.tensor.matmul(out, h_hi[:, k, tok], w_lo[:, u, k, :], start=False, stop=False)
                        last = nc.tensor.matmul(out, h_lo[:, k, tok], w_hi[:, u, k, :], start=False,
                                                stop=(k == KD - 1))
                    last.then_inc(tile_done, 1)

            chunk(0, 0, True)
            with pe.Fori(0, NC_IN // 2 - 1) as j:
                chunk(2 * j + 1, 1, False)
                chunk(2 * j + 2, 0, False)
            chunk(NC_IN - 1, 1, False)


def mix_phase(nc, a, proj_d, mix_d):
    NK = lambda b: (b + 1) * P
    NCH = lambda b: -(-NK(b) // 512)
    pairs_of = lambda b: -(-NK(b) // 1024)
    ITERS = 11

    with ExitStack() as ctx:
        def sb(name, shape, dt=F32):
            return ctx.enter_context(nc.sbuf_tensor(name, shape, dt))

        def psum(name, shape):
            return ctx.enter_context(nc.psum_tensor(name, shape, F32))

        def sem(name):
            return ctx.enter_context(nc.semaphore("m_" + name))

        ident = sb("ident_m", [P, P])
        sums = sb("sums", [P, NM + 1, P])
        pick = sb("pick", [P, NM, P])
        causal = sb("causal", [P, P])
        rope = sb("rope", [P, NB, 2, ROPE])
        lb = sb("lb", [P, 2, HG * HK])
        lbw = sb("lbw", [P, 512])
        g_hg = sb("g_hg", [P, HG * HK])
        row = sb("row", [P, 2, IN_W])
        rt = sb("rt", [P, 4, KV + HEADS, ROPE])
        kdup = sb("kdup", [P, 3, 2, HD])
        wis = sb("wis", [P, 2, IH])
        KT = sb("KT", [P, 3, T])
        V = sb("V", [P, NB, KV * HD])
        qT = sb("qT", [P, 2, 4, P])
        qiT = sb("qiT", [P, 4, P])
        rel = sb("rel", [P, 2, 2, 512])
        score = sb("score", [P, T + 8])
        above = sb("above", [P, T], BF16)
        bias = sb("bias", [P, 2, T], BF16)
        ends = sb("ends", [P, 2])
        mid = sb("mid", [P, 1])
        cnt = sb("cnt", [P, 1])
        side = sb("side", [P, 2], mybir.dt.uint8)
        sign = sb("sign", [P, 2])
        goal = sb("goal", [P, 2])
        left = sb("left", [P, 1])
        left_all = sb("left_all", [P, 1])
        left_int = sb("left_int", [P, 1], mybir.dt.int32)
        iota8 = sb("iota8", [P, 8])
        top8 = sb("top8", [P, 8])
        want8 = sb("want8", [P, 8])
        use8 = sb("use8", [P, 8], mybir.dt.uint8)
        prob = sb("prob", [P, 2, T])
        mxp = sb("mxp", [P, HEADS, 2])
        nmx = sb("nmx", [P, HEADS])
        den = sb("den", [P, HEADS])
        rden = sb("rden", [P, HEADS])
        pT = sb("pT", [P, 2, 512])
        sig = sb("sig", [P, 3, 512])
        hq = sb("hq", [P, 512])
        hk = sb("hk", [P, 512])
        gg = sb("gg", [P, 512])
        fg = sb("fg", [P, 512])
        khat = sb("khat", [P, 512])
        hqT = sb("hqT", [P, HG, P])
        hkT = sb("hkT", [P, HG, P])
        decay = sb("decay", [P, 2, NM, P])
        qe = sb("qe", [P, 2, NM, P])
        ke = sb("ke", [P, 2, NM - 1, P])
        am = sb("am", [P, 2, NM, P])
        elast = sb("elast", [P, HG])
        state = sb("state", [P, HG, HK])
        osb = sb("osb", [P, HG, HK])
        osq = sb("osq", [P, HG, HK])
        hss = sb("hss", [P, HG])
        hvar = sb("hvar", [P, HG])
        hrstd = sb("hrstd", [P, HG])
        mhalf = sb("mhalf_m", [P, HG])
        mix = sb("mix", [P, 2, D])

        SA = psum("SA", [P, 2, 1024])
        SBk = psum("SBk", [P, 2, 512])
        SC = psum("SC", [P, 512])
        SD = psum("SD", [P, 512])

        const_in = sem("const_in")
        row_in = [sem("row_in0"), sem("row_in1")]
        pool_step, dve_step, act_step = sem("pool_step"), sem("dve_step"), sem("act_step")
        bounds_step = sem("bounds_step")
        lb_ready = sem("lb_ready")
        rows_ready = sem("rows_ready")
        sb_full, sb_free = sem("sb_full"), sem("sb_free")
        keys_full, keys_out = sem("keys_full"), sem("keys_out")
        sa_full = sem("sa_full")
        sa_free_act, sa_free_dve = sem("sa_free_act"), sem("sa_free_dve")
        rel_read = sem("rel_read")
        bias_ready = sem("bias_ready")
        left_ready, left_max = sem("left_ready"), sem("left_max")
        nmx_ready, prob_ready = sem("nmx_ready"), sem("prob_ready")
        pv_done = sem("pv_done")
        sig_e, sig_ready = sem("sig_e"), sem("sig_ready")
        hq_ready, hk_ready, gg_ready = sem("hq_ready"), sem("hk_ready"), sem("gg_ready")
        logf_ready = sem("logf_ready")
        tail_full, tail_out = sem("tail_full"), sem("tail_out")
        khat_ready = sem("khat_ready")
        qe_ready, ke_ready = sem("qe_ready"), sem("ke_ready")
        ho_done, ho_out = sem("ho_done"), sem("ho_out")
        kv_done, state_ready = sem("kv_done"), sem("state_ready")
        hss_ready, hrstd_ready = sem("hss_ready"), sem("hrstd_ready")
        mix_ready = sem("mix_ready")
        stored = [sem("stored0"), sem("stored1")]

        use, reader, sb_use, pt_order, idx_order = {}, [], {}, {}, {}

        def enter(key, who):
            use[key] = len(reader)
            reader.append(who)

        def enter_prep(b):
            for what in ("q", "qi"):
                sb_use[what, b] = len(sb_use)
            for c in range(NCH(b) if b >= 2 else 0):
                for j in range(IH // 2):
                    idx_order[b, c, j] = len(idx_order)
                    enter(("idx", b, c, j), "act")

        enter_prep(0)
        for b in range(NB):
            if b + 1 < NB:
                enter_prep(b + 1)
            for what in ("hq", "hk"):
                sb_use[what, b] = len(sb_use)
            for h in range(HG + 1):
                if h < HG:
                    enter(("decay", b, h), "act")
                if h >= 1:
                    enter(("level", b, h - 1), "dve")
            for h in range(HEADS):
                for p in range(pairs_of(b)):
                    enter(("att", b, h, p), "dve")
                for c in range(NCH(b)):
                    sb_use["pT", b, h, c] = len(sb_use)
                    pt_order[b, h, c] = len(pt_order)

        def pair(key):
            return SA[:, use[key] % 2, :]

        def bank(key):
            return SBk[:, sb_use[key] % 2, :]

        def wait_pair_read(eng, n):
            done = reader[:n + 1].count(reader[n])
            eng.wait_ge(sa_free_act if reader[n] == "act" else sa_free_dve, done)

        def wait_pair_free(eng, key):
            if use[key] >= 2:
                wait_pair_read(eng, use[key] - 2)

        def wait_pair_full(eng, key):
            eng.wait_ge(sa_full, use[key] + 1)

        def wait_bank_free(eng, key):
            if sb_use[key] >= 2:
                eng.wait_ge(sb_free, sb_use[key] - 1)

        def linker(eng, step):
            count = [0]

            def link(ins):
                count[0] += 1
                ins.then_inc(step, 1)
                eng.wait_ge(step, count[0])
            return link

        def heads(ap, n=HG):
            return ap.rearrange("p (h t) -> p h t", h=n)

        block = ctx.enter_context(nc.Block())

        @block.sync
        def _(sp):
            for to, name in ((ident, "c_ident"), (sums, "c_sums"), (pick, "c_pick"), (causal, "c_causal"),
                             (rope, "c_rope")):
                sp.dma_start(to[:], a[name]).then_inc(const_in, 16)
            for n in range(2):
                sp.dma_start(lb[:, n, :], a["hg_lower_bound"][n:n + 1, :].broadcast_to([P, 512])).then_inc(const_in, 16)
            sp.dma_start(g_hg[:], a["hg_out_norm"].broadcast_to([P, 512])).then_inc(const_in, 16)

            def load(b):
                if b >= 2:
                    sp.wait_ge(kv_done, b - 1)
                    sp.wait_ge(gg_ready, b - 1)
                sp.dma_start(row[:, b % 2, :], proj_d[b * P:(b + 1) * P, :]).then_inc(row_in[b % 2], 16)

            load(0)
            for b in range(NB):
                if b + 1 < NB:
                    load(b + 1)
                sp.wait_ge(mix_ready, 2 * (b + 1))
                sp.dma_start(mix_d[b * P:(b + 1) * P, :], mix[:, b % 2, :]).then_inc(stored[b % 2], 16)
            for half in stored:
                sp.wait_ge(half, 16 * NB // 2)

        @block.gpsimd
        def _(pool):
            g = nc.gpsimd
            link = linker(pool, pool_step)
            link(g.memset(mhalf[:], -0.5))
            g.iota(iota8[:], [[1, 8]], base=0, channel_multiplier=0,
                   allow_small_or_imprecise_dtypes=True).then_inc(lb_ready, 1)
            pool.wait_ge(const_in, 8 * 16)

            def prep(b):
                pool.wait_ge(row_in[b % 2], 16 * (b // 2 + 1))
                r = row[:, b % 2, :]
                for c0, n_heads in ((Q0, HEADS + KV), (QI0, IH + 1)):
                    x = r[:, c0:c0 + n_heads * HD].rearrange("p (h d) -> p h d", d=HD)
                    x1, x2 = x[:, :, 0:ROPE], x[:, :, ROPE:2 * ROPE]
                    cos = rope[:, b, 0:1, :].broadcast_to([P, n_heads, ROPE])
                    sin = rope[:, b, 1:2, :].broadcast_to([P, n_heads, ROPE])
                    for n, (xx, cs) in enumerate(((x1, cos), (x2, sin), (x2, cos), (x1, sin))):
                        last = g.tensor_tensor(rt[:, n, 0:n_heads, :], xx, cs, ALU.mult)
                    link(last)
                    g.tensor_tensor(x1, rt[:, 0, 0:n_heads, :], rt[:, 1, 0:n_heads, :], ALU.subtract)
                    link(g.tensor_tensor(x2, rt[:, 2, 0:n_heads, :], rt[:, 3, 0:n_heads, :], ALU.add))
                if b >= 1:
                    pool.wait_ge(keys_full, b)
                if b >= 4:
                    pool.wait_ge(rel_read, idx_order[b - 2, NCH(b - 2) - 1, IH // 2 - 1] + 1)
                k = r[:, K0:K0 + KV * HD].rearrange("p (g d) -> p g d", d=HD)
                for n in range(2):
                    g.tensor_copy(kdup[:, 0:KV, n, :], k)
                    g.tensor_copy(kdup[:, KV, n, :], r[:, KI0:KI0 + HD])
                g.tensor_copy(V[:, b, :], r[:, V0:V0 + KV * HD])
                g.tensor_scalar(wis[:, b % 2, :], r[:, WI0:WI0 + IH], IDX_SCALE, None, ALU.mult)\
                    .then_inc(rows_ready, 1)

            def hgrn(b):
                r = row[:, b % 2, :]
                pool.wait_ge(sig_ready, b + 1)
                if b == 0:
                    pool.wait_ge(lb_ready, 2)
                else:
                    pool.wait_ge(kv_done, b)
                    pool.wait_ge(sb_free, sb_use["hk", b - 1] + 1)
                link(g.tensor_tensor(fg[:], sig[:, 1, :], lb[:, 1, :], ALU.mult))
                link(g.tensor_tensor(fg[:], fg[:], lb[:, 0, :], ALU.add))
                g.tensor_scalar(hk[:], fg[:], -1.0, 1.0, ALU.mult, ALU.add).then_inc(hk_ready, 1)
                g.tensor_tensor(hq[:], r[:, HQ0:HQ0 + 512], sig[:, 0, :], ALU.mult).then_inc(hq_ready, 1)
                if b >= 1:
                    pool.wait_ge(mix_ready, 2 * b)
                link(g.tensor_tensor(gg[:], r[:, HG0:HG0 + 512], sig[:, 2, :], ALU.mult))
                g.tensor_tensor(gg[:], gg[:], g_hg[:], ALU.mult).then_inc(gg_ready, 1)
                pool.wait_ge(tail_out, b + 1)
                g.tensor_tensor(khat[:], khat[:], hk[:], ALU.mult).then_inc(khat_ready, 1)
                for h in range(HG):
                    n = HG * b + h
                    wait_pair_read(pool, use["decay", b, h])
                    if n >= 2:
                        wait_pair_full(pool, ("level", (n - 2) // HG, (n - 2) % HG))
                    g.tensor_tensor(ke[:, h % 2], decay[:, h % 2, 0:NM - 1, :],
                                    hkT[:, h:h + 1, :].broadcast_to([P, NM - 1, P]), ALU.mult).then_inc(ke_ready, 1)
                pool.wait_ge(hss_ready, b + 1)
                link(g.tensor_scalar(hvar[:], hss[:], 1.0 / HK, EPS, ALU.mult, ALU.add))
                g.tensor_tensor(hrstd[:], hvar[:], mhalf[:], ALU.pow).then_inc(hrstd_ready, 1)

            prep(0)
            for b in range(NB):
                if b + 1 < NB:
                    prep(b + 1)
                hgrn(b)
                if 2 <= b + 1 < NB:
                    pool.wait_ge(left_ready, b)
                    g.partition_all_reduce(left_all[:], left[:], P, bass.bass_isa.ReduceOp.max).then_inc(left_max, 1)

        @block.scalar
        def _(act):
            s = nc.scalar
            act.wait_ge(bounds_step, 1)
            s.activation(lb[:], lb[:], ACT.Exp).then_inc(bounds_step, 1)

            def prep(b):
                for what, to in (("q", qT[:, b % 2]), ("qi", qiT[:])):
                    act.wait_ge(sb_full, sb_use[what, b] + 1)
                    s.activation(to, heads(bank((what, b)), 4), ACT.Copy).then_inc(sb_free, 1)
                act.wait_ge(keys_full, b + 1)
                s.activation(KT[:, :, b * P:(b + 1) * P], heads(SD[:, 0:3 * P], 3), ACT.Copy).then_inc(keys_out, 1)

            def idx(b):
                for c in range(NCH(b)):
                    w = min(512, NK(b) - 512 * c)
                    for j in range(IH // 2):
                        n = idx_order[b, c, j]
                        wait_pair_full(act, ("idx", b, c, j))
                        if n >= 2:
                            act.wait_ge(rel_read, n - 1)
                        s.activation(rel[:, n % 2, :, 0:w], heads(pair(("idx", b, c, j)), 2)[:, :, 0:w],
                                     ACT.Relu).then_inc(sa_free_act, 1)

            def hgrn(b):
                act.wait_ge(row_in[b % 2], 16 * (b // 2 + 1))
                if b >= 1:
                    act.wait_ge(gg_ready, b)
                r = row[:, b % 2, :]
                s.activation(sig[:, 0:2, :], heads(r[:, HQ0:HQ0 + 1024], 2), ACT.Exp, scale=-1.0)
                s.activation(sig[:, 2, :], r[:, HG0:HG0 + 512], ACT.Exp, scale=-1.0).then_inc(sig_e, 1)
                act.wait_ge(hk_ready, b + 1)
                s.activation(fg[:], fg[:], ACT.Ln).then_inc(logf_ready, 1)
                for what, to in (("hq", hqT), ("hk", hkT)):
                    act.wait_ge(sb_full, sb_use[what, b] + 1)
                    if b >= 1:
                        act.wait_ge(ho_done, HG * b)
                    s.activation(to[:], heads(bank((what, b))), ACT.Copy).then_inc(sb_free, 1)
                act.wait_ge(tail_full, b + 1)
                s.activation(khat[:], SD[:], ACT.Exp).then_inc(tail_out, 1)
                for h in range(HG):
                    n = HG * b + h
                    wait_pair_full(act, ("decay", b, h))
                    if n >= 2:
                        act.wait_ge(ke_ready, n - 1)
                        act.wait_ge(qe_ready, n - 1)
                    s.activation(decay[:, h % 2], heads(pair(("decay", b, h)), NM), ACT.Exp).then_inc(sa_free_act, 1)
                act.wait_ge(ho_done, HG * (b + 1))
                if b >= 1:
                    act.wait_ge(mix_ready, 2 * b)
                s.activation(osb[:], heads(SC[:]), ACT.Copy).then_inc(ho_out, 1)
                act.wait_ge(ho_out, b + 1)
                for h in range(HG):
                    last = s.activation(osq[:, h, :], osb[:, h, :], ACT.Square, accum_out=hss[:, h:h + 1])
                last.then_inc(hss_ready, 1)

            def attention(b):
                for h in range(HEADS):
                    act.wait_ge(nmx_ready, HEADS * b + h + 1)
                    pr = prob[:, h % 2, 0:NK(b)]
                    s.activation(pr, pr, ACT.Exp, bias=nmx[:, h:h + 1], scale=SM_SCALE,
                                 accum_out=den[:, h:h + 1]).then_inc(prob_ready, 1)
                    for c in range(NCH(b)):
                        key = ("pT", b, h, c)
                        w = min(512, NK(b) - 512 * c)
                        m = pt_order[b, h, c]
                        act.wait_ge(sb_full, sb_use[key] + 1)
                        if m >= 2:
                            act.wait_ge(pv_done, m - 1)
                        s.activation(pT[:, m % 2, 0:w], bank(key)[:, 0:w], ACT.Copy).then_inc(sb_free, 1)

            prep(0)
            for b in range(NB):
                if b + 1 < NB:
                    prep(b + 1)
                    if b + 1 >= 2:
                        idx(b + 1)
                hgrn(b)
                attention(b)

        @block.vector
        def _(dve):
            v = nc.vector
            link = linker(dve, dve_step)
            v.memset(sign[:, 0:1], -1.0)
            v.memset(sign[:, 1:2], 1.0)
            v.memset(goal[:, 0:1], -TOPK - 0.5)
            v.memset(goal[:, 1:2], TOPK + 0.5)
            link(v.memset(state[:], 0.0))
            dve.wait_ge(const_in, 8 * 16)
            link(v.tensor_tensor(lbw[:], lb[:, 0, :], lb[:, 1, :], ALU.max))
            v.tensor_tensor(lb[:, 0, :], lb[:, 0, :], lbw[:], ALU.subtract)
            v.tensor_tensor(lb[:, 1, :], lb[:, 1, :], lbw[:], ALU.subtract).then_inc(bounds_step, 1)
            dve.wait_ge(bounds_step, 2)
            link(v.tensor_tensor(lbw[:], lb[:, 0, :], lb[:, 1, :], ALU.add))
            link(v.reciprocal(lbw[:], lbw[:]))
            link(v.tensor_tensor(lb[:, 0, :], lb[:, 0, :], lbw[:], ALU.mult))
            v.tensor_scalar(lb[:, 1, :], lb[:, 0, :], -1.0, 1.0, ALU.mult, ALU.add).then_inc(lb_ready, 1)

            def accumulate(b):
                for c in range(NCH(b)):
                    w = min(512, NK(b) - 512 * c)
                    to = score[:, 512 * c:512 * c + w]
                    for j in range(IH // 2):
                        n = idx_order[b, c, j]
                        wait_pair_read(dve, use["idx", b, c, j])
                        for r in range(2):
                            x, wi = rel[:, n % 2, r, 0:w], wis[:, b % 2, 2 * j + r:2 * j + r + 1]
                            if j == 0 and r == 0:
                                link(v.tensor_scalar(to, x, wi, None, ALU.mult))
                            elif r == 0:
                                link(v.scalar_tensor_tensor(to, x, wi, to, ALU.mult, ALU.add))
                            else:
                                v.scalar_tensor_tensor(to, x, wi, to, ALU.mult, ALU.add).then_inc(rel_read, 1)
                                dve.wait_ge(rel_read, n + 1)

            def halve(t):
                link(v.tensor_scalar(mid[:], ends[:, 0:1], ends[:, 1:2], 0.5, ALU.add, ALU.mult))
                link(v.tensor_scalar(above[:, 0:NK(t)], score[:, 0:NK(t)], mid[:, 0:1], None, ALU.is_gt, ALU.add,
                                     accum_out=cnt[:]))
                link(v.scalar_tensor_tensor(side[:], sign[:], cnt[:, 0:1], goal[:], ALU.mult, ALU.is_gt))
                link(v.copy_predicated(ends[:], side[:], mid[:].broadcast_to([P, 2])))

            def take8(t):
                yield v.max(top8[:], score[:, 0:NK(t)])
                yield v.tensor_scalar(use8[:], iota8[:], left[:, 0:1], None, ALU.is_lt)
                yield v.memset(want8[:], TAKEN)
                yield v.copy_predicated(want8[:], use8[:], top8[:])
                yield v.match_replace(score[:, 0:NK(t) + 8], want8[:], score[:, 0:NK(t) + 8], TAKEN)

            def topk_part(t, part):
                own = slice(t * P, (t + 1) * P)
                if t < 2:
                    if part == 0:
                        if t:
                            v.memset(bias[:, t % 2, 0:t * P], 0.0)
                        v.tensor_copy(bias[:, t % 2, own], causal[:]).then_inc(bias_ready, 1)
                    return
                if part == 0:
                    v.tensor_reduce(ends[:, 0:1], score[:, 0:NK(t)], AX_X, ALU.max)
                    link(v.tensor_reduce(ends[:, 1:2], score[:, 0:NK(t)], AX_X, ALU.min))
                    link(v.tensor_tensor(score[:, own], score[:, own], causal[:], ALU.add))
                elif part < 10:
                    for _ in range(2 if part <= ITERS - 9 else 1):
                        halve(t)
                elif part == 10:
                    v.memset(score[:, NK(t):NK(t) + 8], TAKEN)
                    link(v.tensor_scalar(above[:, 0:NK(t)], score[:, 0:NK(t)], ends[:, 0:1], None, ALU.is_gt,
                                         ALU.add, accum_out=cnt[:]))
                    v.tensor_scalar(left[:], cnt[:], -1.0, float(TOPK), ALU.mult, ALU.add).then_inc(left_ready, 1)
                    link(v.scalar_tensor_tensor(score[:, 0:NK(t)], above[:, 0:NK(t)], TAKEN, score[:, 0:NK(t)],
                                                ALU.mult, ALU.add))
                else:
                    for ins in take8(t):
                        link(ins)
                    dve.wait_ge(left_max, t - 1)
                    link(v.tensor_copy(left_int[:], left_all[:]))
                    most = dve.value_load(left_int[0:1, 0:1], min_val=0, max_val=TOPK)
                    with dve.If(most > 8):
                        with dve.Fori(8, most, 8):
                            v.tensor_scalar(left[:], left[:], -8.0, None, ALU.add)
                            dve.drain()
                            for _ in take8(t):
                                dve.drain()
                    v.tensor_scalar(bias[:, t % 2, 0:NK(t)], score[:, 0:NK(t)], 2.0 / 3 * TAKEN, NEG, ALU.is_gt,
                                    ALU.mult).then_inc(bias_ready, 1)

            def hgrn(b, parts):
                dve.wait_ge(sig_e, b + 1)
                link(v.tensor_scalar(sig[:], sig[:], 1.0, None, ALU.add))
                v.reciprocal(sig[:], sig[:]).then_inc(sig_ready, 1)

                def query(h):
                    n = HG * b + h
                    wait_pair_read(dve, use["decay", b, h])
                    dve.wait_ge(sb_free, sb_use["hk", b] + 1)
                    v.tensor_copy(elast[:, h:h + 1], decay[:, h % 2, NM - 1, P - 1:P])
                    if n >= 2:
                        dve.wait_ge(ho_done, n - 1)
                    v.tensor_tensor(qe[:, h % 2], decay[:, h % 2], hqT[:, h:h + 1, :].broadcast_to([P, NM, P]),
                                    ALU.mult).then_inc(qe_ready, 1)

                def levels(h):
                    n = HG * b + h
                    wait_pair_full(dve, ("level", b, h))
                    if n >= 2:
                        dve.wait_ge(ho_done, n - 1)
                    v.tensor_tensor(am[:, h % 2], heads(pair(("level", b, h)), NM), pick[:], ALU.mult)\
                     .then_inc(sa_free_dve, 1)

                query(0)
                for h in range(HG):
                    if h + 1 < HG:
                        query(h + 1)
                    levels(h)
                    parts(h)
                dve.wait_ge(kv_done, b + 1)
                for h in range(HG):
                    last = v.scalar_tensor_tensor(state[:, h, :], state[:, h, :], elast[:, h:h + 1], heads(SD[:])[:, h, :],
                                                  ALU.mult, ALU.add)
                last.then_inc(state_ready, 1)
                dve.wait_ge(hrstd_ready, b + 1)
                dve.wait_ge(gg_ready, b + 1)
                if b >= 2:
                    dve.wait_ge(stored[b % 2], 16 * (b // 2))
                for h in range(HG):
                    last = v.scalar_tensor_tensor(mix[:, b % 2, 512 + h * HK:512 + (h + 1) * HK], osb[:, h, :],
                                                  hrstd[:, h:h + 1], gg[:, h * HK:(h + 1) * HK], ALU.mult, ALU.mult)
                last.then_inc(mix_ready, 1)

            def attention(b, parts):
                for h in range(HEADS):
                    back = HEADS * b + h - 2
                    if back >= 0:
                        bb, hh = divmod(back, HEADS)
                        dve.wait_ge(sb_full, sb_use["pT", bb, hh, NCH(bb) - 1] + 1)
                    dve.wait_ge(bias_ready, b + 1)
                    for p in range(pairs_of(b)):
                        key = ("att", b, h, p)
                        w = min(1024, NK(b) - 1024 * p)
                        cols = slice(1024 * p, 1024 * p + w)
                        wait_pair_full(dve, key)
                        v.tensor_tensor_reduce(prob[:, h % 2, cols], pair(key)[:, 0:w], bias[:, b % 2, cols], 1.0,
                                               TAKEN, ALU.add, ALU.max, mxp[:, h, p:p + 1]).then_inc(sa_free_dve, 1)
                    wait_pair_read(dve, use[key])
                    if pairs_of(b) == 2:
                        link(v.tensor_tensor(mxp[:, h, 0:1], mxp[:, h, 0:1], mxp[:, h, 1:2], ALU.max))
                    v.tensor_scalar(nmx[:, h:h + 1], mxp[:, h, 0:1], -SM_SCALE, None, ALU.mult).then_inc(nmx_ready, 1)
                    parts(HG + h)
                dve.wait_ge(pv_done, pt_order[b, HEADS - 1, NCH(b) - 1] + 1)
                link(v.reciprocal(rden[:], den[:]))
                v.tensor_tensor(mix[:, b % 2, 0:512].rearrange("p (h d) -> p h d", d=HD),
                                SC[:].rearrange("p (h d) -> p h d", d=HD),
                                rden[:].unsqueeze(2).broadcast_to([P, HEADS, HD]), ALU.mult).then_inc(mix_ready, 1)

            topk_part(0, 0)
            for b in range(NB):
                def parts(n, t=b + 1):
                    if t < NB:
                        topk_part(t, n)
                if 2 <= b + 1 < NB:
                    accumulate(b + 1)
                hgrn(b, parts)
                attention(b, parts)

        @block.tensor
        def _(pe):
            t = nc.tensor
            pe.wait_ge(const_in, 8 * 16)

            def turn(src, to, n):
                for j in range(n):
                    last = t.transpose(to[:, j * P:(j + 1) * P], src(j), ident[:])
                return last

            def prep(b):
                pe.wait_ge(rows_ready, b + 1)
                for what, c0 in (("q", Q0), ("qi", QI0)):
                    wait_bank_free(pe, (what, b))
                    turn(lambda j: row[:, b % 2, c0 + j * P:c0 + (j + 1) * P], bank((what, b)), 4).then_inc(sb_full, 1)
                if b == 1:
                    pe.wait_ge(keys_out, 1)
                if b >= 2:
                    pe.wait_ge(state_ready, b - 1)
                turn(lambda j: kdup[:, j].rearrange("p n d -> p (n d)"), SD, 3).then_inc(keys_full, 1)

            def idx(b):
                pe.wait_ge(sb_free, sb_use["qi", b] + 1)
                pe.wait_ge(keys_out, b + 1)
                for c in range(NCH(b)):
                    w = min(512, NK(b) - 512 * c)
                    for j in range(IH // 2):
                        key = ("idx", b, c, j)
                        wait_pair_free(pe, key)
                        for r in range(2):
                            half = slice(r * HD, (r + 1) * HD)
                            last = t.matmul(pair(key)[:, 512 * r:512 * r + w], qiT[half, j, :],
                                            KT[half, KV, 512 * c:512 * c + w], start=True, stop=True)
                        last.then_inc(sa_full, 1)

            def hgrn(b):
                v = heads(row[:, b % 2, HI0:HI0 + 512])

                def decays(h):
                    wait_pair_free(pe, ("decay", b, h))
                    for m in range(2):
                        last = t.matmul(pair(("decay", b, h))[:, 512 * m:512 * (m + 1)], fg[:, h * HK:(h + 1) * HK],
                                        sums[:, 4 * m:4 * m + 4, :], start=True, stop=True)
                    last.then_inc(sa_full, 1)

                def levels(h):
                    pe.wait_ge(qe_ready, HG * b + h + 1)
                    pe.wait_ge(ke_ready, HG * b + h + 1)
                    wait_pair_free(pe, ("level", b, h))
                    out = heads(pair(("level", b, h)), NM)
                    for m in range(NM - 1):
                        t.matmul(out[:, m, :], ke[:, h % 2, m, :], qe[:, h % 2, m, :], start=True, stop=True)
                    t.matmul(out[:, NM - 1, :], hkT[:, h, :], hqT[:, h, :], start=True, stop=True).then_inc(sa_full, 1)

                def output(h):
                    if h == 0 and b >= 1:
                        pe.wait_ge(mix_ready, 2 * b)
                        pe.wait_ge(state_ready, b)
                    to = heads(SC[:])[:, h, :]
                    t.matmul(to, qe[:, h % 2, NM - 1, :], state[:, h, :], start=True, stop=False)
                    wait_pair_read(pe, use["level", b, h])
                    for m in range(NM):
                        last = t.matmul(to, am[:, h % 2, m, :], v[:, h, :], start=False, stop=(m == NM - 1))
                    last.then_inc(ho_done, 1)

                for what, src, ready in (("hq", hq, hq_ready), ("hk", hk, hk_ready)):
                    pe.wait_ge(ready, b + 1)
                    wait_bank_free(pe, (what, b))
                    turn(lambda j: src[:, j * P:(j + 1) * P], bank((what, b)), HG).then_inc(sb_full, 1)
                pe.wait_ge(logf_ready, b + 1)
                pe.wait_ge(keys_out, min(b + 2, NB))
                t.matmul(SD[:], sums[:, NM, :], fg[:], start=True, stop=True).then_inc(tail_full, 1)
                decays(0)
                for h in range(HG):
                    if h + 1 < HG:
                        decays(h + 1)
                    if h == 0:
                        pe.wait_ge(sb_free, sb_use["hk", b] + 1)
                    levels(h)
                    if h >= 1:
                        output(h - 1)
                output(HG - 1)
                pe.wait_ge(khat_ready, b + 1)
                for h in range(HG):
                    last = t.matmul(heads(SD[:])[:, h, :], khat[:, h * HK:(h + 1) * HK], v[:, h, :], start=True, stop=True)
                last.then_inc(kv_done, 1)

            def attention(b):
                def scores(h):
                    half, g = slice(h % 2 * HD, (h % 2 + 1) * HD), h // GROUP
                    for p in range(pairs_of(b)):
                        key = ("att", b, h, p)
                        wait_pair_free(pe, key)
                        for k0 in range(1024 * p, min(NK(b), 1024 * (p + 1)), 512):
                            w = min(512, NK(b) - k0)
                            last = t.matmul(pair(key)[:, k0 - 1024 * p:k0 - 1024 * p + w], qT[half, b % 2, h // 2, :],
                                            KT[half, g, k0:k0 + w], start=True, stop=True)
                        last.then_inc(sa_full, 1)

                def blocks(c):
                    return range(4 * c, min(4 * c + 4, b + 1))

                def turn_probs(h, c):
                    wait_bank_free(pe, ("pT", b, h, c))
                    turn(lambda j: prob[:, h % 2, (4 * c + j) * P:(4 * c + j + 1) * P], bank(("pT", b, h, c)),
                         len(blocks(c))).then_inc(sb_full, 1)

                def values(h, c):
                    g = h // GROUP
                    pe.wait_ge(sb_free, sb_use["pT", b, h, c] + 1)
                    if h == 0 and c == 0:
                        pe.wait_ge(ho_out, b + 1)
                    for kb in blocks(c):
                        last = t.matmul(SC[:, h * HD:(h + 1) * HD], pT[:, pt_order[b, h, c] % 2, (kb % 4) * P:(kb % 4 + 1) * P],
                                        V[:, kb, g * HD:(g + 1) * HD], start=(kb == 0), stop=(kb == b))
                    last.then_inc(pv_done, 1)

                scores(0)
                for h in range(HEADS):
                    if h + 1 < HEADS:
                        scores(h + 1)
                    pe.wait_ge(prob_ready, HEADS * b + h + 1)
                    for c in range(NCH(b)):
                        turn_probs(h, c)
                        if c:
                            values(h, c - 1)
                    values(h, NCH(b) - 1)

            prep(0)
            for b in range(NB):
                if b + 1 < NB:
                    prep(b + 1)
                    if b + 1 >= 2:
                        idx(b + 1)
                hgrn(b)
                attention(b)

def dense_phase(nc, a, mix_d, out):
    with ExitStack() as ctx:
        def sb(name, shape, dt=F32):
            return ctx.enter_context(nc.sbuf_tensor(name, shape, dt))

        def sem(name):
            return ctx.enter_context(nc.semaphore(name))

        hid_hi = sb("hid_hi", [P, NF, SB], F32R)
        hid_lo = sb("hid_lo", [P, NF, SB], F32R)
        h_hi = sb("h2_hi", [P, KD, SB], F32R)
        h_lo = sb("h2_lo", [P, KD, SB], F32R)
        w_raw = sb("wd_raw", [P, 2 * D])
        w_hi = sb("wd_hi", [P, 2, 2 * D], F32R)
        w_lo = sb("wd_lo", [P, 2, 2 * D], F32R)
        xs = sb("xs", [P, TS, D])
        tb = sb("tb", [P, 2, D])
        act_up = sb("act_up", [P, 2, SB])
        g_mix = sb("g_mix", [P, D])
        g_ffn = sb("g_ffn", [P, D])
        g_out = sb("g_out", [P, D])
        ident = sb("ident_d", [P, P])
        ss = sb("ss_d", [P, 12])
        var = sb("var_d", [P, 12])
        rstd = sb("rstd_d", [P, 12])
        mhalf = sb("mhalf_d", [P, 1])
        eps = sb("eps_d", [P, 1])
        ps = ctx.enter_context(nc.psum_tensor("ps_dense", [P, 8, 512], F32))

        const_in = sem("d_const_in")
        pool_step = sem("d_pool_step")
        mix_in = [sem("d_mix_in0"), sem("d_mix_in1")]
        x_in = sem("d_x_in")
        w_in = sem("d_w_in")
        w_hi_ready = sem("d_w_hi_ready")
        w_lo_ready = sem("d_w_lo_ready")
        rows_unit = sem("d_rows_unit")
        turned = sem("d_turned")
        hi_ready = sem("d_hi_ready")
        lo_ready = sem("d_lo_ready")
        rows_done = sem("d_rows_done")
        ss_rows = sem("d_ss_rows")
        rstd_rows = sem("d_rstd_rows")
        scaled = sem("d_scaled")
        added = sem("d_added")
        ss_x1 = sem("d_ss_x1")
        rstd_x1 = sem("d_rstd_x1")
        xn_ready = sem("d_xn_ready")
        up_done = sem("d_up_done")
        silu_ready = sem("d_silu_ready")
        hidden = sem("d_hidden")
        hid_hi_ready = sem("d_hid_hi_ready")
        hid_lo_ready = sem("d_hid_lo_ready")
        stored = sem("d_stored")

        def wait(eng, semaphore, value):
            if not isinstance(value, int) or value > 0:
                eng.wait_ge(semaphore, value)

        units = [("out", (2 * m, 2 * m + 1)) for m in range(KD // 2)]
        up0 = len(units)
        units += [("up", f) for f in range(NF)]
        down0 = len(units)
        units += [("down", (2 * m, 2 * m + 1)) for m in range(NF // 2 - 1)]
        units += [("down", (NF - 2,)), ("down", (NF - 1,))]
        NU = len(units)
        assert NU % 2 == 0

        def wait_unit(eng, s, k):
            if units[k][0] == "up":
                wait(eng, up_done, NF * s + k - up0 + 1)
            elif k in (up0 - 1, NU - 1):
                wait(eng, rows_done, 2 * TS * s + (TS if k < up0 else 2 * TS))
            else:
                m = k + 1 if k < up0 else k - down0 + up0
                wait(eng, rows_unit, (NU - NF - 2) * s + m)

        def width(k):
            return D * len(units[k][1]) if units[k][0] != "up" else 2 * D

        block = ctx.enter_context(nc.Block())

        @block.sync
        def _(sp):
            for to, name in ((ident, "c_ident"), (g_mix, "norm_post_mix"), (g_ffn, "norm_pre_ffn"),
                             (g_out, "norm_post_ffn")):
                src = a[name] if name == "c_ident" else a[name].broadcast_to([P, D])
                sp.dma_start(to[:], src).then_inc(const_in, 16)
            def superblock(s):
                def load_unit(k):
                    wait(sp, w_lo_ready, NU * s + k)
                    kind, what = units[k]
                    if kind == "up":
                        src = a["w_gu"][what]
                    else:
                        w = a["w_out"] if kind == "out" else a["w_down"]
                        src = w[what[0] * P:(what[-1] + 1) * P, :].rearrange("(j p) n -> p j n", p=P)
                    to = w_raw[:, 0:width(k)]
                    if kind != "up":
                        to = to.rearrange("p (j n) -> p j n", n=D)
                    sp.dma_start(to, src).then_inc(w_in, 16)

                load_unit(0)
                for i in range(TS):
                    if i < 2:
                        wait(sp, added, 2 * TS * s)
                    else:
                        wait(sp, turned, 4 * TS * s + 2 * (i - 1))
                    sp.dma_start(tb[:, i % 2, :], mix_d[bass.ds(s * SB + i * P, P), :])\
                      .then_inc(mix_in[i % 2], 16)
                    if i == 1:
                        wait(sp, stored, 16 * TS * s)
                        sp.dma_start(xs[:], a["x"][0, bass.ds(s * SB, SB), :].rearrange("(i p) d -> p i d", p=P))\
                          .then_inc(x_in, 16)
                for k in range(1, NU):
                    load_unit(k)
                for i in range(TS):
                    wait(sp, added, 2 * TS * s + TS + i + 1)
                    sp.dma_start(out[0, bass.ds(s * SB + i * P, P), :], xs[:, i, :]).then_inc(stored, 16)

            superblock(0)
            with sp.Fori(1, NS) as s:
                superblock(s)
            wait(sp, stored, 16 * TS * NS)

        @block.gpsimd
        def _(pool):
            nc.gpsimd.memset(eps[:], EPS)
            nc.gpsimd.memset(mhalf[:], -0.5).then_inc(pool_step, 1)
            wait(pool, pool_step, 1)
            def superblock(s):
                def root(col, ready, n, done, step):
                    c = slice(col, col + 1)
                    wait(pool, ready, n)
                    nc.gpsimd.tensor_tensor(var[:, c], ss[:, c], eps[:], ALU.add).then_inc(pool_step, 1)
                    wait(pool, pool_step, 12 * s + step + 2)
                    nc.gpsimd.tensor_tensor(rstd[:, c], var[:, c], mhalf[:, 0:1], ALU.pow).then_inc(done, 1)

                root(0, ss_rows, 8 * s + 1, rstd_rows, 0)
                for i in range(TS):
                    if i + 1 < TS:
                        root(i + 1, ss_rows, 8 * s + i + 2, rstd_rows, 2 * i + 1)
                    root(4 + i, ss_x1, 4 * s + i + 1, rstd_x1, 2 * i + 2 - (i == TS - 1))
                for i in range(TS):
                    root(8 + i, ss_rows, 8 * s + TS + i + 1, rstd_rows, 8 + i)

            superblock(0)
            with pool.Fori(1, NS) as s:
                superblock(s)

        def bank(n):
            return ps[:, n, :].rearrange("p (k t) -> p k t", k=4)

        @block.scalar
        def _(act):
            def superblock(s):
                def split_w(k):
                    if k >= NU:
                        return
                    wait(act, w_in, 16 * (NU * s + k + 1))
                    if k < 2:
                        wait(act, rows_done, 2 * TS * s)
                    else:
                        wait_unit(act, s, k - 2)
                    nc.scalar.activation(w_hi[:, k % 2, 0:width(k)], w_raw[:, 0:width(k)], ACT.Copy)\
                      .then_inc(w_hi_ready, 1)

                def split_turned(to, n, i):
                    wait(act, turned, 4 * TS * s + n + 1)
                    k = 4 * (n % 2)
                    nc.scalar.activation(to[:, k:k + 4, i * P:(i + 1) * P], bank(2 * i + n % 2),
                                         ACT.Copy).then_inc(hi_ready, 1)

                def square_rows(i, late):
                    wait(act, rows_done, 2 * TS * s + TS * late + i + 1)
                    if late:
                        wait(act, added, 2 * TS * s + TS + max(i - 1, 0))
                        wait(act, turned, 4 * TS * (s + 1))
                    else:
                        wait(act, turned, 4 * TS * s + 2 * TS + 2 * max(i - 1, 0))
                    nc.scalar.activation(tb[:, i % 2, :], ps[:, 2 * i:2 * i + 2, :].rearrange("p a b -> p (a b)"),
                                         ACT.Square, scale=D ** -0.5, accum_out=ss[:, 8 * late + i:8 * late + i + 1])\
                      .then_inc(ss_rows, 1)

                def square_x1(i):
                    wait(act, added, 2 * TS * s + i + 1)
                    nc.scalar.activation(tb[:, i % 2, :], xs[:, i, :], ACT.Square, scale=D ** -0.5,
                                         accum_out=ss[:, 4 + i:5 + i]).then_inc(ss_x1, 1)

                split_w(0)
                split_w(1)
                for i in range(TS):
                    for k in range(2):
                        split_turned(hid_hi, 2 * i + k, i)
                for k in range(up0):
                    split_w(k + 2)
                square_rows(0, 0)
                for i in range(TS):
                    if i + 1 < TS:
                        square_rows(i + 1, 0)
                    square_x1(i)
                    for k in range(2):
                        split_turned(h_hi, 2 * TS + 2 * i + k, i)
                for f in range(NF):
                    wait(act, up_done, NF * s + f + 1)
                    wait(act, hid_lo_ready, NF * s + max(f - 1, 0))
                    nc.scalar.activation(act_up[:, f % 2, :], ps[:, 2 * (f % 4), :], ACT.Silu)\
                      .then_inc(silu_ready, 1)
                    wait(act, hidden, NF * s + f + 1)
                    nc.scalar.activation(hid_hi[:, f, :], act_up[:, f % 2, :], ACT.Copy).then_inc(hid_hi_ready, 1)
                    split_w(up0 + f + 2)
                for k in range(down0, NU):
                    split_w(k + 2)
                for i in range(TS):
                    square_rows(i, 1)

            superblock(0)
            with act.Fori(1, NS) as s:
                superblock(s)

        @block.vector
        def _(dve):
            wait(dve, const_in, 64)
            def superblock(s):
                def split_w(k):
                    if k >= NU:
                        return
                    wait(dve, w_hi_ready, NU * s + k + 1)
                    w = slice(0, width(k))
                    nc.vector.tensor_tensor(w_lo[:, k % 2, w], w_raw[:, w], w_hi[:, k % 2, w].bitcast(F32),
                                            ALU.subtract).then_inc(w_lo_ready, 1)

                def split_turned(to_hi, to_lo, n, i):
                    wait(dve, hi_ready, 4 * TS * s + n + 1)
                    k = 4 * (n % 2)
                    nc.vector.tensor_tensor(to_lo[:, k:k + 4, i * P:(i + 1) * P], bank(2 * i + n % 2),
                                            to_hi[:, k:k + 4, i * P:(i + 1) * P].bitcast(F32),
                                            ALU.subtract).then_inc(lo_ready, 1)

                def add_rows(i, late, gain):
                    col = 8 * late + i
                    wait(dve, rstd_rows, 2 * TS * s + TS * late + i + 1)
                    nc.vector.scalar_tensor_tensor(tb[:, i % 2, :], ps[:, 2 * i:2 * i + 2, :].rearrange("p a b -> p (a b)"),
                                                   rstd[:, col:col + 1], gain[:], ALU.mult, ALU.mult)\
                      .then_inc(scaled, 1)
                    wait(dve, scaled, 2 * TS * s + TS * late + i + 1)
                    nc.vector.tensor_tensor(xs[:, i, :], xs[:, i, :], tb[:, i % 2, :], ALU.add).then_inc(added, 1)

                split_w(0)
                split_w(1)
                for i in range(TS):
                    for k in range(2):
                        split_turned(hid_hi, hid_lo, 2 * i + k, i)
                for k in range(up0):
                    split_w(k + 2)
                wait(dve, x_in, 16 * (s + 1))
                add_rows(0, 0, g_mix)
                for i in range(TS):
                    if i + 1 < TS:
                        add_rows(i + 1, 0, g_mix)
                    wait(dve, rstd_x1, TS * s + i + 1)
                    nc.vector.scalar_tensor_tensor(tb[:, i % 2, :], xs[:, i, :], rstd[:, 4 + i:5 + i], g_ffn[:],
                                                   ALU.mult, ALU.mult).then_inc(xn_ready, 1)
                    for k in range(2):
                        split_turned(h_hi, h_lo, 2 * TS + 2 * i + k, i)
                for f in range(NF):
                    wait(dve, silu_ready, NF * s + f + 1)
                    au = act_up[:, f % 2, :]
                    nc.vector.tensor_tensor(au, au, ps[:, 2 * (f % 4) + 1, :], ALU.mult).then_inc(hidden, 1)
                    wait(dve, hid_hi_ready, NF * s + f + 1)
                    nc.vector.tensor_tensor(hid_lo[:, f, :], au, hid_hi[:, f, :].bitcast(F32),
                                            ALU.subtract).then_inc(hid_lo_ready, 1)
                    split_w(up0 + f + 2)
                for k in range(down0, NU):
                    split_w(k + 2)
                for i in range(TS):
                    add_rows(i, 1, g_out)

            superblock(0)
            with dve.Fori(1, NS) as s:
                superblock(s)

        @block.tensor
        def _(pe):
            wait(pe, const_in, 64)
            def superblock(s):
                def turn(i, n):
                    for k in range(2):
                        for q in range(4):
                            last = nc.tensor.transpose(ps[:, 2 * i + k, q * P:(q + 1) * P],
                                                       tb[:, i % 2, (4 * k + q) * P:(4 * k + q + 1) * P], ident[:])
                        last.then_inc(turned, 1)

                def rows(k, c, j, first, final):
                    for i in range(TS):
                        tok = slice(i * P, (i + 1) * P)
                        for lhs, w, start, stop in ((hid_hi, w_hi, True, False), (hid_hi, w_lo, False, False),
                                                    (hid_lo, w_hi, False, True)):
                            for n in range(2):
                                last = nc.tensor.matmul(ps[:, 2 * i + n, :], lhs[:, c, tok],
                                                        w[:, k % 2, j * D + n * 512:j * D + n * 512 + 512],
                                                        start=start and first, stop=stop and final)
                        if final:
                            last.then_inc(rows_done, 1)
                    return last

                def product(k0, k1, last_chunk):
                    for k in range(k0, k1):
                        wait(pe, w_lo_ready, NU * s + k + 1)
                        for j, c in enumerate(units[k][1]):
                            last = rows(k, c, j, c == 0, c == last_chunk)
                        if c != last_chunk:
                            last.then_inc(rows_unit, 1)

                wait(pe, added, 2 * TS * s)
                for i in range(TS):
                    wait(pe, mix_in[i % 2], 16 * (2 * s + i // 2 + 1))
                    turn(i, 2 * i)
                wait(pe, lo_ready, 4 * TS * s + 2 * TS)
                product(0, up0, KD - 1)
                for i in range(TS):
                    wait(pe, xn_ready, TS * s + i + 1)
                    turn(i, 2 * TS + 2 * i)
                wait(pe, lo_ready, 4 * TS * (s + 1))
                for f in range(NF):
                    k = up0 + f
                    wait(pe, w_lo_ready, NU * s + k + 1)
                    if f >= 4:
                        wait(pe, hidden, NF * s + f - 3)
                    for m in range(2):
                        for c in range(KD):
                            w = slice((m * KD + c) * P, (m * KD + c + 1) * P)
                            o = ps[:, 2 * (f % 4) + m, :]
                            nc.tensor.matmul(o, w_hi[:, k % 2, w], h_hi[:, c, :], start=(c == 0), stop=False)
                            nc.tensor.matmul(o, w_hi[:, k % 2, w], h_lo[:, c, :], start=False, stop=False)
                            last = nc.tensor.matmul(o, w_lo[:, k % 2, w], h_hi[:, c, :], start=False,
                                                    stop=(c == KD - 1))
                    last.then_inc(up_done, 1)
                wait(pe, hid_lo_ready, NF * (s + 1))
                product(down0, NU, NF - 1)

            superblock(0)
            with pe.Fori(1, NS) as s:
                superblock(s)
def layout_gu(w_gate, w_up):
    w = np.stack([w_gate, w_up]).reshape(2, KD, P, NF, P)
    return np.ascontiguousarray(w.transpose(3, 2, 0, 1, 4)).reshape(NF, P, 2 * KD * P)


def build(nc, a, out):
    proj_d = nc.dram_tensor("proj_d", [T, IN_W], F32, kind="Internal").ap()
    mix_d = nc.dram_tensor("mix_d", [T, D], F32, kind="Internal").ap()
    project_phase(nc, a, proj_d)
    mix_phase(nc, a, proj_d, mix_d)
    dense_phase(nc, a, mix_d, out)


_INS = ["x", "norm_pre_mix", "w_in", "w_out", "norm_post_mix", "hg_lower_bound", "hg_out_norm",
        "norm_pre_ffn", "w_gu", "w_down", "norm_post_ffn"]


def kernel(**inputs):
    import concourse.bacc as bacc
    from concourse.bass_utils import run_bass_kernel_spmd

    given = {n: np.ascontiguousarray(inputs[n]) for n in inputs}
    arrays = {n: given[n] for n in ("x", "norm_pre_mix", "norm_post_mix", "hg_lower_bound", "hg_out_norm",
                                    "norm_pre_ffn", "norm_post_ffn")}
    arrays["w_in"] = np.ascontiguousarray(given["w_in"][0].reshape(KD, P, NC_IN, CW).transpose(2, 1, 0, 3))
    arrays["w_out"] = given["w_out"][0]
    arrays["w_gu"] = layout_gu(given["w_gate"][0], given["w_up"][0])
    arrays["w_down"] = given["w_down"][0]
    arrays.update(shape_constants())

    nc = bacc.Bacc("TRN2", target_bir_lowering=False, num_devices=1)
    a = {n: nc.dram_tensor(f"in_{n}", v.shape, mybir.dt.from_np(v.dtype), kind="ExternalInput").ap()
         for n, v in arrays.items()}
    out = nc.dram_tensor("out_y", (1, T, D), F32, kind="ExternalOutput").ap()
    build(nc, a, out)
    r = run_bass_kernel_spmd(nc, [{f"in_{n}": v for n, v in arrays.items()}], core_ids=[0])
    return r.results[0]["out_y"]
```

```python
from contextlib import ExitStack

import numpy as np

import concourse.bass as bass
from concourse import mybir

F32 = mybir.dt.float32
F32R = mybir.dt.float32r
BF16 = mybir.dt.bfloat16
ALU = mybir.AluOpType
ACT = mybir.ActivationFunctionType
AX_X = mybir.AxisListType.X

P = 128
T, D = 2048, 1024
NB = T // P
KD = D // P
HEADS, KV, HD = 8, 2, 64
GROUP = HEADS // KV
IH = 8
TOPK = 256
HG, HK = 4, 128
FF = 2816
NF = FF // P
EPS = 1e-6
ROPE = 8
THETA = 500000.0
SPLITS = (512, 128, 128, 512, 64, 8, 512, 512, 512, 512)
Q0, K0, V0, QI0, KI0, WI0, HQ0, HF0, HI0, HG0 = [sum(SPLITS[:n]) for n in range(10)]
IN_W = sum(SPLITS)
NC_IN = 10
CW = IN_W // NC_IN
IDX_SCALE = (IH ** -0.5) * (HD ** -0.5)
SM_SCALE = HD ** -0.5
NEG = -1.0e30
TAKEN = -3.0e38
LEVELS = (64, 32, 16, 8, 4, 2, 1)
NM = len(LEVELS) + 1
SB = 512
NS = T // SB
TS = SB // P


def shape_constants():
    t = np.arange(P)
    ident = np.eye(P, dtype=np.float32)
    sums = np.zeros((P, NM + 1, P), np.float32)
    pick = np.zeros((P, NM, P), np.float32)
    u, tt = t[:, None], t[None, :]
    for n, h in enumerate(LEVELS):
        mid = (tt // (2 * h)) * 2 * h + h
        sums[:, n] = np.where(tt >= mid, (u >= mid) & (u <= tt), (u > tt) & (u < mid))
        pick[:, n] = (u // (2 * h) == tt // (2 * h)) & (u % (2 * h) < h) & (tt % (2 * h) >= h)
    sums[:, NM - 1] = u <= tt
    sums[:, NM] = u > tt
    pick[:, NM - 1] = u == tt
    causal = np.where(tt <= u, 0.0, NEG).astype(np.float32)
    half = ROPE
    inv = THETA ** (-np.arange(half, dtype=np.float32) / np.float32(half))
    ang = np.arange(T, dtype=np.float32)[:, None] * inv[None, :].astype(np.float32)
    rope = np.stack([np.cos(ang), np.sin(ang)], 1).astype(np.float32)
    rope = np.ascontiguousarray(rope.reshape(NB, P, 2, half).transpose(1, 0, 2, 3))
    return dict(c_ident=ident, c_sums=sums, c_pick=pick, c_causal=causal, c_rope=rope)


def project_phase(nc, a, proj_d):
    with ExitStack() as ctx:
        def sb(name, shape, dt=F32):
            return ctx.enter_context(nc.sbuf_tensor(name, shape, dt))

        def sem(name):
            return ctx.enter_context(nc.semaphore(name))

        h_hi = sb("h_hi", [P, KD, T], F32R)
        h_lo = sb("h_lo", [P, KD, T], F32R)
        w_raw = sb("w_raw", [P, KD, CW])
        w_hi = sb("w_hi", [P, 2, KD, CW], F32R)
        w_lo = sb("w_lo", [P, 2, KD, CW], F32R)
        stage = sb("stage", [P, 2, 2, CW])
        xt = sb("xt", [P, 2, D])
        gain = sb("gain_in", [P, D])
        ident = sb("ident_p", [P, P])
        ss = sb("ss_p", [P, 2])
        var = sb("var_p", [P, 2])
        rstd = sb("rstd_p", [P, 2])
        mhalf = sb("mhalf_p", [P, 2])
        junk = stage[:, :, :, :].rearrange("p a b c -> p (a b c)")[:, 0:D]
        ps = ctx.enter_context(nc.psum_tensor("ps_proj", [P, 8, 512], F32))

        const_in = sem("p_const_in")
        x_in = [sem("p_x_in0"), sem("p_x_in1")]
        ss_ready = sem("p_ss_ready")
        pool_step = sem("p_pool_step")
        rstd_ready = sem("p_rstd_ready")
        xn_ready = sem("p_xn_ready")
        xT_ready = sem("p_xT_ready")
        h_hi_ready = sem("p_h_hi_ready")
        bank_free = sem("p_bank_free")
        w_in = sem("p_w_in")
        w_hi_ready = sem("p_w_hi_ready")
        w_lo_ready = sem("p_w_lo_ready")
        tile_done = sem("p_tile_done")
        staged = sem("p_staged")
        stored = [sem("p_stored0"), sem("p_stored1")]
        block = ctx.enter_context(nc.Block())

        @block.sync
        def _(sp):
            sp.dma_start(ident[:], a["c_ident"]).then_inc(const_in, 16)
            sp.dma_start(gain[:], a["norm_pre_mix"].broadcast_to([P, D])).then_inc(const_in, 16)
            for i in range(NB):
                if i >= 2:
                    sp.wait_ge(xT_ready, 2 * (i - 1))
                sp.dma_start(xt[:, i % 2, :], a["x"][0, i * P:(i + 1) * P, :]).then_inc(x_in[i % 2], 16)
                if i == 1:
                    sp.dma_start(w_raw[:], a["w_in"][0]).then_inc(w_in, 16)

            def store(c, k):
                sp.wait_ge(staged, 16 * c + 2 * k + 2)
                rows = proj_d[2 * k * P:(2 * k + 2) * P, :].rearrange("(i p) e -> p i e", p=P)
                sp.dma_start(rows[:, :, bass.ds(c * CW, CW)], stage[:, k % 2]).then_inc(stored[k % 2], 16)

            with sp.Fori(0, NC_IN - 1) as c:
                sp.wait_ge(w_lo_ready, c + 1)
                sp.dma_start(w_raw[:], a["w_in"][c + 1]).then_inc(w_in, 16)
                for k in range(NB // 2):
                    store(c, k)
            for k in range(NB // 2):
                store(NC_IN - 1, k)
            for half in stored:
                sp.wait_ge(half, 16 * NC_IN * NB // 4)

        @block.gpsimd
        def _(pool):
            nc.gpsimd.memset(mhalf[:], -0.5).then_inc(pool_step, 1)
            pool.wait_ge(pool_step, 1)
            for i in range(NB):
                s = slice(i % 2, i % 2 + 1)
                pool.wait_ge(ss_ready, i + 1)
                nc.gpsimd.tensor_scalar(var[:, s], ss[:, s], 1.0 / D, EPS, ALU.mult, ALU.add).then_inc(pool_step, 1)
                pool.wait_ge(pool_step, i + 2)
                nc.gpsimd.tensor_tensor(rstd[:, s], var[:, s], mhalf[:, s], ALU.pow).then_inc(rstd_ready, 1)

        @block.scalar
        def _(act):
            def square(i):
                act.wait_ge(x_in[i % 2], 16 * (i // 2 + 1))
                if i >= 2:
                    act.wait_ge(rstd_ready, i - 1)
                if i >= 1:
                    act.wait_ge(ss_ready, i)
                nc.scalar.activation(junk, xt[:, i % 2, :], ACT.Square,
                                     accum_out=ss[:, i % 2:i % 2 + 1]).then_inc(ss_ready, 1)

            def split_hi(i):
                for k in range(2):
                    act.wait_ge(xT_ready, 2 * i + k + 1)
                    nc.scalar.activation(h_hi[:, 4 * k:4 * k + 4, i * P:(i + 1) * P],
                                         ps[:, (2 * i + k) % 8, :].rearrange("p (k t) -> p k t", k=4),
                                         ACT.Copy).then_inc(h_hi_ready, 1)
            square(0)
            for i in range(NB):
                if i + 1 < NB:
                    square(i + 1)
                split_hi(i)
            act.wait_ge(w_in, 16)
            nc.scalar.activation(w_hi[:, 0], w_raw[:], ACT.Copy).then_inc(w_hi_ready, 1)

            def evacuate(c, u, first):
                for i in range(NB):
                    act.wait_ge(tile_done, 16 * c + i + 1)
                    if i % 2 == 0 and not (first and i < 4):
                        act.wait_ge(stored[(i // 2) % 2], 16 * (4 * c + i // 4))
                    nc.scalar.activation(stage[:, (i // 2) % 2, i % 2, :], ps[:, i % 8, 0:CW],
                                         ACT.Copy).then_inc(staged, 1)

            def next_hi(c, u, first):
                act.wait_ge(w_in, 16 * (c + 2))
                if not first:
                    act.wait_ge(tile_done, 16 * c)
                nc.scalar.activation(w_hi[:, 1 - u], w_raw[:], ACT.Copy).then_inc(w_hi_ready, 1)

            next_hi(0, 0, True)
            act.wait_ge(ss_ready, NB)
            evacuate(0, 0, True)
            with act.Fori(0, NC_IN // 2 - 1) as j:
                for c, u in ((2 * j + 1, 1), (2 * j + 2, 0)):
                    next_hi(c, u, False)
                    evacuate(c, u, False)
            evacuate(NC_IN - 1, 1, False)

        @block.vector
        def _(dve):
            dve.wait_ge(const_in, 32)

            def normalise(i):
                dve.wait_ge(rstd_ready, i + 1)
                x = xt[:, i % 2, :]
                nc.vector.scalar_tensor_tensor(x, x, rstd[:, i % 2:i % 2 + 1], gain[:], ALU.mult,
                                               ALU.mult).then_inc(xn_ready, 1)

            def split_lo(i):
                for k in range(2):
                    dve.wait_ge(h_hi_ready, 2 * i + k + 1)
                    to = slice(4 * k, 4 * k + 4), slice(i * P, (i + 1) * P)
                    nc.vector.tensor_tensor(h_lo[:, to[0], to[1]],
                                            ps[:, (2 * i + k) % 8, :].rearrange("p (k t) -> p k t", k=4),
                                            h_hi[:, to[0], to[1]].bitcast(F32),
                                            ALU.subtract).then_inc(bank_free, 1)
            normalise(0)
            for i in range(NB):
                if i + 1 < NB:
                    normalise(i + 1)
                split_lo(i)

            def w_low(c, u):
                dve.wait_ge(w_hi_ready, c + 1)
                nc.vector.tensor_tensor(w_lo[:, u], w_raw[:], w_hi[:, u].bitcast(F32),
                                        ALU.subtract).then_inc(w_lo_ready, 1)
            with dve.Fori(0, NC_IN // 2) as j:
                for u in range(2):
                    w_low(2 * j + u, u)

        @block.tensor
        def _(pe):
            pe.wait_ge(const_in, 32)
            for i in range(NB):
                pe.wait_ge(xn_ready, i + 1)
                for k in range(2):
                    n = 2 * i + k
                    if n >= 8:
                        pe.wait_ge(bank_free, n - 7)
                    for q in range(4):
                        last = nc.tensor.transpose(ps[:, n % 8, q * P:(q + 1) * P],
                                                   xt[:, i % 2, (4 * k + q) * P:(4 * k + q + 1) * P], ident[:])
                    last.then_inc(xT_ready, 1)
            pe.wait_ge(bank_free, 2 * NB)

            def chunk(c, u, first):
                pe.wait_ge(w_lo_ready, c + 1)
                for i in range(NB):
                    if not (first and i < 8):
                        pe.wait_ge(staged, 16 * c + i - 7)
                    tok = slice(i * P, (i + 1) * P)
                    out = ps[:, i % 8, 0:CW]
                    for k in range(KD):
                        nc.tensor.matmul(out, h_hi[:, k, tok], w_hi[:, u, k, :], start=(k == 0), stop=False)
                        nc.tensor.matmul(out, h_hi[:, k, tok], w_lo[:, u, k, :], start=False, stop=False)
                        last = nc.tensor.matmul(out, h_lo[:, k, tok], w_hi[:, u, k, :], start=False,
                                                stop=(k == KD - 1))
                    last.then_inc(tile_done, 1)

            chunk(0, 0, True)
            with pe.Fori(0, NC_IN // 2 - 1) as j:
                chunk(2 * j + 1, 1, False)
                chunk(2 * j + 2, 0, False)
            chunk(NC_IN - 1, 1, False)


def mix_phase(nc, a, proj_d, mix_d):
    NK = lambda b: (b + 1) * P
    NCH = lambda b: -(-NK(b) // 512)
    pairs_of = lambda b: -(-NK(b) // 1024)
    ITERS = 11

    with ExitStack() as ctx:
        def sb(name, shape, dt=F32):
            return ctx.enter_context(nc.sbuf_tensor(name, shape, dt))

        def psum(name, shape):
            return ctx.enter_context(nc.psum_tensor(name, shape, F32))

        def sem(name):
            return ctx.enter_context(nc.semaphore("m_" + name))

        ident = sb("ident_m", [P, P])
        sums = sb("sums", [P, NM + 1, P], F32R)
        pick = sb("pick", [P, NM, P])
        causal = sb("causal", [P, P])
        rope = sb("rope", [P, NB, 2, ROPE])
        lb = sb("lb", [P, 2, HG * HK])
        g_hg = sb("g_hg", [P, HG * HK])
        row = sb("row", [P, 2, IN_W])
        rt = sb("rt", [P, 4, KV + HEADS, ROPE])
        wis = sb("wis", [P, 2, IH])
        KT = sb("KT", [P, 3, T], F32R)
        V = sb("V", [P, NB, KV * HD])
        qT = sb("qT", [P, 2, HEADS, P], F32R)
        qiT = sb("qiT", [P, 2, IH, P], F32R)
        rel = sb("rel", [P, 2, 2, 512])
        score = sb("score", [P, T + 8])
        above = sb("above", [P, T], BF16)
        bias = sb("bias", [P, 2, T], BF16)
        ends = sb("ends", [P, 2])
        mid = sb("mid", [P, 1])
        cnt = sb("cnt", [P, 1])
        side = sb("side", [P, 2], mybir.dt.uint8)
        sign = sb("sign", [P, 2])
        goal = sb("goal", [P, 2])
        left = sb("left", [P, 1])
        left_all = sb("left_all", [P, 1])
        left_int = sb("left_int", [P, 1], mybir.dt.int32)
        iota8 = sb("iota8", [P, 8])
        top8 = sb("top8", [P, 8])
        want8 = sb("want8", [P, 8])
        use8 = sb("use8", [P, 8], mybir.dt.uint8)
        prob = sb("prob", [P, 2, T])
        mxp = sb("mxp", [P, HEADS, 2])
        nmx = sb("nmx", [P, HEADS])
        den = sb("den", [P, HEADS])
        rden = sb("rden", [P, HEADS])
        pT = sb("pT", [P, 2, 512])
        sig = sb("sig", [P, 3, 512])
        hq = sb("hq", [P, 512])
        hk = sb("hk", [P, 512])
        gg = sb("gg", [P, 512])
        fg = sb("fg", [P, 512])
        fg_hi = sb("fg_hi", [P, 512], F32R)
        fg_lo = sb("fg_lo", [P, 512], F32R)
        khat = sb("khat", [P, 512])
        lbw = khat
        hqT = sb("hqT", [P, HG, P])
        hkT = sb("hkT", [P, HG, P])
        decay = sb("decay", [P, 2, NM, P])
        qe = sb("qe", [P, 2, NM, P])
        ke = sb("ke", [P, 2, NM - 1, P])
        am = sb("am", [P, 2, NM, P])
        elast = sb("elast", [P, HG])
        state = sb("state", [P, 2, HG, HK])
        osb = sb("osb", [P, HG, HK])
        osq = sb("osq", [P, HG, HK], BF16)
        hss = sb("hss", [P, HG])
        hvar = sb("hvar", [P, HG])
        hrstd = sb("hrstd", [P, HG])
        mhalf = sb("mhalf_m", [P, HG])
        mix = sb("mix", [P, D])

        SA = psum("SA", [P, 2, 1024])
        SBk = psum("SBk", [P, 2, 512])
        SC = psum("SC", [P, 512])
        SD = psum("SD", [P, 512])

        const_in = sem("const_in")
        row_in = [sem("row_in0"), sem("row_in1")]
        hgr_in = [sem("hgr_in0"), sem("hgr_in1")]
        pool_step, dve_step, act_step = sem("pool_step"), sem("dve_step"), sem("act_step")
        bounds_step = sem("bounds_step")
        lb_ready = sem("lb_ready")
        rows_ready = sem("rows_ready")
        sb_full, sb_free = sem("sb_full"), sem("sb_free")
        hi_out = sem("hi_out")
        doubled = {"q": sem("q_doubled"), "qi": sem("qi_doubled")}
        sums_ready = sem("sums_ready")
        sa_full = sem("sa_full")
        sa_free_act, sa_free_dve = sem("sa_free_act"), sem("sa_free_dve")
        rel_read = sem("rel_read")
        bias_ready = sem("bias_ready")
        left_ready, left_max = sem("left_ready"), sem("left_max")
        nmx_ready, prob_ready = sem("nmx_ready"), sem("prob_ready")
        pv_done = sem("pv_done")
        sig_ready = sem("sig_ready")
        hq_ready, hk_ready, gg_ready = sem("hq_ready"), sem("hk_ready"), sem("gg_ready")
        logf_ready = sem("logf_ready")
        fg_hi_ready, fg_lo_ready = sem("fg_hi_ready"), sem("fg_lo_ready")
        khat_ready = sem("khat_ready")
        qe_ready, ke_ready = sem("qe_ready"), sem("ke_ready")
        ho_done, ho_out = sem("ho_done"), sem("ho_out")
        hss_ready, hrstd_ready = sem("hss_ready"), sem("hrstd_ready")
        hg_half, att_half = sem("hg_half"), sem("att_half")
        stored = sem("stored")

        use, reader, sb_use, pt_order, idx_order, hi_order = {}, [], {}, {}, {}, {}

        def enter(key, who):
            use[key] = len(reader)
            reader.append(who)

        def enter_split(key):
            hi_order[key] = len(hi_order)
            enter(key, "dve")

        def openings(b):
            return ([("keys", 0)] if b == 0 else []) + ([("qi", b + 1)] if 2 <= b + 1 < NB else []) + \
                [("q", b)] + ([("keys", b + 1)] if b + 1 < NB else [])

        def enter_scores(b, h):
            for p in range(pairs_of(b)):
                enter(("att", b, h, p), "dve")

        for key in openings(0):
            enter_split(key)
        for b in range(NB):
            enter(("hqk", b), "act")
            enter(("tail", b), "act")
            for c in range(NCH(b + 1) if 2 <= b + 1 < NB else 0):
                for j in range(IH // 2):
                    idx_order[b + 1, c, j] = len(idx_order)
                    enter(("idx", b + 1, c, j), "act")
            enter(("decay", b, 0), "act")
            enter_scores(b, 0)
            for g in range(HG):
                enter_scores(b, 2 * g + 1)
                enter(("level", b, g), "dve")
                if g + 1 < HG:
                    enter(("decay", b, g + 1), "act")
                    enter_scores(b, 2 * g + 2)
                else:
                    enter(("kv", b), "dve")
                    for key in openings(b + 1) if b + 1 < NB else []:
                        enter_split(key)
            for h in range(HEADS):
                for c in range(NCH(b)):
                    sb_use["pT", b, h, c] = len(sb_use)
                    pt_order[b, h, c] = len(pt_order)

        def pair(key):
            return SA[:, use[key] % 2, :]

        def bank(key):
            return SBk[:, sb_use[key] % 2, :]

        def wait_pair_read(eng, n):
            done = reader[:n + 1].count(reader[n])
            eng.wait_ge(sa_free_act if reader[n] == "act" else sa_free_dve, done)

        def wait_pair_free(eng, key):
            if use[key] >= 2:
                wait_pair_read(eng, use[key] - 2)

        def wait_pair_full(eng, key):
            eng.wait_ge(sa_full, use[key] + 1)

        def wait_bank_free(eng, key):
            if sb_use[key] >= 2:
                eng.wait_ge(sb_free, sb_use[key] - 1)

        def linker(eng, step):
            count = [0]

            def link(ins):
                count[0] += 1
                ins.then_inc(step, 1)
                eng.wait_ge(step, count[0])
            return link

        def heads(ap, n=HG):
            return ap.rearrange("p (h t) -> p h t", h=n)

        block = ctx.enter_context(nc.Block())

        @block.sync
        def _(sp):
            sp.dma_start(ident[:], a["c_ident"]).then_inc(const_in, 16)
            sp.dma_start(prob[:, 0, 0:(NM + 1) * P].rearrange("p (m t) -> p m t", t=P), a["c_sums"])\
              .then_inc(const_in, 16)
            for to, name in ((pick, "c_pick"), (causal, "c_causal"), (rope, "c_rope")):
                sp.dma_start(to[:], a[name]).then_inc(const_in, 16)
            for n in range(2):
                sp.dma_start(lb[:, n, :], a["hg_lower_bound"][n:n + 1, :].broadcast_to([P, 512])).then_inc(const_in, 16)
            sp.dma_start(g_hg[:], a["hg_out_norm"].broadcast_to([P, 512])).then_inc(const_in, 16)

            def load_att(b):
                if b >= 2:
                    wait_pair_full(sp, ("q", b - 2))
                sp.dma_start(row[:, b % 2, 0:HQ0], proj_d[b * P:(b + 1) * P, 0:HQ0]).then_inc(row_in[b % 2], 16)

            def load_hgrn(b):
                if b >= 2:
                    sp.wait_ge(ho_done, HG * (b - 1))
                    sp.wait_ge(gg_ready, b - 1)
                sp.dma_start(row[:, b % 2, HQ0:IN_W], proj_d[b * P:(b + 1) * P, HQ0:IN_W]).then_inc(hgr_in[b % 2], 16)

            def store(b):
                sp.wait_ge(hg_half, b + 1)
                sp.wait_ge(att_half, b + 1)
                sp.dma_start(mix_d[b * P:(b + 1) * P, :], mix[:]).then_inc(stored, 16)

            for b in range(2):
                load_att(b)
                load_hgrn(b)
            for b in range(NB):
                if b + 2 < NB:
                    load_att(b + 2)
                if b >= 1:
                    store(b - 1)
                if b + 2 < NB:
                    load_hgrn(b + 2)
            store(NB - 1)
            sp.wait_ge(stored, 16 * NB)

        @block.gpsimd
        def _(pool):
            g = nc.gpsimd
            link = linker(pool, pool_step)
            link(g.memset(mhalf[:], -0.5))
            g.iota(iota8[:], [[1, 8]], base=0, channel_multiplier=0,
                   allow_small_or_imprecise_dtypes=True).then_inc(lb_ready, 1)
            pool.wait_ge(const_in, 8 * 16)

            def prep(b):
                pool.wait_ge(row_in[b % 2], 16 * (b // 2 + 1))
                r = row[:, b % 2, :]
                for c0, n_heads in ((Q0, HEADS + KV), (QI0, IH + 1)):
                    x = r[:, c0:c0 + n_heads * HD].rearrange("p (h d) -> p h d", d=HD)
                    x1, x2 = x[:, :, 0:ROPE], x[:, :, ROPE:2 * ROPE]
                    cos = rope[:, b, 0:1, :].broadcast_to([P, n_heads, ROPE])
                    sin = rope[:, b, 1:2, :].broadcast_to([P, n_heads, ROPE])
                    for n, (xx, cs) in enumerate(((x1, cos), (x2, sin), (x2, cos), (x1, sin))):
                        last = g.tensor_tensor(rt[:, n, 0:n_heads, :], xx, cs, ALU.mult)
                    link(last)
                    g.tensor_tensor(x1, rt[:, 0, 0:n_heads, :], rt[:, 1, 0:n_heads, :], ALU.subtract)
                    link(g.tensor_tensor(x2, rt[:, 2, 0:n_heads, :], rt[:, 3, 0:n_heads, :], ALU.add))
                if b >= 4:
                    pool.wait_ge(rel_read, idx_order[b - 2, NCH(b - 2) - 1, IH // 2 - 1] + 1)
                g.tensor_copy(V[:, b, :], r[:, V0:V0 + KV * HD])
                g.tensor_scalar(wis[:, b % 2, :], r[:, WI0:WI0 + IH], IDX_SCALE, None, ALU.mult)\
                    .then_inc(rows_ready, 1)

            def gates(b):
                r = row[:, b % 2, :]
                pool.wait_ge(sig_ready, b + 1)
                if b == 0:
                    pool.wait_ge(lb_ready, 2)
                else:
                    wait_pair_full(pool, ("decay", b - 1, HG - 1))
                link(g.tensor_tensor(fg[:], sig[:, 1, :], lb[:, 1, :], ALU.mult))
                g.tensor_tensor(hk[:], lb[:, 1, :], fg[:], ALU.subtract)
                link(g.tensor_tensor(hq[:], r[:, HQ0:HQ0 + 512], sig[:, 0, :], ALU.mult))
                g.tensor_tensor(fg[:], lb[:, 0, :], fg[:], ALU.add).then_inc(hk_ready, 1)
                g.tensor_tensor(hq[:], r[:, HQ0:HQ0 + 512], hq[:], ALU.add).then_inc(hq_ready, 1)

            def log_low(b):
                pool.wait_ge(fg_hi_ready, b + 1)
                g.tensor_tensor(fg_lo[:], fg[:], fg_hi[:].bitcast(F32), ALU.subtract).then_inc(fg_lo_ready, 1)

            def tail_keys(b):
                wait_pair_read(pool, use["tail", b])
                g.tensor_tensor(khat[:], khat[:], hk[:], ALU.mult).then_inc(khat_ready, 1)

            def output_gate(b):
                z = row[:, b % 2, HG0:HG0 + 512]
                if b >= 1:
                    pool.wait_ge(hg_half, b)
                link(g.tensor_tensor(gg[:], z, sig[:, 2, :], ALU.mult))
                link(g.tensor_tensor(gg[:], gg[:], z, ALU.add))
                g.tensor_tensor(gg[:], gg[:], g_hg[:], ALU.mult).then_inc(gg_ready, 1)

            def level_keys(b, h):
                n = HG * b + h
                wait_pair_read(pool, use["decay", b, h])
                if n >= 2:
                    wait_pair_full(pool, ("level", (n - 2) // HG, (n - 2) % HG))
                g.tensor_tensor(ke[:, h % 2], decay[:, h % 2, 0:NM - 1, :],
                                hkT[:, h:h + 1, :].broadcast_to([P, NM - 1, P]), ALU.mult).then_inc(ke_ready, 1)

            def norm(b):
                pool.wait_ge(hss_ready, b + 1)
                if b >= 1:
                    pool.wait_ge(hg_half, b)
                link(g.tensor_scalar(hvar[:], hss[:], 1.0 / HK, EPS, ALU.mult, ALU.add))
                g.tensor_tensor(hrstd[:], hvar[:], mhalf[:], ALU.pow).then_inc(hrstd_ready, 1)

            prep(0)
            prep(1)
            gates(0)
            link(g.tensor_scalar(g_hg[:], g_hg[:], 0.5, None, ALU.mult))
            log_low(0)
            for b in range(NB):
                tail_keys(b)
                level_keys(b, 0)
                if b + 2 < NB:
                    prep(b + 2)
                level_keys(b, 1)
                output_gate(b)
                level_keys(b, 2)
                level_keys(b, 3)
                if b + 1 < NB:
                    gates(b + 1)
                if 2 <= b + 1 < NB:
                    pool.wait_ge(left_ready, b)
                    g.partition_all_reduce(left_all[:], left[:], P, bass.bass_isa.ReduceOp.max).then_inc(left_max, 1)
                if b + 1 < NB:
                    log_low(b + 1)
                norm(b)

        @block.scalar
        def _(act):
            s = nc.scalar
            act.wait_ge(bounds_step, 1)
            s.activation(lb[:], lb[:], ACT.Exp).then_inc(bounds_step, 1)

            act.wait_ge(const_in, 8 * 16)
            s.activation(sums[:], prob[:, 0, 0:(NM + 1) * P].rearrange("p (m t) -> p m t", t=P), ACT.Copy)\
             .then_inc(sums_ready, 1)

            def high(key):
                what, b = key
                wait_pair_full(act, key)
                if what == "keys":
                    s.activation(KT[0:HD, :, b * P:(b + 1) * P], heads(pair(key)[0:HD, 0:3 * P], 3), ACT.Copy)\
                     .then_inc(hi_out, 1)
                else:
                    to = qT if what == "q" else qiT
                    s.activation(to[HD:P, 0], heads(pair(key)[0:HD], 8), ACT.Copy)
                    s.activation(to[0:HD, 0], heads(pair(key)[0:HD], 8), ACT.Copy)\
                     .then_inc(hi_out, 1)

            def idx(b):
                for c in range(NCH(b)):
                    w = min(512, NK(b) - 512 * c)
                    for j in range(IH // 2):
                        n = idx_order[b, c, j]
                        wait_pair_full(act, ("idx", b, c, j))
                        if n >= 2:
                            act.wait_ge(rel_read, n - 1)
                        s.activation(rel[:, n % 2, :, 0:w], heads(pair(("idx", b, c, j)), 2)[:, :, 0:w],
                                     ACT.Relu).then_inc(sa_free_act, 1)

            def double(b):
                for key in openings(b):
                    if key[0] != "keys":
                        to = qT if key[0] == "q" else qiT
                        wait_pair_read(act, use[key])
                        s.activation(to[HD:P, 1], to[0:HD, 1].bitcast(F32), ACT.Copy).then_inc(doubled[key[0]], 1)

            def gates(b):
                act.wait_ge(hgr_in[b % 2], 16 * (b // 2 + 1))
                if b >= 1:
                    act.wait_ge(gg_ready, b)
                r = row[:, b % 2, :]
                s.activation(sig[:, 0:2, :], heads(r[:, HQ0:HQ0 + 1024], 2), ACT.Tanh, scale=0.5)
                s.activation(sig[:, 2, :], r[:, HG0:HG0 + 512], ACT.Tanh, scale=0.5).then_inc(sig_ready, 1)

            def log_gates(b):
                act.wait_ge(hk_ready, b + 1)
                s.activation(fg[:], fg[:], ACT.Ln).then_inc(logf_ready, 1)
                act.wait_ge(logf_ready, b + 1)
                s.activation(fg_hi[:], fg[:], ACT.Copy).then_inc(fg_hi_ready, 1)

            def opening(b):
                wait_pair_full(act, ("hqk", b))
                s.activation(hqT[:], heads(pair(("hqk", b))[:, 0:512]), ACT.Copy, scale=0.5)
                s.activation(hkT[:], heads(pair(("hqk", b))[:, 512:1024]), ACT.Copy).then_inc(sa_free_act, 1)
                wait_pair_full(act, ("tail", b))
                s.activation(khat[:], pair(("tail", b))[:, 0:512], ACT.Exp).then_inc(sa_free_act, 1)

            def decays(b, h):
                n = HG * b + h
                wait_pair_full(act, ("decay", b, h))
                if n >= 2:
                    act.wait_ge(ke_ready, n - 1)
                    act.wait_ge(qe_ready, n - 1)
                s.activation(decay[:, h % 2], heads(pair(("decay", b, h)), NM), ACT.Exp).then_inc(sa_free_act, 1)

            def squares(b):
                act.wait_ge(ho_done, HG * (b + 1))
                if b >= 1:
                    act.wait_ge(hg_half, b)
                s.activation(osb[:], heads(SD[:]), ACT.Copy).then_inc(ho_out, 1)
                act.wait_ge(ho_out, b + 1)
                for h in range(HG):
                    last = s.activation(osq[:, h, :], osb[:, h, :], ACT.Square, accum_out=hss[:, h:h + 1])
                last.then_inc(hss_ready, 1)

            def softmax(b, h):
                act.wait_ge(nmx_ready, HEADS * b + h + 1)
                pr = prob[:, h % 2, 0:NK(b)]
                s.activation(pr, pr, ACT.Exp, bias=nmx[:, h:h + 1], scale=SM_SCALE,
                             accum_out=den[:, h:h + 1]).then_inc(prob_ready, 1)

            def turned_probs(b, h):
                for c in range(NCH(b)):
                    key = ("pT", b, h, c)
                    w = min(512, NK(b) - 512 * c)
                    m = pt_order[b, h, c]
                    act.wait_ge(sb_full, sb_use[key] + 1)
                    if m >= 2:
                        act.wait_ge(pv_done, m - 1)
                    s.activation(pT[:, m % 2, 0:w], bank(key)[:, 0:w], ACT.Copy).then_inc(sb_free, 1)

            for key in openings(0):
                high(key)
            double(0)
            gates(0)
            log_gates(0)
            for b in range(NB):
                opening(b)
                if 2 <= b + 1 < NB:
                    idx(b + 1)
                decays(b, 0)
                softmax(b, 0)
                for g in range(HG):
                    softmax(b, 2 * g + 1)
                    if g + 1 < HG:
                        decays(b, g + 1)
                    turned_probs(b, 2 * g)
                    if g + 1 < HG:
                        softmax(b, 2 * g + 2)
                    elif b + 1 < NB:
                        for key in openings(b + 1):
                            high(key)
                    if g == 2 and b + 1 < NB:
                        gates(b + 1)
                    if g == 3 and b + 1 < NB:
                        log_gates(b + 1)
                    turned_probs(b, 2 * g + 1)
                if b + 1 < NB:
                    double(b + 1)
                squares(b)

        @block.vector
        def _(dve):
            v = nc.vector
            link = linker(dve, dve_step)
            v.memset(sign[:, 0:1], -1.0)
            v.memset(sign[:, 1:2], 1.0)
            v.memset(goal[:, 0:1], -TOPK - 0.5)
            v.memset(goal[:, 1:2], TOPK + 0.5)
            link(v.memset(state[:], 0.0))
            dve.wait_ge(const_in, 8 * 16)
            link(v.tensor_tensor(lbw[:], lb[:, 0, :], lb[:, 1, :], ALU.max))
            v.tensor_tensor(lb[:, 0, :], lb[:, 0, :], lbw[:], ALU.subtract)
            v.tensor_tensor(lb[:, 1, :], lb[:, 1, :], lbw[:], ALU.subtract).then_inc(bounds_step, 1)
            dve.wait_ge(bounds_step, 2)
            link(v.tensor_tensor(lbw[:], lb[:, 0, :], lb[:, 1, :], ALU.add))
            link(v.reciprocal(lbw[:], lbw[:]))
            link(v.tensor_tensor(lb[:, 0, :], lb[:, 0, :], lbw[:], ALU.mult))
            v.tensor_scalar(lb[:, 1, :], lb[:, 0, :], -0.5, 0.5, ALU.mult, ALU.add)
            v.tensor_scalar(lb[:, 0, :], lb[:, 0, :], 0.5, 0.5, ALU.mult, ALU.add).then_inc(lb_ready, 1)

            def low(key):
                what, b = key
                dve.wait_ge(hi_out, hi_order[key] + 1)
                if what == "keys":
                    cols = slice(b * P, (b + 1) * P)
                    v.tensor_tensor(KT[HD:P, :, cols], heads(pair(key)[0:HD, 0:3 * P], 3),
                                    KT[0:HD, :, cols].bitcast(F32), ALU.subtract).then_inc(sa_free_dve, 1)
                else:
                    to = (qT if what == "q" else qiT)[0:HD]
                    if what == "q" and b >= 1:
                        dve.wait_ge(doubled["q"], b)
                    if what == "qi" and b >= 3:
                        dve.wait_ge(doubled["qi"], b - 2)
                    v.tensor_tensor(to[:, 1], heads(pair(key)[0:HD], 8), to[:, 0].bitcast(F32),
                                    ALU.subtract).then_inc(sa_free_dve, 1)

            def accumulate(b):
                for c in range(NCH(b)):
                    w = min(512, NK(b) - 512 * c)
                    to = score[:, 512 * c:512 * c + w]
                    for j in range(IH // 2):
                        n = idx_order[b, c, j]
                        wait_pair_read(dve, use["idx", b, c, j])
                        for r in range(2):
                            x, wi = rel[:, n % 2, r, 0:w], wis[:, b % 2, 2 * j + r:2 * j + r + 1]
                            if j == 0 and r == 0:
                                link(v.tensor_scalar(to, x, wi, None, ALU.mult))
                            elif r == 0:
                                link(v.scalar_tensor_tensor(to, x, wi, to, ALU.mult, ALU.add))
                            else:
                                v.scalar_tensor_tensor(to, x, wi, to, ALU.mult, ALU.add).then_inc(rel_read, 1)
                                dve.wait_ge(rel_read, n + 1)

            def halve(t):
                link(v.tensor_scalar(mid[:], ends[:, 0:1], ends[:, 1:2], 0.5, ALU.add, ALU.mult))
                link(v.tensor_scalar(above[:, 0:NK(t)], score[:, 0:NK(t)], mid[:, 0:1], None, ALU.is_gt, ALU.add,
                                     accum_out=cnt[:]))
                link(v.scalar_tensor_tensor(side[:], sign[:], cnt[:, 0:1], goal[:], ALU.mult, ALU.is_gt))
                link(v.copy_predicated(ends[:], side[:], mid[:].broadcast_to([P, 2])))

            def take8(t):
                yield v.max(top8[:], score[:, 0:NK(t)])
                yield v.tensor_scalar(use8[:], iota8[:], left[:, 0:1], None, ALU.is_lt)
                yield v.memset(want8[:], TAKEN)
                yield v.copy_predicated(want8[:], use8[:], top8[:])
                yield v.match_replace(score[:, 0:NK(t) + 8], want8[:], score[:, 0:NK(t) + 8], TAKEN)

            def topk_part(t, part):
                own = slice(t * P, (t + 1) * P)
                if t < 2:
                    if part == 0:
                        if t:
                            v.memset(bias[:, t % 2, 0:t * P], 0.0)
                        v.tensor_copy(bias[:, t % 2, own], causal[:]).then_inc(bias_ready, 1)
                    return
                if part == 0:
                    v.tensor_reduce(ends[:, 0:1], score[:, 0:NK(t)], AX_X, ALU.max)
                    link(v.tensor_reduce(ends[:, 1:2], score[:, 0:NK(t)], AX_X, ALU.min))
                    link(v.tensor_tensor(score[:, own], score[:, own], causal[:], ALU.add))
                elif part < 10:
                    for _ in range(2 if part <= ITERS - 9 else 1):
                        halve(t)
                elif part == 10:
                    v.memset(score[:, NK(t):NK(t) + 8], TAKEN)
                    link(v.tensor_scalar(above[:, 0:NK(t)], score[:, 0:NK(t)], ends[:, 0:1], None, ALU.is_gt,
                                         ALU.add, accum_out=cnt[:]))
                    v.tensor_scalar(left[:], cnt[:], -1.0, float(TOPK), ALU.mult, ALU.add).then_inc(left_ready, 1)
                    link(v.scalar_tensor_tensor(score[:, 0:NK(t)], above[:, 0:NK(t)], TAKEN, score[:, 0:NK(t)],
                                                ALU.mult, ALU.add))
                else:
                    for ins in take8(t):
                        link(ins)
                    dve.wait_ge(left_max, t - 1)
                    link(v.tensor_copy(left_int[:], left_all[:]))
                    most = dve.value_load(left_int[0:1, 0:1], min_val=0, max_val=TOPK)
                    with dve.If(most > 8):
                        with dve.Fori(8, most, 8):
                            v.tensor_scalar(left[:], left[:], -8.0, None, ALU.add)
                            dve.drain()
                            for _ in take8(t):
                                dve.drain()
                    v.tensor_scalar(bias[:, t % 2, 0:NK(t)], score[:, 0:NK(t)], 2.0 / 3 * TAKEN, NEG, ALU.is_gt,
                                    ALU.mult).then_inc(bias_ready, 1)

            def level_queries(b, h):
                n = HG * b + h
                wait_pair_read(dve, use["decay", b, h])
                v.tensor_copy(elast[:, h:h + 1], decay[:, h % 2, NM - 1, P - 1:P])
                if n >= 2:
                    dve.wait_ge(ho_done, n - 1)
                v.tensor_tensor(qe[:, h % 2], decay[:, h % 2], hqT[:, h:h + 1, :].broadcast_to([P, NM, P]),
                                ALU.mult).then_inc(qe_ready, 1)

            def levels(b, h):
                n = HG * b + h
                wait_pair_full(dve, ("level", b, h))
                if n >= 2:
                    dve.wait_ge(ho_done, n - 1)
                v.tensor_tensor(am[:, h % 2], heads(pair(("level", b, h)), NM), pick[:], ALU.mult)\
                 .then_inc(sa_free_dve, 1)

            def new_state(b):
                wait_pair_full(dve, ("kv", b))
                dve.wait_ge(qe_ready, HG * (b + 1))
                if b >= 1:
                    dve.wait_ge(ho_done, HG * b)
                for h in range(HG):
                    last = v.scalar_tensor_tensor(state[:, (b + 1) % 2, h, :], state[:, b % 2, h, :], elast[:, h:h + 1],
                                                  heads(pair(("kv", b))[:, 0:512])[:, h, :], ALU.mult, ALU.add)
                last.then_inc(sa_free_dve, 1)
                wait_pair_read(dve, use["kv", b])

            def hgrn_half(b):
                dve.wait_ge(hrstd_ready, b + 1)
                dve.wait_ge(gg_ready, b + 1)
                if b >= 1:
                    dve.wait_ge(stored, 16 * b)
                for h in range(HG):
                    last = v.scalar_tensor_tensor(mix[:, 512 + h * HK:512 + (h + 1) * HK], osb[:, h, :],
                                                  hrstd[:, h:h + 1], gg[:, h * HK:(h + 1) * HK], ALU.mult, ALU.mult)
                last.then_inc(hg_half, 1)

            def scores(b, h):
                back = HEADS * b + h - 2
                if back >= 0:
                    bb, hh = divmod(back, HEADS)
                    dve.wait_ge(sb_full, sb_use["pT", bb, hh, NCH(bb) - 1] + 1)
                else:
                    dve.wait_ge(sums_ready, 1)
                dve.wait_ge(bias_ready, b + 1)
                for p in range(pairs_of(b)):
                    key = ("att", b, h, p)
                    w = min(1024, NK(b) - 1024 * p)
                    cols = slice(1024 * p, 1024 * p + w)
                    wait_pair_full(dve, key)
                    v.tensor_tensor_reduce(prob[:, h % 2, cols], pair(key)[:, 0:w], bias[:, b % 2, cols], 1.0,
                                           TAKEN, ALU.add, ALU.max, mxp[:, h, p:p + 1]).then_inc(sa_free_dve, 1)
                wait_pair_read(dve, use[key])
                if pairs_of(b) == 2:
                    link(v.tensor_tensor(mxp[:, h, 0:1], mxp[:, h, 0:1], mxp[:, h, 1:2], ALU.max))
                v.tensor_scalar(nmx[:, h:h + 1], mxp[:, h, 0:1], -SM_SCALE, None, ALU.mult).then_inc(nmx_ready, 1)

            def attention_half(b):
                dve.wait_ge(pv_done, pt_order[b, HEADS - 1, NCH(b) - 1] + 1)
                if b >= 1:
                    dve.wait_ge(stored, 16 * b)
                link(v.reciprocal(rden[:], den[:]))
                v.tensor_tensor(mix[:, 0:512].rearrange("p (h d) -> p h d", d=HD),
                                SC[:].rearrange("p (h d) -> p h d", d=HD),
                                rden[:].unsqueeze(2).broadcast_to([P, HEADS, HD]), ALU.mult).then_inc(att_half, 1)

            for key in openings(0):
                low(key)
            topk_part(0, 0)
            for b in range(NB):
                def part(n, t=b + 1):
                    if t < NB:
                        topk_part(t, n)
                if b >= 1:
                    attention_half(b - 1)
                if 2 <= b + 1 < NB:
                    accumulate(b + 1)
                if b >= 1:
                    hgrn_half(b - 1)
                level_queries(b, 0)
                scores(b, 0)
                for g in range(HG):
                    part(3 * g)
                    scores(b, 2 * g + 1)
                    levels(b, g)
                    if g + 1 == HG:
                        new_state(b)
                    part(3 * g + 1)
                    if g + 1 < HG:
                        level_queries(b, g + 1)
                        scores(b, 2 * g + 2)
                    elif b + 1 < NB:
                        for key in openings(b + 1):
                            low(key)
                    part(3 * g + 2)
            attention_half(NB - 1)
            hgrn_half(NB - 1)

        @block.tensor
        def _(pe):
            t = nc.tensor
            pe.wait_ge(const_in, 8 * 16)

            pe.wait_ge(sums_ready, 1)

            def turn(src, to, n):
                for j in range(n):
                    last = t.transpose(to[:, j * P:(j + 1) * P], src(j), ident[:])
                return last

            def open_split(key):
                what, b = key
                pe.wait_ge(rows_ready, b + 1)
                first = ((K0, K0 + HD, KI0) if what == "keys" else
                         [(Q0 if what == "q" else QI0) + h * HD for h in range(HEADS)])
                wait_pair_free(pe, key)
                for h, c0 in enumerate(first):
                    last = t.transpose(pair(key)[0:HD, h * P:(h + 1) * P], row[:, b % 2, c0:c0 + HD], ident[:])
                last.then_inc(sa_full, 1)

            def opening(b):
                pe.wait_ge(hq_ready, b + 1)
                wait_pair_free(pe, ("hqk", b))
                turn(lambda j: (hq if j < HG else hk)[:, j % HG * P:(j % HG + 1) * P], pair(("hqk", b)), 2 * HG)\
                    .then_inc(sa_full, 1)
                pe.wait_ge(fg_lo_ready, b + 1)
                wait_pair_free(pe, ("tail", b))
                t.matmul(pair(("tail", b))[:, 0:512], sums[:, NM, :], fg_hi[:], start=True, stop=False)
                t.matmul(pair(("tail", b))[:, 0:512], sums[:, NM, :], fg_lo[:], start=False, stop=True)\
                 .then_inc(sa_full, 1)

            def two_passes(to, q, k):
                t.matmul(to, q[:, 0], k, start=True, stop=False)
                return t.matmul(to, q[:, 1], k, start=False, stop=True)

            def idx(b):
                wait_pair_read(pe, use["keys", b])
                pe.wait_ge(doubled["qi"], b - 1)
                for c in range(NCH(b)):
                    w = min(512, NK(b) - 512 * c)
                    for j in range(IH // 2):
                        key = ("idx", b, c, j)
                        wait_pair_free(pe, key)
                        for r in range(2):
                            last = two_passes(pair(key)[:, 512 * r:512 * r + w], qiT[:, :, 2 * j + r, :],
                                              KT[:, KV, 512 * c:512 * c + w])
                        last.then_inc(sa_full, 1)

            def decays(b, h):
                key = ("decay", b, h)
                wait_pair_free(pe, key)
                for m in range(2):
                    for fg_part, start in ((fg_hi, True), (fg_lo, False)):
                        last = t.matmul(pair(key)[:, 512 * m:512 * (m + 1)], fg_part[:, h * HK:(h + 1) * HK],
                                        sums[:, 4 * m:4 * m + 4, :], start=start, stop=not start)
                last.then_inc(sa_full, 1)

            def levels(b, h):
                pe.wait_ge(qe_ready, HG * b + h + 1)
                pe.wait_ge(ke_ready, HG * b + h + 1)
                wait_pair_free(pe, ("level", b, h))
                out = heads(pair(("level", b, h)), NM)
                for m in range(NM - 1):
                    t.matmul(out[:, m, :], ke[:, h % 2, m, :], qe[:, h % 2, m, :], start=True, stop=True)
                t.matmul(out[:, NM - 1, :], hkT[:, h, :], hqT[:, h, :], start=True, stop=True).then_inc(sa_full, 1)

            def output(b, h):
                if h == 0 and b >= 1:
                    pe.wait_ge(ho_out, b)
                    wait_pair_read(pe, use["kv", b - 1])
                to = heads(SD[:])[:, h, :]
                t.matmul(to, qe[:, h % 2, NM - 1, :], state[:, b % 2, h, :], start=True, stop=False)
                wait_pair_read(pe, use["level", b, h])
                v = heads(row[:, b % 2, HI0:HI0 + 512])
                for m in range(NM):
                    last = t.matmul(to, am[:, h % 2, m, :], v[:, h, :], start=False, stop=(m == NM - 1))
                last.then_inc(ho_done, 1)

            def key_values(b):
                key, v = ("kv", b), heads(row[:, b % 2, HI0:HI0 + 512])
                pe.wait_ge(khat_ready, b + 1)
                wait_pair_free(pe, key)
                for h in range(HG):
                    last = t.matmul(pair(key)[:, h * HK:(h + 1) * HK], khat[:, h * HK:(h + 1) * HK], v[:, h, :],
                                    start=True, stop=True)
                last.then_inc(sa_full, 1)

            def scores(b, h):
                for p in range(pairs_of(b)):
                    key = ("att", b, h, p)
                    wait_pair_free(pe, key)
                    for k0 in range(1024 * p, min(NK(b), 1024 * (p + 1)), 512):
                        w = min(512, NK(b) - k0)
                        last = two_passes(pair(key)[:, k0 - 1024 * p:k0 - 1024 * p + w], qT[:, :, h, :],
                                          KT[:, h // GROUP, k0:k0 + w])
                    last.then_inc(sa_full, 1)

            def values(b, h):
                def blocks(c):
                    return range(4 * c, min(4 * c + 4, b + 1))

                def turn_probs(c):
                    wait_bank_free(pe, ("pT", b, h, c))
                    turn(lambda j: prob[:, h % 2, (4 * c + j) * P:(4 * c + j + 1) * P], bank(("pT", b, h, c)),
                         len(blocks(c))).then_inc(sb_full, 1)

                def product(c):
                    g = h // GROUP
                    pe.wait_ge(sb_free, sb_use["pT", b, h, c] + 1)
                    if b >= 1 and h == 0 and c == 0:
                        pe.wait_ge(att_half, b)
                    for kb in blocks(c):
                        last = t.matmul(SC[:, h * HD:(h + 1) * HD], pT[:, pt_order[b, h, c] % 2, (kb % 4) * P:(kb % 4 + 1) * P],
                                        V[:, kb, g * HD:(g + 1) * HD], start=(kb == 0), stop=(kb == b))
                    last.then_inc(pv_done, 1)

                pe.wait_ge(prob_ready, HEADS * b + h + 1)
                for c in range(NCH(b)):
                    turn_probs(c)
                    if c:
                        product(c - 1)
                product(NCH(b) - 1)

            for key in openings(0):
                open_split(key)
            for b in range(NB):
                opening(b)
                if 2 <= b + 1 < NB:
                    idx(b + 1)
                decays(b, 0)
                wait_pair_read(pe, use["keys", b])
                pe.wait_ge(doubled["q"], b + 1)
                scores(b, 0)
                for g in range(HG):
                    scores(b, 2 * g + 1)
                    levels(b, g)
                    if g + 1 < HG:
                        decays(b, g + 1)
                    else:
                        key_values(b)
                    values(b, 2 * g)
                    if g + 1 < HG:
                        scores(b, 2 * g + 2)
                    elif b + 1 < NB:
                        for key in openings(b + 1):
                            open_split(key)
                    output(b, g)
                    values(b, 2 * g + 1)


def dense_phase(nc, a, mix_d, out):
    with ExitStack() as ctx:
        def sb(name, shape, dt=F32):
            return ctx.enter_context(nc.sbuf_tensor(name, shape, dt))

        def sem(name):
            return ctx.enter_context(nc.semaphore(name))

        hid_hi = sb("hid_hi", [P, NF, SB], F32R)
        hid_lo = sb("hid_lo", [P, NF, SB], F32R)
        h_hi = sb("h2_hi", [P, KD, SB], F32R)
        h_lo = sb("h2_lo", [P, KD, SB], F32R)
        w_raw = sb("wd_raw", [P, 2 * D])
        w_hi = sb("wd_hi", [P, 2, 2 * D], F32R)
        w_lo = sb("wd_lo", [P, 2, 2 * D], F32R)
        xs = sb("xs", [P, TS, D])
        tb = sb("tb", [P, 2, D])
        act_up = sb("act_up", [P, 2, SB])
        g_mix = sb("g_mix", [P, D])
        g_ffn = sb("g_ffn", [P, D])
        g_out = sb("g_out", [P, D])
        ident = sb("ident_d", [P, P])
        ss = sb("ss_d", [P, 12])
        var = sb("var_d", [P, 12])
        rstd = sb("rstd_d", [P, 12])
        mhalf = sb("mhalf_d", [P, 1])
        eps = sb("eps_d", [P, 1])
        ps = ctx.enter_context(nc.psum_tensor("ps_dense", [P, 8, 512], F32))

        const_in = sem("d_const_in")
        pool_step = sem("d_pool_step")
        mix_in = [sem("d_mix_in0"), sem("d_mix_in1")]
        x_in = sem("d_x_in")
        w_in = sem("d_w_in")
        w_hi_ready = sem("d_w_hi_ready")
        w_lo_ready = sem("d_w_lo_ready")
        rows_unit = sem("d_rows_unit")
        turned = sem("d_turned")
        hi_ready = sem("d_hi_ready")
        lo_ready = sem("d_lo_ready")
        rows_done = sem("d_rows_done")
        ss_rows = sem("d_ss_rows")
        rstd_rows = sem("d_rstd_rows")
        scaled = sem("d_scaled")
        added = sem("d_added")
        ss_x1 = sem("d_ss_x1")
        rstd_x1 = sem("d_rstd_x1")
        xn_ready = sem("d_xn_ready")
        up_done = sem("d_up_done")
        silu_ready = sem("d_silu_ready")
        hidden = sem("d_hidden")
        hid_hi_ready = sem("d_hid_hi_ready")
        hid_lo_ready = sem("d_hid_lo_ready")
        stored = sem("d_stored")

        def wait(eng, semaphore, value):
            if not isinstance(value, int) or value > 0:
                eng.wait_ge(semaphore, value)

        units = [("out", (2 * m, 2 * m + 1)) for m in range(KD // 2)]
        up0 = len(units)
        units += [("up", f) for f in range(NF)]
        down0 = len(units)
        units += [("down", (2 * m, 2 * m + 1)) for m in range(NF // 2 - 1)]
        units += [("down", (NF - 2,)), ("down", (NF - 1,))]
        NU = len(units)
        assert NU % 2 == 0

        def wait_unit(eng, s, k):
            if units[k][0] == "up":
                wait(eng, up_done, NF * s + k - up0 + 1)
            elif k in (up0 - 1, NU - 1):
                wait(eng, rows_done, 2 * TS * s + (TS if k < up0 else 2 * TS))
            else:
                m = k + 1 if k < up0 else k - down0 + up0
                wait(eng, rows_unit, (NU - NF - 2) * s + m)

        def width(k):
            return D * len(units[k][1]) if units[k][0] != "up" else 2 * D

        block = ctx.enter_context(nc.Block())

        @block.sync
        def _(sp):
            for to, name in ((ident, "c_ident"), (g_mix, "norm_post_mix"), (g_ffn, "norm_pre_ffn"),
                             (g_out, "norm_post_ffn")):
                src = a[name] if name == "c_ident" else a[name].broadcast_to([P, D])
                sp.dma_start(to[:], src).then_inc(const_in, 16)
            def superblock(s):
                def load_unit(k):
                    wait(sp, w_lo_ready, NU * s + k)
                    kind, what = units[k]
                    if kind == "up":
                        src = a["w_gu"][what]
                    else:
                        w = a["w_out"] if kind == "out" else a["w_down"]
                        src = w[what[0] * P:(what[-1] + 1) * P, :].rearrange("(j p) n -> p j n", p=P)
                    to = w_raw[:, 0:width(k)]
                    if kind != "up":
                        to = to.rearrange("p (j n) -> p j n", n=D)
                    sp.dma_start(to, src).then_inc(w_in, 16)

                load_unit(0)
                for i in range(TS):
                    if i < 2:
                        wait(sp, added, 2 * TS * s)
                    else:
                        wait(sp, turned, 4 * TS * s + 2 * (i - 1))
                    sp.dma_start(tb[:, i % 2, :], mix_d[bass.ds(s * SB + i * P, P), :])\
                      .then_inc(mix_in[i % 2], 16)
                    if i == 1:
                        wait(sp, stored, 16 * TS * s)
                        sp.dma_start(xs[:], a["x"][0, bass.ds(s * SB, SB), :].rearrange("(i p) d -> p i d", p=P))\
                          .then_inc(x_in, 16)
                for k in range(1, NU):
                    load_unit(k)
                for i in range(TS):
                    wait(sp, added, 2 * TS * s + TS + i + 1)
                    sp.dma_start(out[0, bass.ds(s * SB + i * P, P), :], xs[:, i, :]).then_inc(stored, 16)

            superblock(0)
            with sp.Fori(1, NS) as s:
                superblock(s)
            wait(sp, stored, 16 * TS * NS)

        @block.gpsimd
        def _(pool):
            nc.gpsimd.memset(eps[:], EPS)
            nc.gpsimd.memset(mhalf[:], -0.5).then_inc(pool_step, 1)
            wait(pool, pool_step, 1)
            def superblock(s):
                def root(col, ready, n, done, step):
                    c = slice(col, col + 1)
                    wait(pool, ready, n)
                    nc.gpsimd.tensor_tensor(var[:, c], ss[:, c], eps[:], ALU.add).then_inc(pool_step, 1)
                    wait(pool, pool_step, 12 * s + step + 2)
                    nc.gpsimd.tensor_tensor(rstd[:, c], var[:, c], mhalf[:, 0:1], ALU.pow).then_inc(done, 1)

                root(0, ss_rows, 8 * s + 1, rstd_rows, 0)
                for i in range(TS):
                    if i + 1 < TS:
                        root(i + 1, ss_rows, 8 * s + i + 2, rstd_rows, 2 * i + 1)
                    root(4 + i, ss_x1, 4 * s + i + 1, rstd_x1, 2 * i + 2 - (i == TS - 1))
                for i in range(TS):
                    root(8 + i, ss_rows, 8 * s + TS + i + 1, rstd_rows, 8 + i)

            superblock(0)
            with pool.Fori(1, NS) as s:
                superblock(s)

        def bank(n):
            return ps[:, n, :].rearrange("p (k t) -> p k t", k=4)

        @block.scalar
        def _(act):
            def superblock(s):
                def split_w(k):
                    if k >= NU:
                        return
                    wait(act, w_in, 16 * (NU * s + k + 1))
                    if k < 2:
                        wait(act, rows_done, 2 * TS * s)
                    else:
                        wait_unit(act, s, k - 2)
                    nc.scalar.activation(w_hi[:, k % 2, 0:width(k)], w_raw[:, 0:width(k)], ACT.Copy)\
                      .then_inc(w_hi_ready, 1)

                def split_turned(to, n, i):
                    wait(act, turned, 4 * TS * s + n + 1)
                    k = 4 * (n % 2)
                    nc.scalar.activation(to[:, k:k + 4, i * P:(i + 1) * P], bank(2 * i + n % 2),
                                         ACT.Copy).then_inc(hi_ready, 1)

                def square_rows(i, late):
                    wait(act, rows_done, 2 * TS * s + TS * late + i + 1)
                    if late:
                        wait(act, added, 2 * TS * s + TS + max(i - 1, 0))
                        wait(act, turned, 4 * TS * (s + 1))
                    else:
                        wait(act, turned, 4 * TS * s + 2 * TS + 2 * max(i - 1, 0))
                    nc.scalar.activation(tb[:, i % 2, :], ps[:, 2 * i:2 * i + 2, :].rearrange("p a b -> p (a b)"),
                                         ACT.Square, scale=D ** -0.5, accum_out=ss[:, 8 * late + i:8 * late + i + 1])\
                      .then_inc(ss_rows, 1)

                def square_x1(i):
                    wait(act, added, 2 * TS * s + i + 1)
                    nc.scalar.activation(tb[:, i % 2, :], xs[:, i, :], ACT.Square, scale=D ** -0.5,
                                         accum_out=ss[:, 4 + i:5 + i]).then_inc(ss_x1, 1)

                split_w(0)
                split_w(1)
                for i in range(TS):
                    for k in range(2):
                        split_turned(hid_hi, 2 * i + k, i)
                for k in range(up0):
                    split_w(k + 2)
                square_rows(0, 0)
                for i in range(TS):
                    if i + 1 < TS:
                        square_rows(i + 1, 0)
                    square_x1(i)
                    for k in range(2):
                        split_turned(h_hi, 2 * TS + 2 * i + k, i)
                for f in range(NF):
                    wait(act, up_done, NF * s + f + 1)
                    wait(act, hid_lo_ready, NF * s + max(f - 1, 0))
                    nc.scalar.activation(act_up[:, f % 2, :], ps[:, 2 * (f % 4), :], ACT.Silu)\
                      .then_inc(silu_ready, 1)
                    wait(act, hidden, NF * s + f + 1)
                    nc.scalar.activation(hid_hi[:, f, :], act_up[:, f % 2, :], ACT.Copy).then_inc(hid_hi_ready, 1)
                    split_w(up0 + f + 2)
                for k in range(down0, NU):
                    split_w(k + 2)
                for i in range(TS):
                    square_rows(i, 1)

            superblock(0)
            with act.Fori(1, NS) as s:
                superblock(s)

        @block.vector
        def _(dve):
            wait(dve, const_in, 64)
            def superblock(s):
                def split_w(k):
                    if k >= NU:
                        return
                    wait(dve, w_hi_ready, NU * s + k + 1)
                    w = slice(0, width(k))
                    nc.vector.tensor_tensor(w_lo[:, k % 2, w], w_raw[:, w], w_hi[:, k % 2, w].bitcast(F32),
                                            ALU.subtract).then_inc(w_lo_ready, 1)

                def split_turned(to_hi, to_lo, n, i):
                    wait(dve, hi_ready, 4 * TS * s + n + 1)
                    k = 4 * (n % 2)
                    nc.vector.tensor_tensor(to_lo[:, k:k + 4, i * P:(i + 1) * P], bank(2 * i + n % 2),
                                            to_hi[:, k:k + 4, i * P:(i + 1) * P].bitcast(F32),
                                            ALU.subtract).then_inc(lo_ready, 1)

                def add_rows(i, late, gain):
                    col = 8 * late + i
                    wait(dve, rstd_rows, 2 * TS * s + TS * late + i + 1)
                    nc.vector.scalar_tensor_tensor(tb[:, i % 2, :], ps[:, 2 * i:2 * i + 2, :].rearrange("p a b -> p (a b)"),
                                                   rstd[:, col:col + 1], gain[:], ALU.mult, ALU.mult)\
                      .then_inc(scaled, 1)
                    wait(dve, scaled, 2 * TS * s + TS * late + i + 1)
                    nc.vector.tensor_tensor(xs[:, i, :], xs[:, i, :], tb[:, i % 2, :], ALU.add).then_inc(added, 1)

                split_w(0)
                split_w(1)
                for i in range(TS):
                    for k in range(2):
                        split_turned(hid_hi, hid_lo, 2 * i + k, i)
                for k in range(up0):
                    split_w(k + 2)
                wait(dve, x_in, 16 * (s + 1))
                add_rows(0, 0, g_mix)
                for i in range(TS):
                    if i + 1 < TS:
                        add_rows(i + 1, 0, g_mix)
                    wait(dve, rstd_x1, TS * s + i + 1)
                    nc.vector.scalar_tensor_tensor(tb[:, i % 2, :], xs[:, i, :], rstd[:, 4 + i:5 + i], g_ffn[:],
                                                   ALU.mult, ALU.mult).then_inc(xn_ready, 1)
                    for k in range(2):
                        split_turned(h_hi, h_lo, 2 * TS + 2 * i + k, i)
                for f in range(NF):
                    wait(dve, silu_ready, NF * s + f + 1)
                    au = act_up[:, f % 2, :]
                    nc.vector.tensor_tensor(au, au, ps[:, 2 * (f % 4) + 1, :], ALU.mult).then_inc(hidden, 1)
                    wait(dve, hid_hi_ready, NF * s + f + 1)
                    nc.vector.tensor_tensor(hid_lo[:, f, :], au, hid_hi[:, f, :].bitcast(F32),
                                            ALU.subtract).then_inc(hid_lo_ready, 1)
                    split_w(up0 + f + 2)
                for k in range(down0, NU):
                    split_w(k + 2)
                for i in range(TS):
                    add_rows(i, 1, g_out)

            superblock(0)
            with dve.Fori(1, NS) as s:
                superblock(s)

        @block.tensor
        def _(pe):
            wait(pe, const_in, 64)
            def superblock(s):
                def turn(i, n):
                    for k in range(2):
                        for q in range(4):
                            last = nc.tensor.transpose(ps[:, 2 * i + k, q * P:(q + 1) * P],
                                                       tb[:, i % 2, (4 * k + q) * P:(4 * k + q + 1) * P], ident[:])
                        last.then_inc(turned, 1)

                def rows(k, c, j, first, final):
                    for i in range(TS):
                        tok = slice(i * P, (i + 1) * P)
                        for lhs, w, start, stop in ((hid_hi, w_hi, True, False), (hid_hi, w_lo, False, False),
                                                    (hid_lo, w_hi, False, True)):
                            for n in range(2):
                                last = nc.tensor.matmul(ps[:, 2 * i + n, :], lhs[:, c, tok],
                                                        w[:, k % 2, j * D + n * 512:j * D + n * 512 + 512],
                                                        start=start and first, stop=stop and final)
                        if final:
                            last.then_inc(rows_done, 1)
                    return last

                def product(k0, k1, last_chunk):
                    for k in range(k0, k1):
                        wait(pe, w_lo_ready, NU * s + k + 1)
                        for j, c in enumerate(units[k][1]):
                            last = rows(k, c, j, c == 0, c == last_chunk)
                        if c != last_chunk:
                            last.then_inc(rows_unit, 1)

                wait(pe, added, 2 * TS * s)
                for i in range(TS):
                    wait(pe, mix_in[i % 2], 16 * (2 * s + i // 2 + 1))
                    turn(i, 2 * i)
                wait(pe, lo_ready, 4 * TS * s + 2 * TS)
                product(0, up0, KD - 1)
                for i in range(TS):
                    wait(pe, xn_ready, TS * s + i + 1)
                    turn(i, 2 * TS + 2 * i)
                wait(pe, lo_ready, 4 * TS * (s + 1))
                for f in range(NF):
                    k = up0 + f
                    wait(pe, w_lo_ready, NU * s + k + 1)
                    if f >= 4:
                        wait(pe, hidden, NF * s + f - 3)
                    for m in range(2):
                        for c in range(KD):
                            w = slice((m * KD + c) * P, (m * KD + c + 1) * P)
                            o = ps[:, 2 * (f % 4) + m, :]
                            nc.tensor.matmul(o, w_hi[:, k % 2, w], h_hi[:, c, :], start=(c == 0), stop=False)
                            nc.tensor.matmul(o, w_hi[:, k % 2, w], h_lo[:, c, :], start=False, stop=False)
                            last = nc.tensor.matmul(o, w_lo[:, k % 2, w], h_hi[:, c, :], start=False,
                                                    stop=(c == KD - 1))
                    last.then_inc(up_done, 1)
                wait(pe, hid_lo_ready, NF * (s + 1))
                product(down0, NU, NF - 1)

            superblock(0)
            with pe.Fori(1, NS) as s:
                superblock(s)
def layout_gu(w_gate, w_up):
    w = np.stack([w_gate, w_up]).reshape(2, KD, P, NF, P)
    return np.ascontiguousarray(w.transpose(3, 2, 0, 1, 4)).reshape(NF, P, 2 * KD * P)


def build(nc, a, out):
    proj_d = nc.dram_tensor("proj_d", [T, IN_W], F32, kind="Internal").ap()
    mix_d = nc.dram_tensor("mix_d", [T, D], F32, kind="Internal").ap()
    project_phase(nc, a, proj_d)
    mix_phase(nc, a, proj_d, mix_d)
    dense_phase(nc, a, mix_d, out)


_INS = ["x", "norm_pre_mix", "w_in", "w_out", "norm_post_mix", "hg_lower_bound", "hg_out_norm",
        "norm_pre_ffn", "w_gu", "w_down", "norm_post_ffn"]


def kernel(**inputs):
    import concourse.bacc as bacc
    from concourse.bass_utils import run_bass_kernel_spmd

    given = {n: np.ascontiguousarray(inputs[n]) for n in inputs}
    arrays = {n: given[n] for n in ("x", "norm_pre_mix", "norm_post_mix", "hg_lower_bound", "hg_out_norm",
                                    "norm_pre_ffn", "norm_post_ffn")}
    arrays["w_in"] = np.ascontiguousarray(given["w_in"][0].reshape(KD, P, NC_IN, CW).transpose(2, 1, 0, 3))
    arrays["w_out"] = given["w_out"][0]
    arrays["w_gu"] = layout_gu(given["w_gate"][0], given["w_up"][0])
    arrays["w_down"] = given["w_down"][0]
    arrays.update(shape_constants())

    nc = bacc.Bacc("TRN2", target_bir_lowering=False, num_devices=1)
    a = {n: nc.dram_tensor(f"in_{n}", v.shape, mybir.dt.from_np(v.dtype), kind="ExternalInput").ap()
         for n, v in arrays.items()}
    out = nc.dram_tensor("out_y", (1, T, D), F32, kind="ExternalOutput").ap()
    build(nc, a, out)
    r = run_bass_kernel_spmd(nc, [{f"in_{n}": v for n, v in arrays.items()}], core_ids=[0])
    return r.results[0]["out_y"]
```

```python
from contextlib import ExitStack

import numpy as np

import concourse.bass as bass
from concourse import mybir

F32 = mybir.dt.float32
F32R = mybir.dt.float32r
BF16 = mybir.dt.bfloat16
ALU = mybir.AluOpType
ACT = mybir.ActivationFunctionType
AX_X = mybir.AxisListType.X

P = 128
T, D = 2048, 1024
NB = T // P
KD = D // P
HEADS, KV, HD = 8, 2, 64
GROUP = HEADS // KV
IH = 8
TOPK = 256
HG, HK = 4, 128
FF = 2816
NF = FF // P
EPS = 1e-6
ROPE = 8
THETA = 500000.0
SPLITS = (512, 128, 128, 512, 64, 8, 512, 512, 512, 512)
Q0, K0, V0, QI0, KI0, WI0, HQ0, HF0, HI0, HG0 = [sum(SPLITS[:n]) for n in range(10)]
IN_W = sum(SPLITS)
NC_IN = 10
CW = IN_W // NC_IN
IDX_SCALE = (IH ** -0.5) * (HD ** -0.5)
SM_SCALE = HD ** -0.5
NEG = -1.0e30
TAKEN = -3.0e38
LEVELS = (64, 32, 16, 8, 4, 2, 1)
NM = len(LEVELS) + 1
SB = 512
NS = T // SB
TS = SB // P


def shape_constants():
    t = np.arange(P)
    ident = np.eye(P, dtype=np.float32)
    sums = np.zeros((P, NM + 1, P), np.float32)
    pick = np.zeros((P, NM, P), np.float32)
    u, tt = t[:, None], t[None, :]
    for n, h in enumerate(LEVELS):
        mid = (tt // (2 * h)) * 2 * h + h
        sums[:, n] = np.where(tt >= mid, (u >= mid) & (u <= tt), (u > tt) & (u < mid))
        pick[:, n] = (u // (2 * h) == tt // (2 * h)) & (u % (2 * h) < h) & (tt % (2 * h) >= h)
    sums[:, NM - 1] = u <= tt
    sums[:, NM] = u > tt
    pick[:, NM - 1] = u == tt
    causal = np.where(tt <= u, 0.0, NEG).astype(np.float32)
    half = ROPE
    inv = THETA ** (-np.arange(half, dtype=np.float32) / np.float32(half))
    ang = np.arange(T, dtype=np.float32)[:, None] * inv[None, :].astype(np.float32)
    rope = np.stack([np.cos(ang), np.sin(ang)], 1).astype(np.float32)
    rope = np.ascontiguousarray(rope.reshape(NB, P, 2, half).transpose(1, 0, 2, 3))
    return dict(c_ident=ident, c_sums=sums, c_pick=pick, c_causal=causal, c_rope=rope)


def project_phase(nc, a, proj_d):
    with ExitStack() as ctx:
        def sb(name, shape, dt=F32):
            return ctx.enter_context(nc.sbuf_tensor(name, shape, dt))

        def sem(name):
            return ctx.enter_context(nc.semaphore(name))

        h_hi = sb("h_hi", [P, KD, T], F32R)
        h_lo = sb("h_lo", [P, KD, T], F32R)
        w_raw = sb("w_raw", [P, KD, CW])
        w_hi = sb("w_hi", [P, 2, KD, CW], F32R)
        w_lo = sb("w_lo", [P, 2, KD, CW], F32R)
        stage = sb("stage", [P, 2, 2, CW])
        xt = sb("xt", [P, 3, D])
        gain = sb("gain_in", [P, D])
        ident = sb("ident_p", [P, P])
        ss = sb("ss_p", [P, 2])
        var = sb("var_p", [P, 2])
        rstd = sb("rstd_p", [P, 2])
        mhalf = sb("mhalf_p", [P, 2])
        junk = sb("junk_p", [P, D], BF16)
        ps = ctx.enter_context(nc.psum_tensor("ps_proj", [P, 8, 512], F32))

        const_in = sem("p_const_in")
        x_in = [sem(f"p_x_in{n}") for n in range(3)]
        ss_ready = sem("p_ss_ready")
        pool_step = sem("p_pool_step")
        rstd_ready = sem("p_rstd_ready")
        xn_ready = sem("p_xn_ready")
        xT_ready = sem("p_xT_ready")
        h_hi_ready = sem("p_h_hi_ready")
        bank_free = sem("p_bank_free")
        w_in = sem("p_w_in")
        w_hi_ready = sem("p_w_hi_ready")
        w_lo_ready = sem("p_w_lo_ready")
        tile_done = sem("p_tile_done")
        staged = sem("p_staged")
        stored = [sem("p_stored0"), sem("p_stored1")]
        block = ctx.enter_context(nc.Block())

        @block.sync
        def _(sp):
            def store(c, k):
                sp.wait_ge(staged, 16 * c + 2 * k + 2)
                rows = proj_d[2 * k * P:(2 * k + 2) * P, :].rearrange("(i p) e -> p i e", p=P)
                sp.dma_start(rows[:, :, bass.ds(c * CW, CW)], stage[:, k % 2]).then_inc(stored[k % 2], 16)

            def load_x(i):
                if i >= 3:
                    sp.wait_ge(xT_ready, 2 * (i - 2))
                sp.dma_start(xt[:, i % 3, :], a["x"][0, i * P:(i + 1) * P, :]).then_inc(x_in[i % 3], 16)

            load_x(0)
            sp.dma_start(gain[:], a["norm_pre_mix"].broadcast_to([P, D])).then_inc(const_in, 16)
            sp.dma_start(ident[:], a["c_ident"]).then_inc(const_in, 16)
            load_x(1)
            sp.dma_start(w_raw[:], a["w_in"][0]).then_inc(w_in, 16)
            for i in range(2, NB):
                load_x(i)
                if i == 5:
                    sp.wait_ge(w_lo_ready, 1)
                    sp.dma_start(w_raw[:], a["w_in"][1]).then_inc(w_in, 16)
                if i >= 5 and i % 2:
                    store(0, (i - 5) // 2)
            for k in range(NB // 2 - 2, NB // 2):
                store(0, k)
            with sp.Fori(1, NC_IN - 1) as c:
                sp.wait_ge(w_lo_ready, c + 1)
                sp.dma_start(w_raw[:], a["w_in"][c + 1]).then_inc(w_in, 16)
                for k in range(NB // 2):
                    store(c, k)
            for k in range(NB // 2):
                store(NC_IN - 1, k)
            for half in stored:
                sp.wait_ge(half, 16 * NC_IN * NB // 4)

        @block.gpsimd
        def _(pool):
            nc.gpsimd.memset(mhalf[:], -0.5).then_inc(pool_step, 1)
            pool.wait_ge(pool_step, 1)
            for i in range(NB):
                s = slice(i % 2, i % 2 + 1)
                pool.wait_ge(ss_ready, i + 1)
                nc.gpsimd.tensor_scalar(var[:, s], ss[:, s], 1.0 / D, EPS, ALU.mult, ALU.add).then_inc(pool_step, 1)
                pool.wait_ge(pool_step, i + 2)
                nc.gpsimd.tensor_tensor(rstd[:, s], var[:, s], mhalf[:, s], ALU.pow).then_inc(rstd_ready, 1)

        @block.scalar
        def _(act):
            def square(i):
                act.wait_ge(x_in[i % 3], 16 * (i // 3 + 1))
                if i >= 2:
                    act.wait_ge(rstd_ready, i - 1)
                if i >= 1:
                    act.wait_ge(ss_ready, i)
                nc.scalar.activation(junk[:], xt[:, i % 3, :], ACT.Square,
                                     accum_out=ss[:, i % 2:i % 2 + 1]).then_inc(ss_ready, 1)

            def split_hi(i):
                for k in range(2):
                    act.wait_ge(xT_ready, 2 * i + k + 1)
                    nc.scalar.activation(h_hi[:, 4 * k:4 * k + 4, i * P:(i + 1) * P],
                                         ps[:, (2 * i + k) % 4, :].rearrange("p (k t) -> p k t", k=4),
                                         ACT.Copy).then_inc(h_hi_ready, 1)
            def evacuate(c, i, bank):
                act.wait_ge(tile_done, 16 * c + i + 1)
                if i % 2 == 0 and not (isinstance(c, int) and c == 0 and i < 4):
                    act.wait_ge(stored[(i // 2) % 2], 16 * (4 * c + i // 4))
                nc.scalar.activation(stage[:, (i // 2) % 2, i % 2, :], ps[:, bank, 0:CW],
                                     ACT.Copy).then_inc(staged, 1)

            def next_hi(c, u, first):
                act.wait_ge(w_in, 16 * (c + 2))
                if not first:
                    act.wait_ge(tile_done, 16 * c)
                nc.scalar.activation(w_hi[:, 1 - u], w_raw[:], ACT.Copy).then_inc(w_hi_ready, 1)

            square(0)
            square(1)
            act.wait_ge(w_in, 16)
            nc.scalar.activation(w_hi[:, 0], w_raw[:], ACT.Copy).then_inc(w_hi_ready, 1)
            for i in range(NB):
                if i == 8:
                    next_hi(0, 0, True)
                if 2 <= i + 1 < NB:
                    square(i + 1)
                split_hi(i)
                if i >= 2:
                    evacuate(0, i - 2, 4 + (i - 2) % 4)
            for i in range(NB - 2, NB):
                evacuate(0, i, 4 + i % 4)
            with act.Fori(0, NC_IN // 2 - 1) as j:
                for c, u in ((2 * j + 1, 1), (2 * j + 2, 0)):
                    next_hi(c, u, False)
                    for i in range(NB):
                        evacuate(c, i, i % 8)
            for i in range(NB):
                evacuate(NC_IN - 1, i, i % 8)

        @block.vector
        def _(dve):
            dve.wait_ge(const_in, 32)

            def normalise(i):
                dve.wait_ge(rstd_ready, i + 1)
                x = xt[:, i % 3, :]
                nc.vector.scalar_tensor_tensor(x, x, rstd[:, i % 2:i % 2 + 1], gain[:], ALU.mult,
                                               ALU.mult).then_inc(xn_ready, 1)

            def split_lo(i):
                for k in range(2):
                    dve.wait_ge(h_hi_ready, 2 * i + k + 1)
                    to = slice(4 * k, 4 * k + 4), slice(i * P, (i + 1) * P)
                    nc.vector.tensor_tensor(h_lo[:, to[0], to[1]],
                                            ps[:, (2 * i + k) % 4, :].rearrange("p (k t) -> p k t", k=4),
                                            h_hi[:, to[0], to[1]].bitcast(F32),
                                            ALU.subtract).then_inc(bank_free, 1)
            def w_low(c, u):
                dve.wait_ge(w_hi_ready, c + 1)
                nc.vector.tensor_tensor(w_lo[:, u], w_raw[:], w_hi[:, u].bitcast(F32),
                                        ALU.subtract).then_inc(w_lo_ready, 1)
            normalise(0)
            for i in range(NB):
                if i + 1 < NB:
                    normalise(i + 1)
                split_lo(i)
                if i in (0, 8):
                    w_low(i // 8, i // 8)
            with dve.Fori(1, NC_IN // 2) as j:
                for u in range(2):
                    w_low(2 * j + u, u)

        @block.tensor
        def _(pe):
            pe.wait_ge(const_in, 32)
            def turn(i):
                pe.wait_ge(xn_ready, i + 1)
                for k in range(2):
                    n = 2 * i + k
                    if n >= 4:
                        pe.wait_ge(bank_free, n - 3)
                    for q in range(4):
                        last = nc.tensor.transpose(ps[:, n % 4, q * P:(q + 1) * P],
                                                   xt[:, i % 3, (4 * k + q) * P:(4 * k + q + 1) * P], ident[:])
                    last.then_inc(xT_ready, 1)

            def product(i, u, bank):
                tok, out = slice(i * P, (i + 1) * P), ps[:, bank, 0:CW]
                for k in range(KD):
                    nc.tensor.matmul(out, h_hi[:, k, tok], w_hi[:, u, k, :], start=(k == 0), stop=False)
                    nc.tensor.matmul(out, h_hi[:, k, tok], w_lo[:, u, k, :], start=False, stop=False)
                    last = nc.tensor.matmul(out, h_lo[:, k, tok], w_hi[:, u, k, :], start=False,
                                            stop=(k == KD - 1))
                last.then_inc(tile_done, 1)

            def first_product(i):
                pe.wait_ge(bank_free, 2 * i + 2)
                pe.wait_ge(w_lo_ready, 1)
                if i >= 4:
                    pe.wait_ge(staged, i - 3)
                product(i, 0, 4 + i % 4)

            def chunk(c, u):
                pe.wait_ge(w_lo_ready, c + 1)
                for i in range(NB):
                    pe.wait_ge(staged, 16 * c + i - 7)
                    product(i, u, i % 8)

            turn(0)
            for i in range(NB):
                if i + 1 < NB:
                    turn(i + 1)
                first_product(i)
            with pe.Fori(0, NC_IN // 2 - 1) as j:
                chunk(2 * j + 1, 1)
                chunk(2 * j + 2, 0)
            chunk(NC_IN - 1, 1)


def mix_phase(nc, a, proj_d, mix_d):
    NK = lambda b: (b + 1) * P
    NCH = lambda b: -(-NK(b) // 512)
    pairs_of = lambda b: -(-NK(b) // 1024)
    asked, answered = (1, 4, 7), (2, 5, 8)
    own_halvings = (1, 1, 1, 0, 1, 1, 1, 1, 1)
    COUNTS = len(asked)

    with ExitStack() as ctx:
        def sb(name, shape, dt=F32):
            return ctx.enter_context(nc.sbuf_tensor(name, shape, dt))

        def psum(name, shape):
            return ctx.enter_context(nc.psum_tensor(name, shape, F32))

        def sem(name):
            return ctx.enter_context(nc.semaphore("m_" + name))

        ident = sb("ident_m", [P, P])
        sums = sb("sums", [P, NM + 1, P], F32R)
        pick = sb("pick", [P, NM, P])
        causal = sb("causal", [P, P])
        rope = sb("rope", [P, NB, 2, ROPE])
        lb = sb("lb", [P, 2, HG * HK])
        g_hg = sb("g_hg", [P, HG * HK])
        row = sb("row", [P, 2, IN_W])
        rt = sb("rt", [P, 4, KV + HEADS, ROPE])
        wis = sb("wis", [P, 2, IH])
        KT = sb("KT", [P, 3, T], F32R)
        V = sb("V", [P, NB, KV * HD])
        qT = sb("qT", [P, 2, HEADS, P], F32R)
        qiT = sb("qiT", [P, 2, IH, P], F32R)
        rel = sb("rel", [P, 2, 1024])
        score = sb("score", [P, T + 8])
        above = sb("above", [P, T], BF16)
        bias = sb("bias", [P, 2, T], BF16)
        ends = sb("ends", [P, 2])
        mid = sb("mid", [P, 1])
        cnt = sb("cnt", [P, 1])
        side = sb("side", [P, 2], mybir.dt.uint8)
        sign = sb("sign", [P, 2])
        goal = sb("goal", [P, 2])
        act_cnt = sb("act_cnt", [P, 1])
        act_sign = sb("act_sign", [P, 2])
        act_goal = sb("act_goal", [P, 2])
        left = sb("left", [P, 1])
        left_all = sb("left_all", [P, 1])
        left_int = sb("left_int", [P, 1], mybir.dt.int32)
        iota8 = sb("iota8", [P, 8])
        top8 = sb("top8", [P, 8])
        want8 = sb("want8", [P, 8])
        use8 = sb("use8", [P, 8], mybir.dt.uint8)
        prob = sb("prob", [P, 2, T])
        mxp = sb("mxp", [P, HEADS, 2])
        nmx = sb("nmx", [P, HEADS])
        den = sb("den", [P, HEADS])
        rden = sb("rden", [P, HEADS])
        pT = sb("pT", [P, 2, 512])
        sig = sb("sig", [P, 3, 512])
        hq = sb("hq", [P, 512])
        hk = sb("hk", [P, 512])
        gg = sb("gg", [P, 512])
        fg = sb("fg", [P, 512])
        fg_hi = sb("fg_hi", [P, 512], F32R)
        fg_lo = sb("fg_lo", [P, 512], F32R)
        khat = sb("khat", [P, 512])
        lbw = khat
        hqT = sb("hqT", [P, HG, P])
        hkT = sb("hkT", [P, HG, P])
        decay = sb("decay", [P, 2, NM, P])
        qe = sb("qe", [P, 2, NM, P])
        ke = sb("ke", [P, 2, NM - 1, P])
        am = sb("am", [P, 2, NM, P])
        elast = sb("elast", [P, HG])
        state = sb("state", [P, 2, HG, HK])
        osb = sb("osb", [P, HG, HK])
        osq = sb("osq", [P, HG, HK], BF16)
        hss = sb("hss", [P, HG])
        hvar = sb("hvar", [P, HG])
        hrstd = sb("hrstd", [P, HG])
        mhalf = sb("mhalf_m", [P, HG])
        mix = sb("mix", [P, D])

        SA = psum("SA", [P, 2, 1024])
        SBk = psum("SBk", [P, 2, 512])
        SC = psum("SC", [P, 512])
        SD = psum("SD", [P, 512])

        const_in = sem("const_in")
        row_in = [sem("row_in0"), sem("row_in1")]
        hgr_in = [sem("hgr_in0"), sem("hgr_in1")]
        pool_step, dve_step = sem("pool_step"), sem("dve_step")
        bounds_step = sem("bounds_step")
        lb_ready = sem("lb_ready")
        rows_ready = sem("rows_ready")
        sb_full, sb_free = sem("sb_full"), sem("sb_free")
        hi_out = sem("hi_out")
        doubled = {"q": sem("q_doubled"), "qi": sem("qi_doubled")}
        sums_ready = sem("sums_ready")
        sa_full = sem("sa_full")
        sa_free_act, sa_free_dve = sem("sa_free_act"), sem("sa_free_dve")
        rel_read = sem("rel_read")
        bias_ready = sem("bias_ready")
        mid_ready, counted = sem("mid_ready"), sem("counted")
        left_ready, left_max = sem("left_ready"), sem("left_max")
        nmx_ready, prob_ready = sem("nmx_ready"), sem("prob_ready")
        pv_done = sem("pv_done")
        sig_ready = sem("sig_ready")
        hq_ready, hk_ready, gg_ready = sem("hq_ready"), sem("hk_ready"), sem("gg_ready")
        logf_ready = sem("logf_ready")
        fg_hi_ready, fg_lo_ready = sem("fg_hi_ready"), sem("fg_lo_ready")
        khat_ready = sem("khat_ready")
        qe_ready, ke_ready = sem("qe_ready"), sem("ke_ready")
        am_ready = sem("am_ready")
        ho_done, ho_out = sem("ho_done"), sem("ho_out")
        hss_ready, hrstd_ready = sem("hss_ready"), sem("hrstd_ready")
        hg_half, att_half = sem("hg_half"), sem("att_half")
        stored = sem("stored")

        use, reader, sb_use, pt_order, idx_order, hi_order = {}, [], {}, {}, {}, {}

        def enter(key, who):
            use[key] = len(reader)
            reader.append(who)

        def enter_split(key):
            hi_order[key] = len(hi_order)
            enter(key, "dve")

        def openings(b):
            return ([("keys", 0)] if b == 0 else []) + ([("qi", b + 1)] if 2 <= b + 1 < NB else []) + \
                [("q", b)] + ([("keys", b + 1)] if b + 1 < NB else [])

        def enter_idx(b, chunks):
            for c in chunks:
                for h in range(IH):
                    idx_order[b, c, h] = len(idx_order)
                    enter(("idx", b, c, h), "act")

        def enter_scores(b, h):
            for p in range(pairs_of(b)):
                enter(("att", b, h, p), "dve")

        for key in openings(0):
            enter_split(key)
        for b in range(NB):
            chunks = pairs_of(b + 1) if 2 <= b + 1 < NB else 0
            before = 1 if chunks > 1 else 0
            enter_idx(b + 1, range(before))
            enter(("hqk", b), "act")
            enter(("tail", b), "act")
            enter_idx(b + 1, range(before, chunks))
            enter(("decay", b, 0), "act")
            enter_scores(b, 0)
            for g in range(HG):
                if g == 0:
                    enter(("level", b, g), "dve")
                enter_scores(b, 2 * g + 1)
                if g:
                    enter(("level", b, g), "dve")
                if g + 1 < HG:
                    enter(("decay", b, g + 1), "act")
                    enter_scores(b, 2 * g + 2)
                else:
                    enter(("kv", b), "dve")
                    for key in openings(b + 1) if b + 1 < NB else []:
                        enter_split(key)
            for h in range(HEADS):
                for c in range(NCH(b)):
                    sb_use["pT", b, h, c] = len(sb_use)
                    pt_order[b, h, c] = len(pt_order)

        def pair(key):
            return SA[:, use[key] % 2, :]

        def bank(key):
            return SBk[:, sb_use[key] % 2, :]

        def wait_pair_read(eng, n):
            done = reader[:n + 1].count(reader[n])
            eng.wait_ge(sa_free_act if reader[n] == "act" else sa_free_dve, done)

        def wait_pair_free(eng, key):
            if use[key] >= 2:
                wait_pair_read(eng, use[key] - 2)

        def wait_pair_full(eng, key):
            eng.wait_ge(sa_full, use[key] + 1)

        def wait_bank_free(eng, key):
            if sb_use[key] >= 2:
                eng.wait_ge(sb_free, sb_use[key] - 1)

        def linker(eng, step):
            count = [0]

            def link(ins):
                count[0] += 1
                ins.then_inc(step, 1)
                eng.wait_ge(step, count[0])
            return link

        def heads(ap, n=HG):
            return ap.rearrange("p (h t) -> p h t", h=n)

        block = ctx.enter_context(nc.Block())

        @block.sync
        def _(sp):
            sp.dma_start(ident[:], a["c_ident"]).then_inc(const_in, 16)
            sp.dma_start(prob[:, 0, 0:(NM + 1) * P].rearrange("p (m t) -> p m t", t=P), a["c_sums"])\
              .then_inc(const_in, 16)
            for to, name in ((pick, "c_pick"), (causal, "c_causal"), (rope, "c_rope")):
                sp.dma_start(to[:], a[name]).then_inc(const_in, 16)
            for n in range(2):
                sp.dma_start(lb[:, n, :], a["hg_lower_bound"][n:n + 1, :].broadcast_to([P, 512])).then_inc(const_in, 16)
            sp.dma_start(g_hg[:], a["hg_out_norm"].broadcast_to([P, 512])).then_inc(const_in, 16)

            def load_att(b):
                if b >= 2:
                    wait_pair_full(sp, ("q", b - 2))
                sp.dma_start(row[:, b % 2, 0:HQ0], proj_d[b * P:(b + 1) * P, 0:HQ0]).then_inc(row_in[b % 2], 16)

            def load_hgrn(b):
                if b >= 2:
                    sp.wait_ge(ho_done, HG * (b - 1))
                    sp.wait_ge(gg_ready, b - 1)
                sp.dma_start(row[:, b % 2, HQ0:IN_W], proj_d[b * P:(b + 1) * P, HQ0:IN_W]).then_inc(hgr_in[b % 2], 16)

            def store(b):
                sp.wait_ge(hg_half, b + 1)
                sp.wait_ge(att_half, b + 1)
                sp.dma_start(mix_d[b * P:(b + 1) * P, :], mix[:]).then_inc(stored, 16)

            for b in range(2):
                load_att(b)
                load_hgrn(b)
            for b in range(NB):
                if b + 2 < NB:
                    load_att(b + 2)
                if b >= 1:
                    store(b - 1)
                if b + 2 < NB:
                    load_hgrn(b + 2)
            store(NB - 1)
            sp.wait_ge(stored, 16 * NB)

        @block.gpsimd
        def _(pool):
            g = nc.gpsimd
            link = linker(pool, pool_step)
            link(g.memset(mhalf[:], -0.5))
            g.iota(iota8[:], [[1, 8]], base=0, channel_multiplier=0,
                   allow_small_or_imprecise_dtypes=True).then_inc(lb_ready, 1)
            pool.wait_ge(const_in, 8 * 16)

            def prep(b):
                pool.wait_ge(row_in[b % 2], 16 * (b // 2 + 1))
                r = row[:, b % 2, :]
                for c0, n_heads in ((Q0, HEADS + KV), (QI0, IH + 1)):
                    x = r[:, c0:c0 + n_heads * HD].rearrange("p (h d) -> p h d", d=HD)
                    x1, x2 = x[:, :, 0:ROPE], x[:, :, ROPE:2 * ROPE]
                    cos = rope[:, b, 0:1, :].broadcast_to([P, n_heads, ROPE])
                    sin = rope[:, b, 1:2, :].broadcast_to([P, n_heads, ROPE])
                    for n, (xx, cs) in enumerate(((x1, cos), (x2, sin), (x2, cos), (x1, sin))):
                        last = g.tensor_tensor(rt[:, n, 0:n_heads, :], xx, cs, ALU.mult)
                    link(last)
                    g.tensor_tensor(x1, rt[:, 0, 0:n_heads, :], rt[:, 1, 0:n_heads, :], ALU.subtract)
                    link(g.tensor_tensor(x2, rt[:, 2, 0:n_heads, :], rt[:, 3, 0:n_heads, :], ALU.add))
                if b >= 4:
                    pool.wait_ge(rel_read, idx_order[b - 2, pairs_of(b - 2) - 1, IH - 1] + 1)
                g.tensor_copy(V[:, b, :], r[:, V0:V0 + KV * HD])
                g.tensor_scalar(wis[:, b % 2, :], r[:, WI0:WI0 + IH], IDX_SCALE, None, ALU.mult)\
                    .then_inc(rows_ready, 1)

            def gates(b):
                r = row[:, b % 2, :]
                pool.wait_ge(sig_ready, b + 1)
                if b == 0:
                    pool.wait_ge(lb_ready, 2)
                else:
                    wait_pair_full(pool, ("decay", b - 1, HG - 1))
                link(g.tensor_tensor(fg[:], sig[:, 1, :], lb[:, 1, :], ALU.mult))
                g.tensor_tensor(hk[:], lb[:, 1, :], fg[:], ALU.subtract)
                link(g.tensor_tensor(hq[:], r[:, HQ0:HQ0 + 512], sig[:, 0, :], ALU.mult))
                g.tensor_tensor(fg[:], lb[:, 0, :], fg[:], ALU.add).then_inc(hk_ready, 1)
                g.tensor_tensor(hq[:], r[:, HQ0:HQ0 + 512], hq[:], ALU.add).then_inc(hq_ready, 1)

            def log_low(b):
                pool.wait_ge(fg_hi_ready, b + 1)
                g.tensor_tensor(fg_lo[:], fg[:], fg_hi[:].bitcast(F32), ALU.subtract).then_inc(fg_lo_ready, 1)

            def tail_keys(b):
                wait_pair_read(pool, use["tail", b])
                g.tensor_tensor(khat[:], khat[:], hk[:], ALU.mult).then_inc(khat_ready, 1)

            def output_gate(b):
                z = row[:, b % 2, HG0:HG0 + 512]
                if b >= 1:
                    pool.wait_ge(hg_half, b)
                link(g.tensor_tensor(gg[:], z, sig[:, 2, :], ALU.mult))
                link(g.tensor_tensor(gg[:], gg[:], z, ALU.add))
                g.tensor_tensor(gg[:], gg[:], g_hg[:], ALU.mult).then_inc(gg_ready, 1)

            def level_keys(b, h):
                n = HG * b + h
                wait_pair_read(pool, use["decay", b, h])
                if n >= 2:
                    wait_pair_full(pool, ("level", (n - 2) // HG, (n - 2) % HG))
                g.tensor_tensor(ke[:, h % 2], decay[:, h % 2, 0:NM - 1, :],
                                hkT[:, h:h + 1, :].broadcast_to([P, NM - 1, P]), ALU.mult).then_inc(ke_ready, 1)

            def level_sum(b, h):
                wait_pair_read(pool, use["level", b, h])
                x = am[:, h % 2]
                link(g.tensor_tensor(x[:, 0:4, :], x[:, 0:4, :], x[:, 4:8, :], ALU.add))
                link(g.tensor_tensor(x[:, 0:2, :], x[:, 0:2, :], x[:, 2:4, :], ALU.add))
                g.tensor_tensor(x[:, 0:1, :], x[:, 0:1, :], x[:, 1:2, :], ALU.add).then_inc(am_ready, 1)

            def norm(b):
                pool.wait_ge(hss_ready, b + 1)
                if b >= 1:
                    pool.wait_ge(hg_half, b)
                link(g.tensor_scalar(hvar[:], hss[:], 1.0 / HK, EPS, ALU.mult, ALU.add))
                g.tensor_tensor(hrstd[:], hvar[:], mhalf[:], ALU.pow).then_inc(hrstd_ready, 1)

            prep(0)
            prep(1)
            gates(0)
            link(g.tensor_scalar(g_hg[:], g_hg[:], 0.5, None, ALU.mult))
            log_low(0)
            for b in range(NB):
                tail_keys(b)
                level_keys(b, 0)
                if b + 2 < NB:
                    prep(b + 2)
                level_keys(b, 1)
                level_sum(b, 0)
                output_gate(b)
                level_keys(b, 2)
                level_sum(b, 1)
                level_keys(b, 3)
                level_sum(b, 2)
                if b + 1 < NB:
                    gates(b + 1)
                level_sum(b, 3)
                if 2 <= b + 1 < NB:
                    pool.wait_ge(left_ready, b)
                    g.partition_all_reduce(left_all[:], left[:], P, bass.bass_isa.ReduceOp.max).then_inc(left_max, 1)
                if b + 1 < NB:
                    log_low(b + 1)
                norm(b)

        @block.scalar
        def _(act):
            s = nc.scalar
            act.wait_ge(bounds_step, 1)
            s.activation(lb[:], lb[:], ACT.Exp).then_inc(bounds_step, 1)

            act.wait_ge(const_in, 8 * 16)
            s.activation(sums[:], prob[:, 0, 0:(NM + 1) * P].rearrange("p (m t) -> p m t", t=P), ACT.Copy)\
             .then_inc(sums_ready, 1)

            def high(key):
                what, b = key
                wait_pair_full(act, key)
                if what == "keys":
                    s.activation(KT[0:HD, :, b * P:(b + 1) * P], heads(pair(key)[0:HD, 0:3 * P], 3), ACT.Copy)\
                     .then_inc(hi_out, 1)
                else:
                    to = qT if what == "q" else qiT
                    s.activation(to[HD:P, 0], heads(pair(key)[0:HD], 8), ACT.Copy)
                    s.activation(to[0:HD, 0], heads(pair(key)[0:HD], 8), ACT.Copy)\
                     .then_inc(hi_out, 1)

            def idx(b):
                for c in range(pairs_of(b)):
                    if c == 1:
                        opening(b - 1)
                    w = min(1024, NK(b) - 1024 * c)
                    for h in range(IH):
                        n = idx_order[b, c, h]
                        wait_pair_full(act, ("idx", b, c, h))
                        if n >= 2:
                            act.wait_ge(rel_read, n - 1)
                        s.activation(rel[:, n % 2, 0:w], pair(("idx", b, c, h))[:, 0:w],
                                     ACT.Relu).then_inc(sa_free_act, 1)

            def double(b):
                for key in openings(b):
                    if key[0] != "keys":
                        to = qT if key[0] == "q" else qiT
                        wait_pair_read(act, use[key])
                        s.activation(to[HD:P, 1], to[0:HD, 1].bitcast(F32), ACT.Copy).then_inc(doubled[key[0]], 1)

            def count(t, k):
                if 2 <= t < NB and k in asked:
                    act.wait_ge(mid_ready, COUNTS * (t - 2) + asked.index(k) + 1)
                    s.activation(above[:, 0:NK(t)], score[:, 0:NK(t)], ACT.Sign, bias=mid[:, 0:1], scale=-1.0,
                                 accum_out=act_cnt[:]).then_inc(counted, 1)

            def gates(b):
                act.wait_ge(hgr_in[b % 2], 16 * (b // 2 + 1))
                if b >= 1:
                    act.wait_ge(gg_ready, b)
                r = row[:, b % 2, :]
                s.activation(sig[:, 0:2, :], heads(r[:, HQ0:HQ0 + 1024], 2), ACT.Tanh, scale=0.5)
                s.activation(sig[:, 2, :], r[:, HG0:HG0 + 512], ACT.Tanh, scale=0.5).then_inc(sig_ready, 1)

            def log_gates(b):
                act.wait_ge(hk_ready, b + 1)
                s.activation(fg[:], fg[:], ACT.Ln).then_inc(logf_ready, 1)
                act.wait_ge(logf_ready, b + 1)
                s.activation(fg_hi[:], fg[:], ACT.Copy).then_inc(fg_hi_ready, 1)

            def opening(b):
                wait_pair_full(act, ("hqk", b))
                s.activation(hqT[:], heads(pair(("hqk", b))[:, 0:512]), ACT.Copy, scale=0.5)
                s.activation(hkT[:], heads(pair(("hqk", b))[:, 512:1024]), ACT.Copy).then_inc(sa_free_act, 1)
                wait_pair_full(act, ("tail", b))
                s.activation(khat[:], pair(("tail", b))[:, 0:512], ACT.Exp).then_inc(sa_free_act, 1)

            def decays(b, h):
                n = HG * b + h
                wait_pair_full(act, ("decay", b, h))
                if n >= 2:
                    act.wait_ge(ke_ready, n - 1)
                    act.wait_ge(qe_ready, n - 1)
                s.activation(decay[:, h % 2], heads(pair(("decay", b, h)), NM), ACT.Exp).then_inc(sa_free_act, 1)

            def squares(b):
                act.wait_ge(ho_done, HG * (b + 1))
                if b >= 1:
                    act.wait_ge(hg_half, b)
                s.activation(osb[:], heads(SD[:]), ACT.Copy).then_inc(ho_out, 1)
                act.wait_ge(ho_out, b + 1)
                for h in range(HG):
                    last = s.activation(osq[:, h, :], osb[:, h, :], ACT.Square, accum_out=hss[:, h:h + 1])
                last.then_inc(hss_ready, 1)

            def softmax(b, h):
                act.wait_ge(nmx_ready, HEADS * b + h + 1)
                pr = prob[:, h % 2, 0:NK(b)]
                s.activation(pr, pr, ACT.Exp, bias=nmx[:, h:h + 1], scale=SM_SCALE,
                             accum_out=den[:, h:h + 1]).then_inc(prob_ready, 1)

            def turned_probs(b, h):
                for c in range(NCH(b)):
                    key = ("pT", b, h, c)
                    w = min(512, NK(b) - 512 * c)
                    m = pt_order[b, h, c]
                    act.wait_ge(sb_full, sb_use[key] + 1)
                    if m >= 2:
                        act.wait_ge(pv_done, m - 1)
                    s.activation(pT[:, m % 2, 0:w], bank(key)[:, 0:w], ACT.Copy).then_inc(sb_free, 1)

            for key in openings(0):
                high(key)
            double(0)
            gates(0)
            log_gates(0)
            for b in range(NB):
                if not (2 <= b + 1 < NB and pairs_of(b + 1) > 1):
                    opening(b)
                if 2 <= b + 1 < NB:
                    idx(b + 1)
                decays(b, 0)
                softmax(b, 0)
                for g in range(HG):
                    turned_probs(b, 2 * g)
                    softmax(b, 2 * g + 1)
                    count(b + 1, 3 * g)
                    if g + 1 < HG:
                        decays(b, g + 1)
                    if g == 2 and b + 1 < NB:
                        gates(b + 1)
                    if g == 3 and b + 1 < NB:
                        log_gates(b + 1)
                        for key in openings(b + 1):
                            high(key)
                    turned_probs(b, 2 * g + 1)
                    count(b + 1, 3 * g + 1)
                    if g + 1 < HG:
                        softmax(b, 2 * g + 2)
                    count(b + 1, 3 * g + 2)
                if b + 1 < NB:
                    double(b + 1)
                squares(b)

        @block.vector
        def _(dve):
            v = nc.vector
            link = linker(dve, dve_step)
            v.memset(sign[:, 0:1], -1.0)
            v.memset(sign[:, 1:2], 1.0)
            v.memset(goal[:, 0:1], -TOPK - 0.5)
            v.memset(goal[:, 1:2], TOPK + 0.5)
            v.memset(act_sign[:, 0:1], 1.0)
            v.memset(act_sign[:, 1:2], -1.0)
            link(v.memset(state[:], 0.0))
            dve.wait_ge(const_in, 8 * 16)
            link(v.tensor_tensor(lbw[:], lb[:, 0, :], lb[:, 1, :], ALU.max))
            v.tensor_tensor(lb[:, 0, :], lb[:, 0, :], lbw[:], ALU.subtract)
            v.tensor_tensor(lb[:, 1, :], lb[:, 1, :], lbw[:], ALU.subtract).then_inc(bounds_step, 1)
            dve.wait_ge(bounds_step, 2)
            link(v.tensor_tensor(lbw[:], lb[:, 0, :], lb[:, 1, :], ALU.add))
            link(v.reciprocal(lbw[:], lbw[:]))
            link(v.tensor_tensor(lb[:, 0, :], lb[:, 0, :], lbw[:], ALU.mult))
            v.tensor_scalar(lb[:, 1, :], lb[:, 0, :], -0.5, 0.5, ALU.mult, ALU.add)
            v.tensor_scalar(lb[:, 0, :], lb[:, 0, :], 0.5, 0.5, ALU.mult, ALU.add).then_inc(lb_ready, 1)

            def low(key):
                what, b = key
                dve.wait_ge(hi_out, hi_order[key] + 1)
                if what == "keys":
                    cols = slice(b * P, (b + 1) * P)
                    v.tensor_tensor(KT[HD:P, :, cols], heads(pair(key)[0:HD, 0:3 * P], 3),
                                    KT[0:HD, :, cols].bitcast(F32), ALU.subtract).then_inc(sa_free_dve, 1)
                else:
                    to = (qT if what == "q" else qiT)[0:HD]
                    if what == "q" and b >= 1:
                        dve.wait_ge(doubled["q"], b)
                    if what == "qi" and b >= 3:
                        dve.wait_ge(doubled["qi"], b - 2)
                    v.tensor_tensor(to[:, 1], heads(pair(key)[0:HD], 8), to[:, 0].bitcast(F32),
                                    ALU.subtract).then_inc(sa_free_dve, 1)

            def accumulate(b):
                for c in range(pairs_of(b)):
                    w = min(1024, NK(b) - 1024 * c)
                    to = score[:, 1024 * c:1024 * c + w]
                    for h in range(IH):
                        n = idx_order[b, c, h]
                        wait_pair_read(dve, use["idx", b, c, h])
                        x, wi = rel[:, n % 2, 0:w], wis[:, b % 2, h:h + 1]
                        if h == 0:
                            ins = v.tensor_scalar(to, x, wi, None, ALU.mult)
                        else:
                            ins = v.scalar_tensor_tensor(to, x, wi, to, ALU.mult, ALU.add)
                        ins.then_inc(rel_read, 1)
                        dve.wait_ge(rel_read, n + 1)

            def halve(t):
                link(v.tensor_scalar(mid[:], ends[:, 0:1], ends[:, 1:2], 0.5, ALU.add, ALU.mult))
                link(v.tensor_scalar(above[:, 0:NK(t)], score[:, 0:NK(t)], mid[:, 0:1], None, ALU.is_gt, ALU.add,
                                     accum_out=cnt[:]))
                link(v.scalar_tensor_tensor(side[:], sign[:], cnt[:, 0:1], goal[:], ALU.mult, ALU.is_gt))
                link(v.copy_predicated(ends[:], side[:], mid[:].broadcast_to([P, 2])))

            def ask(t):
                v.tensor_scalar(mid[:], ends[:, 0:1], ends[:, 1:2], 0.5, ALU.add, ALU.mult).then_inc(mid_ready, 1)

            def answer(t, k):
                dve.wait_ge(counted, COUNTS * (t - 2) + k)
                link(v.scalar_tensor_tensor(side[:], act_sign[:], act_cnt[:, 0:1], act_goal[:], ALU.mult, ALU.is_gt))
                link(v.copy_predicated(ends[:], side[:], mid[:].broadcast_to([P, 2])))

            def take8(t):
                yield v.max(top8[:], score[:, 0:NK(t)])
                yield v.tensor_scalar(use8[:], iota8[:], left[:, 0:1], None, ALU.is_lt)
                yield v.memset(want8[:], TAKEN)
                yield v.copy_predicated(want8[:], use8[:], top8[:])
                yield v.match_replace(score[:, 0:NK(t) + 8], want8[:], score[:, 0:NK(t) + 8], TAKEN)

            def topk_part(t, part):
                own = slice(t * P, (t + 1) * P)
                if t < 2:
                    if part == 0:
                        if t:
                            v.memset(bias[:, t % 2, 0:t * P], 0.0)
                        v.tensor_copy(bias[:, t % 2, own], causal[:]).then_inc(bias_ready, 1)
                    return
                if part == 0:
                    v.tensor_reduce(ends[:, 0:1], score[:, 0:NK(t)], AX_X, ALU.max)
                    link(v.tensor_reduce(ends[:, 1:2], score[:, 0:NK(t)], AX_X, ALU.min))
                    link(v.tensor_tensor(score[:, own], score[:, own], causal[:], ALU.add))
                    v.memset(act_goal[:, 0:1], NK(t) - 2 * TOPK - 0.5)
                    v.memset(act_goal[:, 1:2], -(NK(t) - 2 * TOPK - 0.5))
                elif part < 10:
                    if part in answered:
                        answer(t, answered.index(part) + 1)
                    for _ in range(own_halvings[part - 1]):
                        halve(t)
                    if part in asked:
                        ask(t)
                elif part == 10:
                    if part in answered:
                        answer(t, COUNTS)
                    v.memset(score[:, NK(t):NK(t) + 8], TAKEN)
                    link(v.tensor_scalar(above[:, 0:NK(t)], score[:, 0:NK(t)], ends[:, 0:1], None, ALU.is_gt,
                                         ALU.add, accum_out=cnt[:]))
                    v.tensor_scalar(left[:], cnt[:], -1.0, float(TOPK), ALU.mult, ALU.add).then_inc(left_ready, 1)
                    link(v.scalar_tensor_tensor(score[:, 0:NK(t)], above[:, 0:NK(t)], TAKEN, score[:, 0:NK(t)],
                                                ALU.mult, ALU.add))
                else:
                    for ins in take8(t):
                        link(ins)
                    dve.wait_ge(left_max, t - 1)
                    link(v.tensor_copy(left_int[:], left_all[:]))
                    most = dve.value_load(left_int[0:1, 0:1], min_val=0, max_val=TOPK)
                    with dve.If(most > 8):
                        with dve.Fori(8, most, 8):
                            v.tensor_scalar(left[:], left[:], -8.0, None, ALU.add)
                            dve.drain()
                            for _ in take8(t):
                                dve.drain()
                    v.tensor_scalar(bias[:, t % 2, 0:NK(t)], score[:, 0:NK(t)], 2.0 / 3 * TAKEN, NEG, ALU.is_gt,
                                    ALU.mult).then_inc(bias_ready, 1)

            def level_queries(b, h):
                n = HG * b + h
                wait_pair_read(dve, use["decay", b, h])
                v.tensor_copy(elast[:, h:h + 1], decay[:, h % 2, NM - 1, P - 1:P])
                if n >= 2:
                    dve.wait_ge(ho_done, n - 1)
                v.tensor_tensor(qe[:, h % 2], decay[:, h % 2], hqT[:, h:h + 1, :].broadcast_to([P, NM, P]),
                                ALU.mult).then_inc(qe_ready, 1)

            def levels(b, h):
                n = HG * b + h
                wait_pair_full(dve, ("level", b, h))
                if n >= 2:
                    dve.wait_ge(ho_done, n - 1)
                v.tensor_tensor(am[:, h % 2], heads(pair(("level", b, h)), NM), pick[:], ALU.mult)\
                 .then_inc(sa_free_dve, 1)

            def new_state(b):
                wait_pair_full(dve, ("kv", b))
                dve.wait_ge(qe_ready, HG * (b + 1))
                if b >= 1:
                    dve.wait_ge(ho_done, HG * b)
                for h in range(HG):
                    last = v.scalar_tensor_tensor(state[:, (b + 1) % 2, h, :], state[:, b % 2, h, :], elast[:, h:h + 1],
                                                  heads(pair(("kv", b))[:, 0:512])[:, h, :], ALU.mult, ALU.add)
                last.then_inc(sa_free_dve, 1)
                wait_pair_read(dve, use["kv", b])

            def hgrn_half(b):
                dve.wait_ge(hrstd_ready, b + 1)
                dve.wait_ge(gg_ready, b + 1)
                if b >= 1:
                    dve.wait_ge(stored, 16 * b)
                for h in range(HG):
                    last = v.scalar_tensor_tensor(mix[:, 512 + h * HK:512 + (h + 1) * HK], osb[:, h, :],
                                                  hrstd[:, h:h + 1], gg[:, h * HK:(h + 1) * HK], ALU.mult, ALU.mult)
                last.then_inc(hg_half, 1)

            def scores(b, h):
                back = HEADS * b + h - 2
                if back >= 0:
                    bb, hh = divmod(back, HEADS)
                    dve.wait_ge(sb_full, sb_use["pT", bb, hh, NCH(bb) - 1] + 1)
                else:
                    dve.wait_ge(sums_ready, 1)
                dve.wait_ge(bias_ready, b + 1)
                for p in range(pairs_of(b)):
                    key = ("att", b, h, p)
                    w = min(1024, NK(b) - 1024 * p)
                    cols = slice(1024 * p, 1024 * p + w)
                    wait_pair_full(dve, key)
                    v.tensor_tensor_reduce(prob[:, h % 2, cols], pair(key)[:, 0:w], bias[:, b % 2, cols], 1.0,
                                           TAKEN, ALU.add, ALU.max, mxp[:, h, p:p + 1]).then_inc(sa_free_dve, 1)
                wait_pair_read(dve, use[key])
                if pairs_of(b) == 2:
                    link(v.tensor_tensor(mxp[:, h, 0:1], mxp[:, h, 0:1], mxp[:, h, 1:2], ALU.max))
                v.tensor_scalar(nmx[:, h:h + 1], mxp[:, h, 0:1], -SM_SCALE, None, ALU.mult).then_inc(nmx_ready, 1)

            def attention_half(b):
                dve.wait_ge(pv_done, pt_order[b, HEADS - 1, NCH(b) - 1] + 1)
                if b >= 1:
                    dve.wait_ge(stored, 16 * b)
                link(v.reciprocal(rden[:], den[:]))
                v.tensor_tensor(mix[:, 0:512].rearrange("p (h d) -> p h d", d=HD),
                                SC[:].rearrange("p (h d) -> p h d", d=HD),
                                rden[:].unsqueeze(2).broadcast_to([P, HEADS, HD]), ALU.mult).then_inc(att_half, 1)

            for key in openings(0):
                low(key)
            topk_part(0, 0)
            for b in range(NB):
                def part(n, t=b + 1):
                    if t < NB:
                        topk_part(t, n)
                if b >= 1:
                    attention_half(b - 1)
                if 2 <= b + 1 < NB:
                    accumulate(b + 1)
                if b >= 1:
                    hgrn_half(b - 1)
                level_queries(b, 0)
                scores(b, 0)
                for g in range(HG):
                    if g == 0:
                        levels(b, g)
                    scores(b, 2 * g + 1)
                    part(3 * g)
                    if g:
                        levels(b, g)
                    part(3 * g + 1)
                    if g + 1 < HG:
                        level_queries(b, g + 1)
                        scores(b, 2 * g + 2)
                    else:
                        new_state(b)
                        for key in openings(b + 1) if b + 1 < NB else []:
                            low(key)
                    part(3 * g + 2)
            attention_half(NB - 1)
            hgrn_half(NB - 1)

        @block.tensor
        def _(pe):
            t = nc.tensor
            pe.wait_ge(const_in, 8 * 16)

            pe.wait_ge(sums_ready, 1)

            def turn(src, to, n):
                for j in range(n):
                    last = t.transpose(to[:, j * P:(j + 1) * P], src(j), ident[:])
                return last

            def open_split(key):
                what, b = key
                pe.wait_ge(rows_ready, b + 1)
                first = ((K0, K0 + HD, KI0) if what == "keys" else
                         [(Q0 if what == "q" else QI0) + h * HD for h in range(HEADS)])
                wait_pair_free(pe, key)
                for h, c0 in enumerate(first):
                    last = t.transpose(pair(key)[0:HD, h * P:(h + 1) * P], row[:, b % 2, c0:c0 + HD], ident[:])
                last.then_inc(sa_full, 1)

            def opening(b):
                pe.wait_ge(hq_ready, b + 1)
                wait_pair_free(pe, ("hqk", b))
                turn(lambda j: (hq if j < HG else hk)[:, j % HG * P:(j % HG + 1) * P], pair(("hqk", b)), 2 * HG)\
                    .then_inc(sa_full, 1)
                pe.wait_ge(fg_lo_ready, b + 1)
                wait_pair_free(pe, ("tail", b))
                t.matmul(pair(("tail", b))[:, 0:512], sums[:, NM, :], fg_hi[:], start=True, stop=False)
                t.matmul(pair(("tail", b))[:, 0:512], sums[:, NM, :], fg_lo[:], start=False, stop=True)\
                 .then_inc(sa_full, 1)

            def two_passes(to, q, k):
                t.matmul(to, q[:, 0], k, start=True, stop=False)
                return t.matmul(to, q[:, 1], k, start=False, stop=True)

            def idx(b):
                wait_pair_read(pe, use["keys", b])
                pe.wait_ge(doubled["qi"], b - 1)
                for c in range(pairs_of(b)):
                    if c == 1:
                        opening(b - 1)
                    for h in range(IH):
                        key = ("idx", b, c, h)
                        wait_pair_free(pe, key)
                        for k0 in range(1024 * c, min(NK(b), 1024 * (c + 1)), 512):
                            w = min(512, NK(b) - k0)
                            last = two_passes(pair(key)[:, k0 - 1024 * c:k0 - 1024 * c + w], qiT[:, :, h, :],
                                              KT[:, KV, k0:k0 + w])
                        last.then_inc(sa_full, 1)

            def decays(b, h):
                key = ("decay", b, h)
                wait_pair_free(pe, key)
                for m in range(2):
                    for fg_part, start in ((fg_hi, True), (fg_lo, False)):
                        last = t.matmul(pair(key)[:, 512 * m:512 * (m + 1)], fg_part[:, h * HK:(h + 1) * HK],
                                        sums[:, 4 * m:4 * m + 4, :], start=start, stop=not start)
                last.then_inc(sa_full, 1)

            def levels(b, h):
                pe.wait_ge(qe_ready, HG * b + h + 1)
                pe.wait_ge(ke_ready, HG * b + h + 1)
                wait_pair_free(pe, ("level", b, h))
                out = heads(pair(("level", b, h)), NM)
                for m in range(NM - 1):
                    t.matmul(out[:, m, :], ke[:, h % 2, m, :], qe[:, h % 2, m, :], start=True, stop=True)
                t.matmul(out[:, NM - 1, :], hkT[:, h, :], hqT[:, h, :], start=True, stop=True).then_inc(sa_full, 1)

            def output(b, h):
                if h == 0 and b >= 1:
                    pe.wait_ge(ho_out, b)
                    wait_pair_read(pe, use["kv", b - 1])
                to = heads(SD[:])[:, h, :]
                t.matmul(to, qe[:, h % 2, NM - 1, :], state[:, b % 2, h, :], start=True, stop=False)
                pe.wait_ge(am_ready, HG * b + h + 1)
                v = heads(row[:, b % 2, HI0:HI0 + 512])
                t.matmul(to, am[:, h % 2, 0, :], v[:, h, :], start=False, stop=True).then_inc(ho_done, 1)

            def key_values(b):
                key, v = ("kv", b), heads(row[:, b % 2, HI0:HI0 + 512])
                pe.wait_ge(khat_ready, b + 1)
                wait_pair_free(pe, key)
                for h in range(HG):
                    last = t.matmul(pair(key)[:, h * HK:(h + 1) * HK], khat[:, h * HK:(h + 1) * HK], v[:, h, :],
                                    start=True, stop=True)
                last.then_inc(sa_full, 1)

            def scores(b, h):
                for p in range(pairs_of(b)):
                    key = ("att", b, h, p)
                    wait_pair_free(pe, key)
                    for k0 in range(1024 * p, min(NK(b), 1024 * (p + 1)), 512):
                        w = min(512, NK(b) - k0)
                        last = two_passes(pair(key)[:, k0 - 1024 * p:k0 - 1024 * p + w], qT[:, :, h, :],
                                          KT[:, h // GROUP, k0:k0 + w])
                    last.then_inc(sa_full, 1)

            def values(b, h):
                def blocks(c):
                    return range(4 * c, min(4 * c + 4, b + 1))

                def turn_probs(c):
                    wait_bank_free(pe, ("pT", b, h, c))
                    turn(lambda j: prob[:, h % 2, (4 * c + j) * P:(4 * c + j + 1) * P], bank(("pT", b, h, c)),
                         len(blocks(c))).then_inc(sb_full, 1)

                def product(c):
                    g = h // GROUP
                    pe.wait_ge(sb_free, sb_use["pT", b, h, c] + 1)
                    if b >= 1 and h == 0 and c == 0:
                        pe.wait_ge(att_half, b)
                    for kb in blocks(c):
                        last = t.matmul(SC[:, h * HD:(h + 1) * HD], pT[:, pt_order[b, h, c] % 2, (kb % 4) * P:(kb % 4 + 1) * P],
                                        V[:, kb, g * HD:(g + 1) * HD], start=(kb == 0), stop=(kb == b))
                    last.then_inc(pv_done, 1)

                pe.wait_ge(prob_ready, HEADS * b + h + 1)
                for c in range(NCH(b)):
                    turn_probs(c)
                    if c:
                        product(c - 1)
                product(NCH(b) - 1)

            for key in openings(0):
                open_split(key)
            for b in range(NB):
                if not (2 <= b + 1 < NB and pairs_of(b + 1) > 1):
                    opening(b)
                if 2 <= b + 1 < NB:
                    idx(b + 1)
                decays(b, 0)
                wait_pair_read(pe, use["keys", b])
                pe.wait_ge(doubled["q"], b + 1)
                scores(b, 0)
                for g in range(HG):
                    if g == 0:
                        levels(b, g)
                    scores(b, 2 * g + 1)
                    values(b, 2 * g)
                    if g:
                        levels(b, g)
                    if g + 1 < HG:
                        decays(b, g + 1)
                    else:
                        key_values(b)
                    if g >= 1:
                        output(b, g - 1)
                    if g + 1 < HG:
                        scores(b, 2 * g + 2)
                    elif b + 1 < NB:
                        for key in openings(b + 1):
                            open_split(key)
                    values(b, 2 * g + 1)
                output(b, HG - 1)


def out_phase(nc, a, mix_d, x1_d, h2_d):
    with ExitStack() as ctx:
        def sb(name, shape, dt=F32):
            return ctx.enter_context(nc.sbuf_tensor(name, shape, dt))

        def sem(name):
            return ctx.enter_context(nc.semaphore("o_" + name))

        w_raw = sb("wo_raw", [P, KD, D])
        w_hi = sb("wo_hi", [P, KD, D], F32R)
        w_lo = sb("wo_lo", [P, KD, D], F32R)
        mt = sb("mt", [P, 2, D])
        m_hi = sb("m_hi", [P, 2, KD, P], F32R)
        m_lo = sb("m_lo", [P, 2, KD, P], F32R)
        xt = sb("xt_o", [P, 2, D])
        normed = sb("normed", [P, D])
        xn = sb("xn", [P, 2, D])
        hT = sb("hT", [P, KD, P])
        junk = sb("junk_o", [P, 2, D], BF16)
        g_mix = sb("g_mix", [P, D])
        g_ffn = sb("g_ffn", [P, D])
        ident = sb("ident_o", [P, P])
        ss = sb("ss_o", [P, 4])
        var = sb("var_o", [P, 4])
        rstd = sb("rstd_o", [P, 4])
        mhalf = sb("mhalf_o", [P, 1])
        eps = sb("eps_o", [P, 1])
        po = ctx.enter_context(nc.psum_tensor("po", [P, 2, D], F32))
        pm = ctx.enter_context(nc.psum_tensor("pm", [P, KD, P], F32))
        ph = ctx.enter_context(nc.psum_tensor("ph", [P, KD, P], F32))

        ident_in, gains_in = sem("ident_in"), sem("gains_in")
        w_in = [sem(f"w_in{n}") for n in range(4)]
        mix_in = [sem("mix_in0"), sem("mix_in1")]
        x_in = [sem("x_in0"), sem("x_in1")]
        w_hi_ready, w_lo_ready = sem("w_hi_ready"), sem("w_lo_ready")
        m_turned, m_hi_ready, m_lo_ready = sem("m_turned"), sem("m_hi_ready"), sem("m_lo_ready")
        rows_done, ss_rows, rstd_rows = sem("rows_done"), sem("ss_rows"), sem("rstd_rows")
        scaled, added = sem("scaled"), sem("added")
        ss_x1, rstd_x1, xn_ready = sem("ss_x1"), sem("rstd_x1"), sem("xn_ready")
        h_turned, hT_ready, pool_step = sem("h_turned"), sem("hT_ready"), sem("pool_step")
        x1_stored = [sem("x1_stored0"), sem("x1_stored1")]
        h_stored = sem("h_stored")

        def wait(eng, semaphore, value):
            if not isinstance(value, int) or value > 0:
                eng.wait_ge(semaphore, value)

        def tiles(eng, step):
            step(0, 0, 0)
            step(1, 0, 1)
            with eng.Fori(1, NB // 2 - 1) as j:
                step(2 * j, j, 0)
                step(2 * j + 1, j, 1)
            step(NB - 2, NB // 2 - 1, 0)
            step(NB - 1, NB // 2 - 1, 1)

        def known(i, value):
            return isinstance(i, int) and i == value

        block = ctx.enter_context(nc.Block())

        @block.sync
        def _(sp):
            def load_mix(i, u):
                sp.dma_start(mt[:, u, :], mix_d[bass.ds(i * P, P), :]).then_inc(mix_in[u], 16)

            def load_x(i, u):
                sp.dma_start(xt[:, u, :], a["x"][0, bass.ds(i * P, P), :]).then_inc(x_in[u], 16)

            sp.dma_start(ident[:], a["c_ident"]).then_inc(ident_in, 16)
            load_mix(0, 0)
            for n in range(4):
                src = a["w_out"][2 * n * P:(2 * n + 2) * P, :].rearrange("(j p) n -> p j n", p=P)
                sp.dma_start(w_raw[:, 2 * n:2 * n + 2, :], src).then_inc(w_in[n], 16)
                if n == 1:
                    load_mix(1, 1)
            load_x(0, 0)
            sp.dma_start(g_mix[:], a["norm_post_mix"].broadcast_to([P, D])).then_inc(gains_in, 16)
            sp.dma_start(g_ffn[:], a["norm_pre_ffn"].broadcast_to([P, D])).then_inc(gains_in, 16)
            load_x(1, 1)

            def step(i, half, u):
                if not (known(i, NB - 2) or known(i, NB - 1)):
                    wait(sp, m_turned, i + 1)
                    load_mix(i + 2, u)
                if not (known(i, 0) or known(i, NB - 1)):
                    wait(sp, x1_stored[1 - u], 16 * (half + u))
                    wait(sp, xn_ready, i)
                    load_x(i + 1, 1 - u)
            tiles(sp, step)
            for stores in x1_stored:
                sp.wait_ge(stores, 16 * NB // 2)
            sp.wait_ge(h_stored, 16 * NB)

        @block.gpsimd
        def _(pool):
            nc.gpsimd.memset(eps[:], EPS)
            nc.gpsimd.memset(mhalf[:], -0.5).then_inc(pool_step, 1)
            wait(pool, pool_step, 1)

            def root(c, ready, n, done, step):
                c = slice(c, c + 1)
                wait(pool, ready, n)
                nc.gpsimd.tensor_tensor(var[:, c], ss[:, c], eps[:], ALU.add).then_inc(pool_step, 1)
                wait(pool, pool_step, step + 2)
                nc.gpsimd.tensor_tensor(rstd[:, c], var[:, c], mhalf[:, 0:1], ALU.pow).then_inc(done, 1)

            def step(i, half, u):
                if not known(i, 0):
                    root(2 + (1 - u), ss_x1, i, rstd_x1, 2 * i - 1)
                root(u, ss_rows, i + 1, rstd_rows, 2 * i)
            tiles(pool, step)
            root(3, ss_x1, NB, rstd_x1, 2 * NB - 1)

        @block.scalar
        def _(act):
            def turned_high(i, u):
                wait(act, m_turned, i + 1)
                wait(act, rows_done, i - 1)
                nc.scalar.activation(m_hi[:, u], pm[:], ACT.Copy).then_inc(m_hi_ready, 1)

            def finish(i, u, half):
                wait(act, h_turned, i + 1)
                wait(act, h_stored, 16 * i)
                nc.scalar.activation(hT[:], ph[:], ACT.Copy).then_inc(hT_ready, 1)
                wait(act, hT_ready, i + 1)
                act.dma_start(h2_d[i], hT[:]).then_inc(h_stored, 16)

            turned_high(0, 0)
            for k in range(KD):
                if k % 2 == 0:
                    wait(act, w_in[k // 2], 16)
                nc.scalar.activation(w_hi[:, k, :], w_raw[:, k, :], ACT.Copy).then_inc(w_hi_ready, 1)

            def step(i, half, u):
                if not known(i, NB - 1):
                    turned_high(i + 1, 1 - u)
                if not known(i, 0):
                    wait(act, added, i)
                    act.dma_start(x1_d[bass.ds((i - 1) * P, P), :], xt[:, 1 - u, :]).then_inc(x1_stored[1 - u], 16)
                    wait(act, ss_x1, i - 1)
                    wait(act, rstd_rows, i - 1)
                    nc.scalar.activation(junk[:, 1, :], xt[:, 1 - u, :], ACT.Square, scale=D ** -0.5,
                                         accum_out=ss[:, 3 - u:4 - u]).then_inc(ss_x1, 1)
                wait(act, rows_done, i + 1)
                wait(act, ss_rows, i)
                nc.scalar.activation(junk[:, 0, :], po[:, u, :], ACT.Square, scale=D ** -0.5,
                                     accum_out=ss[:, u:u + 1]).then_inc(ss_rows, 1)
                if not known(i, 0):
                    finish(i - 1, 1 - u, half)
            tiles(act, step)
            wait(act, added, NB)
            act.dma_start(x1_d[(NB - 1) * P:NB * P, :], xt[:, 1, :]).then_inc(x1_stored[1], 16)
            wait(act, ss_x1, NB - 1)
            nc.scalar.activation(junk[:, 1, :], xt[:, 1, :], ACT.Square, scale=D ** -0.5,
                                 accum_out=ss[:, 3:4]).then_inc(ss_x1, 1)
            finish(NB - 1, 1, 0)

        @block.vector
        def _(dve):
            v = nc.vector

            def turned_low(i, u):
                wait(dve, m_hi_ready, i + 1)
                v.tensor_tensor(m_lo[:, u], pm[:], m_hi[:, u].bitcast(F32), ALU.subtract).then_inc(m_lo_ready, 1)

            def norm_x1(i, u):
                wait(dve, rstd_x1, i + 1)
                wait(dve, h_turned, i)
                v.scalar_tensor_tensor(xn[:, u, :], xt[:, u, :], rstd[:, 2 + u:3 + u], g_ffn[:], ALU.mult,
                                       ALU.mult).then_inc(xn_ready, 1)

            turned_low(0, 0)
            for k in range(KD):
                wait(dve, w_hi_ready, k + 1)
                v.tensor_tensor(w_lo[:, k, :], w_raw[:, k, :], w_hi[:, k, :].bitcast(F32),
                                ALU.subtract).then_inc(w_lo_ready, 1)
            dve.wait_ge(gains_in, 32)

            def step(i, half, u):
                if not known(i, NB - 1):
                    turned_low(i + 1, 1 - u)
                if not known(i, 0):
                    norm_x1(i - 1, 1 - u)
                wait(dve, rstd_rows, i + 1)
                v.scalar_tensor_tensor(normed[:], po[:, u, :], rstd[:, u:u + 1], g_mix[:], ALU.mult,
                                       ALU.mult).then_inc(scaled, 1)
                wait(dve, scaled, i + 1)
                wait(dve, x_in[u], 16 * (half + 1))
                v.tensor_tensor(xt[:, u, :], xt[:, u, :], normed[:], ALU.add).then_inc(added, 1)
            tiles(dve, step)
            norm_x1(NB - 1, 1)

        @block.tensor
        def _(pe):
            def turn_mix(i, u, half):
                wait(pe, mix_in[u], 16 * (half + 1))
                wait(pe, m_lo_ready, i)
                for k in range(KD):
                    last = nc.tensor.transpose(pm[:, k, :], mt[:, u, k * P:(k + 1) * P], ident[:])
                last.then_inc(m_turned, 1)

            def turn_x1(i, u):
                wait(pe, xn_ready, i + 1)
                wait(pe, hT_ready, i)
                for k in range(KD):
                    last = nc.tensor.transpose(ph[:, k, :], xn[:, u, k * P:(k + 1) * P], ident[:])
                last.then_inc(h_turned, 1)

            def step(i, half, u):
                if not known(i, NB - 1):
                    turn_mix(i + 1, 1 - u, half + u)
                wait(pe, m_lo_ready, i + 1)
                wait(pe, scaled, i - 1)
                for k in range(KD):
                    if known(i, 0):
                        wait(pe, w_lo_ready, k + 1)
                    for n in range(2):
                        o, c = po[:, u, n * 512:(n + 1) * 512], slice(n * 512, (n + 1) * 512)
                        nc.tensor.matmul(o, m_hi[:, u, k, :], w_hi[:, k, c], start=(k == 0), stop=False)
                        nc.tensor.matmul(o, m_hi[:, u, k, :], w_lo[:, k, c], start=False, stop=False)
                        last = nc.tensor.matmul(o, m_lo[:, u, k, :], w_hi[:, k, c], start=False, stop=(k == KD - 1))
                last.then_inc(rows_done, 1)
                if not known(i, 0):
                    turn_x1(i - 1, 1 - u)

            pe.wait_ge(ident_in, 16)
            turn_mix(0, 0, 0)
            tiles(pe, step)
            turn_x1(NB - 1, 1)


def ffn_phase(nc, a, x1_d, h2_d, out):
    with ExitStack() as ctx:
        def sb(name, shape, dt=F32):
            return ctx.enter_context(nc.sbuf_tensor(name, shape, dt))

        def sem(name):
            return ctx.enter_context(nc.semaphore("f_" + name))

        hid_hi = sb("hid_hi", [P, NF, SB], F32R)
        hid_lo = sb("hid_lo", [P, NF, SB], F32R)
        h_raw = sb("h_raw", [P, KD, P])
        h_hi = sb("h2_hi", [P, KD, SB], F32R)
        h_lo = sb("h2_lo", [P, KD, SB], F32R)
        w_raw = sb("wd_raw", [P, 2 * D])
        w_hi = sb("wd_hi", [P, 2, 2 * D], F32R)
        w_lo = sb("wd_lo", [P, 2, 2 * D], F32R)
        xs = sb("xs", [P, TS, D])
        tb = sb("tb", [P, 2, D])
        act_up = sb("act_up", [P, 2, SB])
        g_out = sb("g_out", [P, D])
        ss = sb("ss_d", [P, TS])
        var = sb("var_d", [P, TS])
        rstd = sb("rstd_d", [P, TS])
        mhalf = sb("mhalf_d", [P, 1])
        eps = sb("eps_d", [P, 1])
        ps = ctx.enter_context(nc.psum_tensor("ps_dense", [P, 8, 512], F32))

        const_in = sem("const_in")
        pool_step = sem("pool_step")
        h_in, h_hi_ready, h_lo_ready = sem("h_in"), sem("h_hi_ready"), sem("h_lo_ready")
        h0_in = [sem(f"h0_in{i}") for i in range(TS)]
        x_in = sem("x_in")
        w_in = sem("w_in")
        w_hi_ready = sem("w_hi_ready")
        w_lo_ready = sem("w_lo_ready")
        down_unit = sem("down_unit")
        rows_done = sem("rows_done")
        ss_rows = sem("ss_rows")
        rstd_rows = sem("rstd_rows")
        scaled = sem("scaled")
        added = sem("added")
        up_done = sem("up_done")
        silu_ready = sem("silu_ready")
        hidden = sem("hidden")
        hid_hi_ready = sem("hid_hi_ready")
        hid_lo_ready = sem("hid_lo_ready")
        stored = sem("stored")

        def wait(eng, semaphore, value):
            if not isinstance(value, int) or value > 0:
                eng.wait_ge(semaphore, value)

        units = [("up", f) for f in range(NF)]
        units += [("down", (2 * m, 2 * m + 1)) for m in range(NF // 2 - 1)]
        units += [("down", (NF - 2,)), ("down", (NF - 1,))]
        NU = len(units)
        ND = NU - NF
        assert NU % 2 == 0

        def wait_unit(eng, s, k):
            if k < NF:
                wait(eng, up_done, NF * s + k + 1)
            elif k == NU - 1:
                wait(eng, rows_done, TS * (s + 1))
            else:
                wait(eng, down_unit, (ND - 1) * s + k - NF + 1)

        def width(k):
            return D * len(units[k][1]) if units[k][0] == "down" else 2 * D

        def superblocks(eng, body):
            body(0, True)
            with eng.Fori(1, NS - 1) as s:
                body(s, True)
            body(NS - 1, False)

        def known_first(s):
            return isinstance(s, int) and s == 0

        def h_source(s, i):
            return xs[:, i, :].rearrange("p (k t) -> p k t", k=KD) if known_first(s) else h_raw[:]

        H_UNITS = (NF + 1, NF + 3, NF + 5, NF + 7)
        block = ctx.enter_context(nc.Block())

        @block.sync
        def _(sp):
            def load_unit(s, k):
                wait(sp, w_lo_ready, NU * s + k)
                kind, what = units[k]
                if kind == "up":
                    src, to = a["w_gu"][what], w_raw[:]
                else:
                    src = a["w_down"][what[0] * P:(what[-1] + 1) * P, :].rearrange("(j p) n -> p j n", p=P)
                    to = w_raw[:, 0:width(k)].rearrange("p (j n) -> p j n", n=D)
                sp.dma_start(to, src).then_inc(w_in, 16)

            def load_h(s, i):
                wait(sp, h_lo_ready, TS * s + i)
                sp.dma_start(h_raw[:], h2_d[s * TS + i]).then_inc(h_in, 16)

            for i in range(TS):
                sp.dma_start(xs[:, i, :].rearrange("p (k t) -> p k t", k=KD), h2_d[i]).then_inc(h0_in[i], 16)
                if i == 0:
                    load_unit(0, 0)
            load_unit(0, 1)
            sp.dma_start(g_out[:], a["norm_post_ffn"].broadcast_to([P, D])).then_inc(const_in, 16)

            def superblock(s, more):
                for k in range(2, NU):
                    load_unit(s, k)
                    if k == NF - 2:
                        wait(sp, stored, 16 * TS * s)
                        sp.dma_start(xs[:], x1_d[bass.ds(s * SB, SB), :].rearrange("(i p) d -> p i d", p=P))\
                          .then_inc(x_in, 16)
                    if more and k in H_UNITS:
                        load_h(s + 1, H_UNITS.index(k))
                if more:
                    load_unit(s + 1, 0)
                    load_unit(s + 1, 1)
                for i in range(TS):
                    wait(sp, added, TS * s + i + 1)
                    sp.dma_start(out[0, bass.ds(s * SB + i * P, P), :], xs[:, i, :]).then_inc(stored, 16)
            superblocks(sp, superblock)
            wait(sp, stored, 16 * TS * NS)

        @block.gpsimd
        def _(pool):
            nc.gpsimd.memset(eps[:], EPS)
            nc.gpsimd.memset(mhalf[:], -0.5).then_inc(pool_step, 1)
            wait(pool, pool_step, 1)

            def superblock(s, more):
                for i in range(TS):
                    c = slice(i, i + 1)
                    wait(pool, ss_rows, TS * s + i + 1)
                    nc.gpsimd.tensor_tensor(var[:, c], ss[:, c], eps[:], ALU.add).then_inc(pool_step, 1)
                    wait(pool, pool_step, TS * s + i + 2)
                    nc.gpsimd.tensor_tensor(rstd[:, c], var[:, c], mhalf[:, 0:1], ALU.pow).then_inc(rstd_rows, 1)
            superblocks(pool, superblock)

        @block.scalar
        def _(act):
            def split_w(s, k):
                wait(act, w_in, 16 * (NU * s + k + 1))
                if k >= 2:
                    wait_unit(act, s, k - 2)
                elif not isinstance(s, int) or s > 0:
                    wait_unit(act, s - 1, NU + k - 2)
                nc.scalar.activation(w_hi[:, k % 2, 0:width(k)], w_raw[:, 0:width(k)], ACT.Copy)\
                  .then_inc(w_hi_ready, 1)

            def split_h(s, i):
                if known_first(s):
                    wait(act, h0_in[i], 16)
                else:
                    wait(act, h_in, 16 * (TS * (s - 1) + i + 1))
                    wait(act, up_done, NF * s)
                nc.scalar.activation(h_hi[:, :, i * P:(i + 1) * P], h_source(s, i), ACT.Copy).then_inc(h_hi_ready, 1)

            split_w(0, 0)
            for i in range(TS):
                split_h(0, i)
            split_w(0, 1)

            def superblock(s, more):
                for f in range(NF):
                    wait(act, up_done, NF * s + f + 1)
                    wait(act, hid_lo_ready, NF * s + max(f - 1, 0))
                    nc.scalar.activation(act_up[:, f % 2, :], ps[:, 2 * (f % 4), :], ACT.Silu)\
                      .then_inc(silu_ready, 1)
                    wait(act, hidden, NF * s + f + 1)
                    nc.scalar.activation(hid_hi[:, f, :], act_up[:, f % 2, :], ACT.Copy).then_inc(hid_hi_ready, 1)
                    split_w(s, f + 2)
                for k in range(NF + 2, NU):
                    split_w(s, k)
                    if more and k - 2 in H_UNITS:
                        split_h(s + 1, H_UNITS.index(k - 2))
                if more:
                    split_w(s + 1, 0)
                for i in range(TS):
                    wait(act, rows_done, TS * s + i + 1)
                    wait(act, added, TS * s + max(i - 1, 0))
                    nc.scalar.activation(tb[:, i % 2, :], ps[:, 2 * i:2 * i + 2, :].rearrange("p a b -> p (a b)"),
                                         ACT.Square, scale=D ** -0.5, accum_out=ss[:, i:i + 1]).then_inc(ss_rows, 1)
                if more:
                    split_w(s + 1, 1)
            superblocks(act, superblock)

        @block.vector
        def _(dve):
            def split_w(s, k):
                wait(dve, w_hi_ready, NU * s + k + 1)
                w = slice(0, width(k))
                nc.vector.tensor_tensor(w_lo[:, k % 2, w], w_raw[:, w], w_hi[:, k % 2, w].bitcast(F32),
                                        ALU.subtract).then_inc(w_lo_ready, 1)

            def split_h(s, i):
                wait(dve, h_hi_ready, TS * s + i + 1)
                tok = slice(i * P, (i + 1) * P)
                nc.vector.tensor_tensor(h_lo[:, :, tok], h_source(s, i), h_hi[:, :, tok].bitcast(F32),
                                        ALU.subtract).then_inc(h_lo_ready, 1)

            split_w(0, 0)
            for i in range(TS):
                split_h(0, i)
            split_w(0, 1)
            wait(dve, const_in, 16)

            def superblock(s, more):
                for f in range(NF):
                    wait(dve, silu_ready, NF * s + f + 1)
                    au = act_up[:, f % 2, :]
                    nc.vector.tensor_tensor(au, au, ps[:, 2 * (f % 4) + 1, :], ALU.mult).then_inc(hidden, 1)
                    wait(dve, hid_hi_ready, NF * s + f + 1)
                    nc.vector.tensor_tensor(hid_lo[:, f, :], au, hid_hi[:, f, :].bitcast(F32),
                                            ALU.subtract).then_inc(hid_lo_ready, 1)
                    split_w(s, f + 2)
                for k in range(NF + 2, NU):
                    split_w(s, k)
                    if more and k - 2 in H_UNITS:
                        split_h(s + 1, H_UNITS.index(k - 2))
                if more:
                    split_w(s + 1, 0)
                wait(dve, x_in, 16 * (s + 1))
                for i in range(TS):
                    wait(dve, rstd_rows, TS * s + i + 1)
                    nc.vector.scalar_tensor_tensor(tb[:, i % 2, :], ps[:, 2 * i:2 * i + 2, :].rearrange("p a b -> p (a b)"),
                                                   rstd[:, i:i + 1], g_out[:], ALU.mult, ALU.mult).then_inc(scaled, 1)
                    wait(dve, scaled, TS * s + i + 1)
                    nc.vector.tensor_tensor(xs[:, i, :], xs[:, i, :], tb[:, i % 2, :], ALU.add).then_inc(added, 1)
                    if more and i == 1:
                        split_w(s + 1, 1)
            superblocks(dve, superblock)

        @block.tensor
        def _(pe):
            def superblock(s, more):
                wait(pe, h_lo_ready, TS * (s + 1))
                for f in range(NF):
                    wait(pe, w_lo_ready, NU * s + f + 1)
                    if f >= 4:
                        wait(pe, hidden, NF * s + f - 3)
                    else:
                        wait(pe, scaled, TS * (s - 1) + f + 1)
                    for m in range(2):
                        for c in range(KD):
                            w = slice((m * KD + c) * P, (m * KD + c + 1) * P)
                            o = ps[:, 2 * (f % 4) + m, :]
                            nc.tensor.matmul(o, w_hi[:, f % 2, w], h_hi[:, c, :], start=(c == 0), stop=False)
                            nc.tensor.matmul(o, w_hi[:, f % 2, w], h_lo[:, c, :], start=False, stop=False)
                            last = nc.tensor.matmul(o, w_lo[:, f % 2, w], h_hi[:, c, :], start=False,
                                                    stop=(c == KD - 1))
                    last.then_inc(up_done, 1)
                for k in range(NF, NU):
                    wait(pe, w_lo_ready, NU * s + k + 1)
                    for j, c in enumerate(units[k][1]):
                        first, final = c == 0, c == NF - 1
                        if final:
                            wait(pe, hid_lo_ready, NF * (s + 1))
                        for i in ((2, 3, 0, 1) if first else range(TS)):
                            if first:
                                wait(pe, hidden, NF * s + (NF - 5 + i if i >= 2 else NF - 1 + i))
                                wait(pe, hid_lo_ready, NF * s + 1)
                            elif c < NF - 1 and i == 0:
                                wait(pe, hid_lo_ready, NF * s + c + 1)
                            tok = slice(i * P, (i + 1) * P)
                            for lhs, w, start, stop in ((hid_hi, w_hi, True, False), (hid_hi, w_lo, False, False),
                                                        (hid_lo, w_hi, False, True)):
                                for n in range(2):
                                    last = nc.tensor.matmul(ps[:, 2 * i + n, :], lhs[:, c, tok],
                                                            w[:, k % 2, j * D + n * 512:j * D + n * 512 + 512],
                                                            start=start and first, stop=stop and final)
                            if final:
                                last.then_inc(rows_done, 1)
                    if k < NU - 1:
                        last.then_inc(down_unit, 1)
            superblocks(pe, superblock)


def layout_gu(w_gate, w_up):
    w = np.stack([w_gate, w_up]).reshape(2, KD, P, NF, P)
    return np.ascontiguousarray(w.transpose(3, 2, 0, 1, 4)).reshape(NF, P, 2 * KD * P)


def build(nc, a, out):
    proj_d = nc.dram_tensor("proj_d", [T, IN_W], F32, kind="Internal").ap()
    mix_d = nc.dram_tensor("mix_d", [T, D], F32, kind="Internal").ap()
    project_phase(nc, a, proj_d)
    mix_phase(nc, a, proj_d, mix_d)
    x1_d = nc.dram_tensor("x1_d", [T, D], F32, kind="Internal").ap()
    h2_d = nc.dram_tensor("h2_d", [NB, P, KD, P], F32, kind="Internal").ap()
    out_phase(nc, a, mix_d, x1_d, h2_d)
    ffn_phase(nc, a, x1_d, h2_d, out)


_INS = ["x", "norm_pre_mix", "w_in", "w_out", "norm_post_mix", "hg_lower_bound", "hg_out_norm",
        "norm_pre_ffn", "w_gu", "w_down", "norm_post_ffn"]


def kernel(**inputs):
    import concourse.bacc as bacc
    from concourse.bass_utils import run_bass_kernel_spmd

    given = {n: np.ascontiguousarray(inputs[n]) for n in inputs}
    arrays = {n: given[n] for n in ("x", "norm_pre_mix", "norm_post_mix", "hg_lower_bound", "hg_out_norm",
                                    "norm_pre_ffn", "norm_post_ffn")}
    arrays["w_in"] = np.ascontiguousarray(given["w_in"][0].reshape(KD, P, NC_IN, CW).transpose(2, 1, 0, 3))
    arrays["w_out"] = given["w_out"][0]
    arrays["w_gu"] = layout_gu(given["w_gate"][0], given["w_up"][0])
    arrays["w_down"] = given["w_down"][0]
    arrays.update(shape_constants())

    nc = bacc.Bacc("TRN2", target_bir_lowering=False, num_devices=1)
    a = {n: nc.dram_tensor(f"in_{n}", v.shape, mybir.dt.from_np(v.dtype), kind="ExternalInput").ap()
         for n, v in arrays.items()}
    out = nc.dram_tensor("out_y", (1, T, D), F32, kind="ExternalOutput").ap()
    build(nc, a, out)
    r = run_bass_kernel_spmd(nc, [{f"in_{n}": v for n, v in arrays.items()}], core_ids=[0])
    return r.results[0]["out_y"]
```
